# Optimizing a Trainium2 kernel written in Bass

```python
import jax, jax.numpy as jnp
from jax import lax
import numpy as np

D_MODEL = 1024
BATCH = 1
SEQ = 1024
DEPTH = 1

GRID_W = 64
CTX_LEN = 256
N_MOD = 6
POOL_WINDOWS = (2, 4, 8, 16)
N_POOL_GROUPS = 4
POOL_GROUP_DIM = D_MODEL // 8
POOL_WIDTH = N_POOL_GROUPS * POOL_GROUP_DIM
HEAD_DIM = 64
NA_HEADS = (D_MODEL // 2) // HEAD_DIM
NA_WIDTH = NA_HEADS * HEAD_DIM
NA_ROWS = 8
NA_COLS = 16
D_FF = 4 * D_MODEL
ROPE_THETA = 10000.0
EPS = 1e-6
IN_WIDTH = POOL_WIDTH + 3 * NA_WIDTH + 2 * D_MODEL
SPLIT_POINTS = (POOL_WIDTH, POOL_WIDTH + NA_WIDTH, POOL_WIDTH + 2 * NA_WIDTH,
                POOL_WIDTH + 3 * NA_WIDTH, POOL_WIDTH + 3 * NA_WIDTH + D_MODEL)
KV_START = POOL_WIDTH + NA_WIDTH
KV_END = POOL_WIDTH + 3 * NA_WIDTH

kernel_name = "hybrid_pool_natten_dit_block"

def rmsnorm(x, g):
    xf = x.astype(jnp.float32)
    y = xf * lax.rsqrt(jnp.mean(xf * xf, axis=-1, keepdims=True) + EPS)
    return (y * g.astype(jnp.float32)).astype(x.dtype)

def heads(a):
    return a.reshape(a.shape[0], a.shape[1], NA_HEADS, HEAD_DIM)

def axial_rope(a, ang_row, ang_col):
    n = HEAD_DIM // 4

    def rot(xh, ang):
        cs = jnp.cos(ang)[None, :, None, :]
        sn = jnp.sin(ang)[None, :, None, :]
        x1, x2 = xh[..., :n], xh[..., n:]
        return jnp.concatenate([x1 * cs - x2 * sn, x1 * sn + x2 * cs], axis=-1)

    af = a.astype(jnp.float32)
    out = jnp.concatenate([rot(af[..., :2 * n], ang_row), rot(af[..., 2 * n:], ang_col)], axis=-1)
    return out.astype(a.dtype)

def pool_mixer(u, pool_w, pool_scale):
    L = u.shape[1]
    uf = u.astype(jnp.float32)
    cs = jnp.concatenate([jnp.zeros_like(uf[:, :1]), jnp.cumsum(uf, axis=1)], axis=1)
    t = jnp.arange(L)
    outs = []
    for g, w in enumerate(POOL_WINDOWS):
        lo = jnp.clip(t - w // 2, 0, L)
        hi = jnp.clip(t + w // 2, 0, L)
        csg = cs[..., g * POOL_GROUP_DIM:(g + 1) * POOL_GROUP_DIM]
        mean = (csg[:, hi] - csg[:, lo]) / (hi - lo).astype(jnp.float32)[:, None]
        outs.append(mean - uf[..., g * POOL_GROUP_DIM:(g + 1) * POOL_GROUP_DIM])
    d = jnp.stack(outs, axis=2).astype(u.dtype)
    y = jnp.einsum('blgc,gce->blge', d, pool_w)
    return y.reshape(u.shape) * pool_scale

def neighbourhood_attention(q_rot, q_plain, k_rot, v, k_ctx, v_ctx, rpb):
    B, L = q_rot.shape[0], q_rot.shape[1]
    rows = L // GRID_W
    kr = min(NA_ROWS, rows)
    kc = NA_COLS
    scale = HEAD_DIM ** -0.5

    def grid(a):
        return a.reshape(B, rows, GRID_W, NA_HEADS, HEAD_DIM)

    qg, qpg, kg, vg = grid(q_rot), grid(q_plain), grid(k_rot), grid(v)
    col = jnp.arange(GRID_W)
    c0 = jnp.clip(col - kc // 2, 0, GRID_W - kc)
    col_idx = c0[:, None] + jnp.arange(kc)[None, :]
    col_rel = col_idx - col[:, None] + (NA_COLS - 1)

    def row_block(r):
        r0 = jnp.clip(r - kr // 2, 0, rows - kr)
        q_r = lax.dynamic_index_in_dim(qg, r, axis=1, keepdims=False)
        qp_r = lax.dynamic_index_in_dim(qpg, r, axis=1, keepdims=False)
        k_rows = lax.dynamic_slice_in_dim(kg, r0, kr, axis=1)
        v_rows = lax.dynamic_slice_in_dim(vg, r0, kr, axis=1)
        k_win = k_rows[:, :, col_idx]
        v_win = v_rows[:, :, col_idx]
        row_rel = r0 + jnp.arange(kr) - r + (NA_ROWS - 1)
        bias = rpb[:, row_rel][:, :, col_rel].transpose(0, 2, 1, 3)
        s_loc = jnp.einsum('bchd,brckhd->bhcrk', q_r, k_win).astype(jnp.float32) * scale
        s_loc = s_loc + bias.astype(jnp.float32)[None]
        s_ctx = jnp.einsum('bchd,bnhd->bhcn', qp_r, k_ctx).astype(jnp.float32) * scale
        s = jnp.concatenate([s_loc.reshape(B, NA_HEADS, GRID_W, kr * kc), s_ctx], axis=-1)
        p = jax.nn.softmax(s, axis=-1).astype(v.dtype)
        p_loc = p[..., :kr * kc].reshape(B, NA_HEADS, GRID_W, kr, kc)
        p_ctx = p[..., kr * kc:]
        return (jnp.einsum('bhcrk,brckhd->bchd', p_loc, v_win)
                + jnp.einsum('bhcn,bnhd->bchd', p_ctx, v_ctx))

    o = lax.map(row_block, jnp.arange(rows))
    return o.transpose(1, 0, 2, 3, 4).reshape(B, L, NA_WIDTH)

def context_attention(q, k, v):
    s = jnp.einsum('bqhd,bkhd->bhqk', q, k).astype(jnp.float32) * (HEAD_DIM ** -0.5)
    p = jax.nn.softmax(s, axis=-1).astype(v.dtype)
    o = jnp.einsum('bhqk,bkhd->bqhd', p, v)
    return o.reshape(o.shape[0], o.shape[1], NA_WIDTH)

def sq_relu_mlp(h, w1, w2):
    a = jax.nn.relu(h @ w1)
    return (a * a) @ w2

def setup_inputs(seed: int = 0) -> dict:
    key = jax.random.key(seed)
    ks = jax.random.split(key, 19)
    f32 = jnp.float32
    nrm = lambda k, shape, s: jax.random.normal(k, shape, f32) * s
    return {
        "x": nrm(ks[0], (BATCH, SEQ, D_MODEL), 1.0),
        "c": nrm(ks[1], (BATCH, D_MODEL), 1.0),
        "ctx": nrm(ks[2], (BATCH, CTX_LEN, D_MODEL), 1.0),
        "c_ctx": nrm(ks[3], (D_MODEL,), 1.0),
        "ada_w": nrm(ks[4], (DEPTH, D_MODEL, N_MOD * D_MODEL), D_MODEL ** -0.5),
        "ada_b": nrm(ks[5], (DEPTH, N_MOD * D_MODEL), 0.02),
        "norm1_g": 1.0 + nrm(ks[6], (DEPTH, D_MODEL), 0.05),
        "norm2_g": 1.0 + nrm(ks[7], (DEPTH, D_MODEL), 0.05),
        "w_in": nrm(ks[8], (DEPTH, D_MODEL, IN_WIDTH), D_MODEL ** -0.5),
        "pool_w": nrm(ks[9], (DEPTH, N_POOL_GROUPS, POOL_GROUP_DIM, POOL_GROUP_DIM), POOL_GROUP_DIM ** -0.5),
        "pool_scale": 1.0 + nrm(ks[10], (DEPTH, POOL_WIDTH), 0.1),
        "q_norm_g": 1.0 + nrm(ks[11], (DEPTH, HEAD_DIM), 0.05),
        "k_norm_g": 1.0 + nrm(ks[12], (DEPTH, HEAD_DIM), 0.05),
        "rpb": nrm(ks[13], (DEPTH, NA_HEADS, 2 * NA_ROWS - 1, 2 * NA_COLS - 1), 0.2),
        "w_branch_pool": nrm(ks[14], (DEPTH, POOL_WIDTH, D_MODEL), POOL_WIDTH ** -0.5),
        "w_branch_na": nrm(ks[15], (DEPTH, NA_WIDTH, D_MODEL), NA_WIDTH ** -0.5),
        "w_out": nrm(ks[16], (DEPTH, D_MODEL, D_MODEL), D_MODEL ** -0.5),
        "mlp_w1": nrm(ks[17], (DEPTH, D_MODEL, D_FF), D_MODEL ** -0.5),
        "mlp_w2": nrm(ks[18], (DEPTH, D_FF, D_MODEL), D_FF ** -0.5),
    }

def reference(x, c, ctx, c_ctx, ada_w, ada_b, norm1_g, norm2_g, w_in, pool_w, pool_scale,
              q_norm_g, k_norm_g, rpb, w_branch_pool, w_branch_na, w_out, mlp_w1, mlp_w2):
    L = x.shape[1]
    t = jnp.arange(L)
    n_freq = HEAD_DIM // 4
    inv = ROPE_THETA ** (-jnp.arange(n_freq, dtype=jnp.float32) / n_freq)
    ang_row = (t // GRID_W).astype(jnp.float32)[:, None] * inv
    ang_col = (t % GRID_W).astype(jnp.float32)[:, None] * inv
    silu_c = jax.nn.silu(c)
    silu_cc = jax.nn.silu(c_ctx)

    for l in range(DEPTH):
        last = l == DEPTH - 1
        mod = (silu_c @ ada_w[l] + ada_b[l])[:, None, :]
        sh1, s1, g1, sh2, s2, g2 = jnp.split(mod, N_MOD, axis=-1)
        mod_c = silu_cc @ ada_w[l] + ada_b[l]
        csh1, cs1, cg1, csh2, cs2, cg2 = jnp.split(mod_c, N_MOD, axis=-1)

        h = rmsnorm(x, norm1_g[l]) * (1.0 + s1) + sh1
        hc = rmsnorm(ctx, norm1_g[l]) * (1.0 + cs1) + csh1
        z = h @ w_in[l]
        u_pool, q, k, v, gate_pool, gate_na = jnp.split(z, SPLIT_POINTS, axis=-1)
        if last:
            zc_kv = hc @ w_in[l][:, KV_START:KV_END]
            kc_, vc_ = jnp.split(zc_kv, 2, axis=-1)
        else:
            zc = hc @ w_in[l]
            uc_pool, qc_, kc_, vc_, gc_pool, gc_na = jnp.split(zc, SPLIT_POINTS, axis=-1)
        k_ctx = rmsnorm(heads(kc_), k_norm_g[l])
        v_ctx = heads(vc_)

        q = rmsnorm(heads(q), q_norm_g[l])
        k = rmsnorm(heads(k), k_norm_g[l])
        q_rot = axial_rope(q, ang_row, ang_col)
        k_rot = axial_rope(k, ang_row, ang_col)
        na = neighbourhood_attention(q_rot, q, k_rot, heads(v), k_ctx, v_ctx, rpb[l])
        pool = pool_mixer(u_pool, pool_w[l], pool_scale[l])
        merged = (jax.nn.sigmoid(gate_pool) * (pool @ w_branch_pool[l])
                  + jax.nn.sigmoid(gate_na) * (na @ w_branch_na[l]))
        x_new = x + g1 * (merged @ w_out[l])
        h2 = rmsnorm(x_new, norm2_g[l]) * (1.0 + s2) + sh2
        x_new = x_new + g2 * sq_relu_mlp(h2, mlp_w1[l], mlp_w2[l])

        if not last:
            qc = rmsnorm(heads(qc_), q_norm_g[l])
            na_c = context_attention(qc, k_ctx, v_ctx)
            pool_c = pool_mixer(uc_pool, pool_w[l], pool_scale[l])
            merged_c = (jax.nn.sigmoid(gc_pool) * (pool_c @ w_branch_pool[l])
                        + jax.nn.sigmoid(gc_na) * (na_c @ w_branch_na[l]))
            ctx = ctx + cg1 * (merged_c @ w_out[l])
            h2c = rmsnorm(ctx, norm2_g[l]) * (1.0 + cs2) + csh2
            ctx = ctx + cg2 * sq_relu_mlp(h2c, mlp_w1[l], mlp_w2[l])
        x = x_new
    return x


_drawn_inputs = setup_inputs


def setup_inputs(seed=0):
    import zlib

    import numpy as np

    out = dict(_drawn_inputs(seed))
    spreads = {}
    factors = {'norm1_g': 2.932, 'q_norm_g': 8.0, 'k_norm_g': 8.0, 'rpb': 8.0}
    for name, (base, spread) in spreads.items():
        noise = np.random.default_rng([zlib.crc32(name.encode()), seed]).standard_normal(out[name].shape)
        drawn = base * np.exp(spread * noise) if base else spread * noise
        out[name] = __import__('jax').numpy.asarray(drawn.astype(out[name].dtype))
    for name, factor in factors.items():
        out[name] = (out[name] * factor).astype(out[name].dtype)
    return out
```

```python
from contextlib import ExitStack

import numpy as np
import concourse.bass as bass
from concourse import mybir

P = 128
D = 1024
L = 1024
CTX = 256
T = L + CTX
KD = D // P
NT = L // P
NTA = T // P
GRID_W = 64
ROWS = L // GRID_W
WINDOWS = (16, 8, 4, 2)
POOL_ORDER = (3, 2, 1, 0)
NG = 4
PAD = 8
HD = 64
HEADS = 8
PAIRS = HEADS // 2
NA_ROWS, NA_COLS = 8, 16
D_FF = 4096
FG = 512
NFG = D_FF // FG
FCH = FG // P
EPS = 1e-6
HALF = 512
BIG = -1e30
SLOTS_FULL = 14
SLOTS_INNER = 9
BIASW = (SLOTS_FULL + SLOTS_INNER) * GRID_W

U_POOL = 0
U_GATE = U_POOL + NG
U_ATT = U_GATE + 3 * KD
U_NA = U_ATT + 3 * PAIRS
U_OUT = U_NA + 4
U_MLP = U_OUT + 8
UNITS = U_MLP + 8 * NFG
MLP_ORDER = (("w1", 0, 0), ("w1", 1, 1), ("w2", 0, 2), ("w1", 2, 0),
             ("w2", 1, 3), ("w1", 3, 1), ("w2", 2, 4), ("w2", 3, 5))

F32 = mybir.dt.float32
F32R = mybir.dt.float32r
ALU = mybir.AluOpType
ACT = mybir.ActivationFunctionType
AX = mybir.AxisListType


def key_tile(i):
    return min(max(i - 2, 0), 4)


def inner(i):
    return 2 <= i <= 5


class Steps:

    def __init__(self, eng, sem):
        self.eng, self.sem, self.base, self.n = eng, sem, 0, 0

    def done(self, ins):
        ins.then_inc(self.sem, 1)
        self.n += 1

    def wait(self):
        self.eng.wait_ge(self.sem, self.base + self.n)

    def link(self, ins):
        self.done(ins)
        self.wait()

    def enter(self, i, first, per_turn):
        self.base, self.n, self.per, self.start = self.start_of(i, first, per_turn), 0, per_turn, self.base + self.n

    def start_of(self, i, first, per_turn):
        return (i - first) * per_turn + (self.base + self.n)

    def leave(self, turns):
        assert self.n == self.per, (self.n, self.per)
        self.base, self.n = self.start + self.per * turns, 0


def build(nc, a, out):
    with ExitStack() as ctx:
        build_in(nc, a, out, ctx)


def build_in(nc, a, out, ctx):
    KB = 1024
    CONST = 32 * KB
    H = 35 * KB
    R = H + 80 * KB
    base = 16 * KB + 512

    def at(name, shape, dt, off):
        return nc.alloc_sbuf_tensor_at(name, shape, dt, offset=base + off)

    ringA_hi = at("ringA_hi", [P, 3, 1024], F32R, 0)
    ringA_lo = at("ringA_lo", [P, 3, 1024], F32R, 12 * KB)
    rawA = at("rawA", [P, 2, 1024], F32, 24 * KB)
    off = CONST
    def const(name, shape, dt=F32):
        nonlocal off
        n = 4 * int(np.prod(shape[1:]))
        t = at(name, shape, dt, off)
        off += (n + 31) // 32 * 32
        assert off <= H
        return t
    ident = const("ident", [P, P])
    ones = const("ones", [P, P])
    c_col = const("c_col", [P, KD, 2])
    c_sig = const("c_sig", [P, KD, 2])
    c_silu = const("c_silu", [P, KD, 2])
    norm_g = const("norm_g", [P, 2, KD])
    ada_b = const("ada_b", [P, 48])
    pscale = const("pscale", [P, NG])
    edge_inv = const("edge_inv", [P, NG, 2 * PAD])
    edge_tmp = const("edge_tmp", [P, PAD])
    mod1 = const("mod1", [P, 16, 2])
    gain1 = const("gain1", [P, KD, 2])
    mod2 = const("mod2", [P, 4, KD])
    gain2 = const("gain2", [P, KD])
    ms = const("ms", [P, 40])
    rs = const("rs", [P, 40])
    rt = const("rt", [P, 40])
    row_ss = const("row_ss", [P, NT])
    cmax = const("cmax", [P, 2])
    smax = const("smax", [P, 2])
    nmax = const("nmax", [P, 2])
    den = const("den", [P, 2])
    rden = const("rden", [P, 2])
    gate_cell = const("gate_cell", [P, 2])
    ringB_hi = at("ringB_hi", [P, 3, 1024], F32R, R)
    ringB_lo = at("ringB_lo", [P, 3, 1024], F32R, R + 12 * KB)
    rawB = at("rawB", [P, 2, 1024], F32, R + 24 * KB)
    ada1 = at("ada1", [P, 16, 1024], F32, H)
    xsq = at("xsq", [P, 2, T], F32, H + 64 * KB)
    xT = at("xT", [P, KD, T], F32, R + 32 * KB)
    hfull = at("hfull", [P, 2, T], F32, R + 72 * KB)
    diag = at("diag", [P, NTA, P], F32, R + 82 * KB)
    hT_hi = at("hT_hi", [P, KD, T], F32R, H)
    hT_lo = at("hT_lo", [P, KD, T], F32R, H + 40 * KB)
    poolT_hi = at("poolT_hi", [P, NG, L], F32R, R + 32 * KB)
    poolT_lo = at("poolT_lo", [P, NG, L], F32R, R + 48 * KB)
    W = L + 2 * PAD
    up = at("up", [P, W], F32, R + 64 * KB)
    win = [at(f"win{n}", [P, W], F32, R + 64 * KB + 4160 * (n + 1)) for n in range(2)]
    dT_hi = at("dT_hi", [P, L], F32R, R + 64 * KB + 12480)
    dT_lo = at("dT_lo", [P, L], F32R, R + 64 * KB + 16576)
    pw_lo = at("pw_lo", [P, NG, P], F32R, R + 64 * KB + 20672)
    pw_raw = at("pw_raw", [P, NG, P], F32, R + 89088)
    pw_hi = at("pw_hi", [P, NG, P], F32R, R + 91136)
    sgp = at("sgp", [P, 2, HALF], F32, R + 64 * KB)
    sgn = at("sgn", [P, 2, HALF], F32, R + 68 * KB)
    mpool = at("mpool", [P, 2, HALF], F32, R + 72 * KB)
    acc = at("acc", [P, 1024], F32, R + 76 * KB)
    ada2 = at("ada2", [P, 2, 1024], F32, R + 80 * KB)
    qrT = at("qrT", [P, L], F32R, R)
    qpT = at("qpT", [P, L], F32R, R + 4 * KB)
    krT_hi = at("krT_hi", [P, L], F32R, R + 8 * KB)
    krT_lo = at("krT_lo", [P, L], F32R, R + 12 * KB)
    kcT_hi = at("kcT_hi", [P, CTX], F32R, R + 16 * KB)
    kcT_lo = at("kcT_lo", [P, CTX], F32R, R + 17 * KB)
    vcur = at("vcur", [P, NTA, P], F32, R + 18 * KB)
    probT = at("probT", [P, 7, P], F32, R + 23 * KB)
    rope_c = at("rope_c", [P, NT, HD], F32, R + 26 * KB + 512)
    rope_s = at("rope_s", [P, NT, HD], F32, R + 28 * KB + 512)
    qk_g = at("qk_g", [P, 256], F32, R + 30 * KB + 512)
    z = at("z", [P, NTA, 384], F32, R + 32 * KB)
    nrm = at("nrm", [P, NTA, 256], F32, R + 47 * KB)
    rot_q = at("rot_q", [P, NT, 2, HD], F32, R + 57 * KB)
    rot_k = at("rot_k", [P, NT, 2, 2, HD], F32, R + 61 * KB)
    kc2 = at("kc2", [P, 2, 2, 2, HD], F32, R + 69 * KB)
    rope_t = at("rope_t", [P, NT, HD], F32, R + 71 * KB)
    prob = at("prob", [P, 2, 832], F32, R + 73 * KB)
    bias = at("bias", [P, BIASW], F32, R + 73 * KB + 6656)
    na_tok = at("na_tok", [P, NT, P], F32, R + 73 * KB + 6656 + 4 * BIASW)
    naT_out = at("naT_out", [P, L], F32, R + 57 * KB)
    mT_hi = at("mT_hi", [P, KD, L], F32R, H)
    mT_lo = at("mT_lo", [P, KD, L], F32R, H + 32 * KB)
    gn_in = at("gn_in", [P, 2, HALF], F32, H + 64 * KB)
    mp_in = at("mp_in", [P, 2, HALF], F32, H + 68 * KB)
    naT_hi = at("naT_hi", [P, PAIRS, L], F32R, R + 32 * KB)
    naT_lo = at("naT_lo", [P, PAIRS, L], F32R, R + 48 * KB)
    naT_in = at("naT_in", [P, PAIRS, L], F32, R + 64 * KB)
    xn = at("xn", [P, NT, D], F32, R + 32 * KB)
    nx = [at("nx0", [P, 4, D], F32, R + 64 * KB), at("nx1", [P, 4, D], F32, H + 64 * KB)]
    gb = at("gb", [P, D], F32, R + 80 * KB)
    otmp = at("otmp", [P, 2, HALF], F32, R + 84 * KB)
    gdiag = at("gdiag", [P, KD, P], F32, R + 88 * KB)
    h2_hi = at("h2_hi", [P, KD, L], F32R, H)
    h2_lo = at("h2_lo", [P, KD, L], F32R, H + 32 * KB)
    aT_hi = at("aT_hi", [P, FCH, L], F32R, H + 64 * KB)
    aT_lo = at("aT_lo", [P, FCH, L], F32R, R + 64 * KB)
    relu = at("relu", [P, 2, HALF], F32, R + 84 * KB)
    ytmp = at("ytmp", [P, 2, HALF], F32, R + 88 * KB)

    ps = ctx.enter_context(nc.psum_tensor("ps", [P, 8, HALF], F32))
    bank = [ps[:, b, :] for b in range(8)]
    psflat = ps[:, :, :].rearrange("p b n -> p (b n)")

    spill_m = nc.dram_tensor("spill_m", (2, KD, 2, P, HALF), F32, kind="Internal").ap()
    spill_na = nc.dram_tensor("spill_na", (PAIRS, P, L), F32, kind="Internal").ap()

    def hi(s):
        return (ringA_hi if s < 3 else ringB_hi)[:, s % 3, :]

    def lo(s):
        return (ringA_lo if s < 3 else ringB_lo)[:, s % 3, :]

    def raw(r):
        return (rawA if r < 2 else rawB)[:, r % 2, :]

    def sem(name):
        return ctx.enter_context(nc.semaphore(name))

    d_const = sem("d_const")
    d_att = sem("d_att")
    d_x = [sem(f"d_x{k}") for k in range(KD)]
    d_ada1 = [sem(f"d_ada1_{q}") for q in range(4)]
    d_raw = [sem(f"d_raw{r}") for r in range(4)]
    cell_set = sem("cell_set")
    split_hi = sem("split_hi")
    split = sem("split")
    v_own = sem("v_own")
    a_own = sem("a_own")
    sig_done = sem("sig_done")
    silu_done = sem("silu_done")
    sq_done = sem("sq_done")
    ssq_ps = sem("ssq_ps")
    ms_ready = sem("ms_ready")
    sqrt_done = sem("sqrt_done")
    diag_ready = sem("diag_ready")
    rb_ps = sem("rb_ps")
    mod1_ps = sem("mod1_ps")
    xr_ready = sem("xr_ready")
    h_hi_done = sem("h_hi_done")
    h_done = sem("h_done")
    pw_done = sem("pw_done")
    u_ps = sem("u_ps")
    pads_done = sem("pads_done")
    u_copied = sem("u_copied")
    d_made = sem("d_made")
    d_hi_done = sem("d_hi_done")
    d_done = sem("d_done")
    y_ps = sem("y_ps")
    y_hi_done = sem("y_hi_done")
    y_done = sem("y_done")
    m1_ps = sem("m1_ps")
    sg_done = sem("sg_done")
    mp_done = sem("mp_done")
    spill_g = [sem(f"spill_g{n}") for n in range(2)]
    spill_p = [sem(f"spill_p{n}") for n in range(2)]
    d_ada2 = [sem(f"d_ada2_{n}") for n in range(2)]
    ada2_used = sem("ada2_used")
    acc_ready = sem("acc_ready")
    mod2_ps = sem("mod2_ps")
    mod2_done = sem("mod2_done")
    z_ps = sem("z_ps")
    z_set = sem("z_set")
    z_copied = sem("z_copied")
    v_taken = sem("v_taken")
    zsq_done = sem("zsq_done")
    qk_ms = sem("qk_ms")
    qk_sqrt = sem("qk_sqrt")
    nrm_done = sem("nrm_done")
    rot_done = sem("rot_done")
    t_ps = sem("t_ps")
    t_hi_done = sem("t_hi_done")
    t_done = sem("t_done")
    s_ps = sem("s_ps")
    sm_ready = sem("sm_ready")
    exp_done = sem("exp_done")
    pt_ps = sem("pt_ps")
    ptA_copied = sem("ptA_copied")
    ptB_copied = sem("ptB_copied")
    pv_ps = sem("pv_ps")
    na_done = sem("na_done")
    nat_ps = sem("nat_ps")
    nat_copied = sem("nat_copied")
    na_spilled = sem("na_spilled")
    d_bias = sem("d_bias")
    d_na = [sem(f"d_na{p}") for p in range(PAIRS)]
    na_hi_done = sem("na_hi_done")
    na_split = sem("na_split")
    d_m = [sem(f"d_m{n}") for n in range(2)]
    m2_ps = sem("m2_ps")
    m_sum = sem("m_sum")
    m_hi_done = sem("m_hi_done")
    m_done = sem("m_done")
    d_xn = [sem(f"d_xn{n}") for n in range(2)]
    g_diag = sem("g_diag")
    g_ps = sem("g_ps")
    g_ready = sem("g_ready")
    o_ps = sem("o_ps")
    xn_done = sem("xn_done")
    xss_done = sem("xss_done")
    xms = sem("xms")
    xsqrt = sem("xsqrt")
    nx_done = sem("nx_done")
    h2_ps = sem("h2_ps")
    h2_full = sem("h2_full")
    h2_hi_done = sem("h2_hi_done")
    h2_done = sem("h2_done")
    f1_ps = sem("f1_ps")
    relu_done = sem("relu_done")
    a_done = sem("a_done")
    f2_ps = sem("f2_ps")
    x_done = sem("x_done")
    d_out = sem("d_out")

    G_RAW = (0, 1, 2, 3)
    M1_RAW = (0, 1, 2, 0, 1, 2)
    M1_SLOT = (4, 5, 0, 1, 2, 3)
    A_RAW = (0, 1, 0)
    N_RAW = (0, 1, 2, 3)
    O_RAW = (0, 1, 2, 3, 0, 1, 2, 3)
    O_SLOT = (4, 5, 0, 1, 2, 3, 4, 5)
    F_RAW = (0, 1, 2, 3, 0, 1, 2, 3)
    raws_before = {}
    seen = [0] * 4
    for name, table, turns in (("pool", G_RAW, 1), ("gate", M1_RAW, 4), ("att", A_RAW, PAIRS),
                               ("na", N_RAW, 1), ("out", O_RAW, 1), ("mlp", F_RAW, NFG)):
        raws_before[name] = (table, list(seen))
        for r in table:
            seen[r] += turns

    def landed(phase, turn, r):
        table, before = raws_before[phase]
        s = table[r]
        return s, 16 * (before[s] + turn * table.count(s) + table[:r + 1].count(s))

    block = ctx.enter_context(nc.Block())

    @block.sync
    def _(sp):
        consts = [(ident, "ident"), (ones, "ones"), (c_col, "c_col"), (norm_g, "norm_g"),
                  (ada_b, "ada_b"), (pscale, "pscale"), (edge_inv, "edge_inv"), (pw_raw, "pool_w")]
        for t, name in consts:
            sp.dma_start(t[:], a[name]).then_inc(d_const, 16)
        for k in range(KD):
            sp.dma_start(xT[:, k, :], a["xT"][k]).then_inc(d_x[k], 16)
        for q in range(4):
            sp.dma_start(ada1[:, 4 * q:4 * q + 4, :],
                         a["ada1"][4 * q:4 * q + 4].rearrange("j p n -> p j n")).then_inc(d_ada1[q], 16)

        def load(phase, turn, r, unit, cols=1024):
            s, _ = landed(phase, turn, r)
            sp.dma_start(raw(s)[:, 0:cols], a["units"][unit, :, 0:cols]).then_inc(d_raw[s], 16)

        for g in range(NG):
            load("pool", 0, g, U_POOL + g)
        with sp.Fori(0, 4) as j:
            for r in range(6):
                unit = U_GATE + j * 6 + r
                sp.wait_ge(split, unit - 2)
                load("gate", j, r, unit, 1024 if r % 3 < 2 else 512)
        with sp.Fori(0, PAIRS) as p:
            for r, back in ((0, 0), (1, 2), (2, 1)):
                unit = U_ATT + p * 3 + r
                sp.wait_ge(split, unit - back)
                load("att", p, r, unit)
        for r in range(4):
            sp.wait_ge(split, (U_NA, U_NA - 1, U_NA, U_NA)[r])
            if r == 2:
                sp.wait_ge(pv_ps, 8 * HEADS)
            load("na", 0, r, U_NA + r)
        for r in range(8):
            sp.wait_ge(split, U_OUT + r - 3)
            load("out", 0, r, U_OUT + r)
        with sp.Fori(0, NFG) as g:
            for r in range(8):
                unit = U_MLP + g * 8 + r
                sp.wait_ge(split, unit - 3)
                load("mlp", g, r, unit)
        for dh in range(2):
            for t in range(NT):
                sp.wait_ge(x_done, 16 * (NFG - 1) + 8 * dh + t + 1)
                sp.dma_start(out[t * P:(t + 1) * P, dh * HALF:(dh + 1) * HALF],
                             xn[:, t, dh * HALF:(dh + 1) * HALF]).then_inc(d_out, 16)
        sp.wait_ge(d_out, 16 * 16)

    @block.gpsimd
    def _(pool):
        def split_unit(phase, turn, r, slot, unit, cols=1024):
            s, count = landed(phase, turn, r)
            pool.wait_ge(d_raw[s], count)
            h, l, w = hi(slot)[:, 0:cols], lo(slot)[:, 0:cols], raw(s)[:, 0:cols]
            nc.gpsimd.tensor_tensor(gate_cell[:, 1:2], gate_cell[:, 0:1], gate_cell[:, 0:1], ALU.mult)
            nc.gpsimd.tensor_copy(h, w).then_inc(split_hi, 1)
            pool.wait_ge(split_hi, unit + 1)
            nc.gpsimd.tensor_tensor(l, w, h.bitcast(F32), ALU.subtract).then_inc(split, 1)

        nc.gpsimd.memset(gate_cell[:, 0:1], 1.0).then_inc(cell_set, 1)
        pool.wait_ge(cell_set, 1)
        for g in range(NG):
            split_unit("pool", 0, g, g, U_POOL + g)
        def gate_turn(j):
            for r in range(6):
                d = j * 2 + r // 3
                if isinstance(j, int) and j == 0:
                    if r >= 2:
                        pool.wait_ge(u_ps, 2 * (r - 1))
                else:
                    pool.wait_ge(m1_ps, (d - 2) * 6 + 4 + r % 3)
                split_unit("gate", j, r, M1_SLOT[r], U_GATE + j * 6 + r, 1024 if r % 3 < 2 else 512)
        gate_turn(0)
        with pool.Fori(1, 4) as j:
            gate_turn(j)
        for r in range(3):
            pool.wait_ge(m1_ps, (42, 46, 47)[r])
            split_unit("att", 0, r, r, U_ATT + r)
        with pool.Fori(1, PAIRS) as p:
            pool.wait_ge(z_ps, p * NTA)
            for r in range(3):
                split_unit("att", p, r, r, U_ATT + p * 3 + r)
        pool.wait_ge(z_ps, PAIRS * NTA)
        for r in range(4):
            if r == 2:
                pool.wait_ge(pv_ps, 8 * HEADS)
            split_unit("na", 0, r, r, U_NA + r)
        for r in range(8):
            if 2 <= r < 6:
                pool.wait_ge(m2_ps, 4 * (r - 1))
            if r == 6:
                pool.wait_ge(o_ps, 8)
            split_unit("out", 0, r, O_SLOT[r], U_OUT + r)
        def mlp_turn(g):
            first = isinstance(g, int)
            for r, (kind, c, slot) in enumerate(MLP_ORDER):
                if kind == "w1" and c >= 2:
                    pool.wait_ge(f1_ps, g * 8 + 2 * (c - 2) + 2)
                elif kind == "w1":
                    if first:
                        pool.wait_ge(o_ps, 8)
                    else:
                        pool.wait_ge(f1_ps, (g - 1) * 8 + 2 * (c + 2) + 2)
                elif first:
                    pool.wait_ge(o_ps, 16)
                else:
                    pool.wait_ge(f2_ps, g * 16)
                split_unit("mlp", g, r, slot, U_MLP + g * 8 + r)
        mlp_turn(0)
        with pool.Fori(1, NFG) as g:
            mlp_turn(g)

    @block.tensor
    def _(pe):
        mm = nc.tensor.matmul

        def three(o, wh, wl, xh, xl, first, last):
            mm(o, wh, xh, start=first, stop=False)
            mm(o, wh, xl, start=False, stop=False)
            return mm(o, wl, xh, start=False, stop=last)

        for k in range(KD):
            pe.wait_ge(sq_done, k + 1)
            if k == 0:
                pe.wait_ge(d_const, 8 * 16)
            for t in range(NTA):
                last = mm(bank[0][:, t:t + 1], xsq[:, k % 2, t * P:(t + 1) * P], ones[:, 0:1],
                          start=(k == 0 and t == 0), stop=(k == KD - 1), skip_group_check=True)
            last.then_inc(ssq_ps, 1)
        pe.wait_ge(silu_done, 1)
        for j in range(16):
            pe.wait_ge(d_ada1[j // 4], 16)
            for k in range(KD):
                last = mm(bank[4][:, 2 * j:2 * j + 2], ada1[:, j, k * P:(k + 1) * P], c_silu[:, k, :],
                          start=(k == 0), stop=(k == KD - 1))
        last.then_inc(mod1_ps, 1)
        for t in range(NTA):
            pe.wait_ge(diag_ready, t + 1)
            last = mm(psflat[:, HALF + t * P:HALF + (t + 1) * P], ones[:, :], diag[:, t, :],
                      start=True, stop=True)
        last.then_inc(rb_ps, 1)

        def pool_u(g):
            pe.wait_ge(split, U_POOL + g + 1)
            for half in range(2):
                q = 2 * g + half
                if q >= 4:
                    pe.wait_ge(u_copied, q - 3)
                for k in range(KD):
                    if q == 0:
                        pe.wait_ge(h_done, k + 1)
                    x = slice(half * HALF, (half + 1) * HALF)
                    last = three(bank[4 + q % 4], hi(g)[:, k * P:(k + 1) * P], lo(g)[:, k * P:(k + 1) * P],
                                 hT_hi[:, k, x], hT_lo[:, k, x], k == 0, k == KD - 1)
                last.then_inc(u_ps, 1)

        def pool_y(g):
            if g == 0:
                pe.wait_ge(pw_done, 2)
            pe.wait_ge(d_done, g + 1)
            for half in range(2):
                q = 2 * g + half
                if q >= 4:
                    pe.wait_ge(y_done, q - 3)
                x = slice(half * HALF, (half + 1) * HALF)
                c = POOL_ORDER[g]
                three(bank[q % 4], pw_hi[:, c, :], pw_lo[:, c, :], dT_hi[:, x], dT_lo[:, x],
                      True, True).then_inc(y_ps, 1)

        for g in range(NG):
            pool_u(g)
            if g:
                pool_y(g - 1)
        pool_y(NG - 1)

        def gate_turn(j):
            for e in range(2):
                d = j * 2 + e
                sg, sn, sb = M1_SLOT[3 * e:3 * e + 3]
                for half in range(2):
                    x = slice(half * HALF, (half + 1) * HALF)
                    for n, slot in enumerate((sg, sn)):
                        if half == 0:
                            pe.wait_ge(split, U_GATE + d * 3 + n + 1)
                        if isinstance(j, int) and j == 0 and e == 0:
                            if half == 0 and n == 0:
                                pe.wait_ge(y_done, 8)
                                pe.wait_ge(u_copied, 8)
                        else:
                            pe.wait_ge(sg_done, d * 4 + half * 2 + n - 3)
                        for k in range(KD):
                            w = slice(k * P, (k + 1) * P)
                            last = three(bank[3 * half + n], hi(slot)[:, w], lo(slot)[:, w],
                                         hT_hi[:, k, x], hT_lo[:, k, x], k == 0, k == KD - 1)
                        last.then_inc(m1_ps, 1)
                    if half == 0:
                        pe.wait_ge(split, U_GATE + d * 3 + 3)
                    if not (isinstance(j, int) and j == 0 and e == 0):
                        pe.wait_ge(mp_done, d * 2 + half - 1)
                    for k in range(NG):
                        w = slice(k * P, (k + 1) * P)
                        last = three(bank[3 * half + 2], hi(sb)[:, w], lo(sb)[:, w],
                                     poolT_hi[:, k, x], poolT_lo[:, k, x], k == 0, k == NG - 1)
                    last.then_inc(m1_ps, 1)
            pe.wait_ge(acc_ready, j + 1)
            if not isinstance(j, int):
                pe.wait_ge(mod2_done, j)
            for k in range(KD):
                last = mm(bank[6][:, k:k + 1], acc[:, k * P:(k + 1) * P], ones[:, 0:1],
                          start=True, stop=True)
            last.then_inc(mod2_ps, 1)

        gate_turn(0)
        with pe.Fori(1, 4) as j:
            gate_turn(j)

        def qkv(p, t):
            if t == 0:
                pe.wait_ge(split, U_ATT + p * 3 + 3)
            if not (isinstance(p, int) and p == 0 and t == 0):
                pe.wait_ge(z_copied, p * NTA + t)
            c = 0 if t < NT else 1
            for k in range(KD):
                w = slice(k * P, (k + 1) * P)
                x = slice(t * P, (t + 1) * P)
                last = three(bank[7][:, c * P:384].rearrange("p (u n) -> p u n", n=P),
                             hT_hi[:, k, x], hT_lo[:, k, x],
                             ringA_hi[:, c:3, w], ringA_lo[:, c:3, w], k == 0, k == KD - 1)
            last.then_inc(z_ps, 1)

        def free_banks(s):
            pe.wait_ge(exp_done, s)
            pe.wait_ge(ptA_copied, s)
            pe.wait_ge(ptB_copied, s)
            pe.wait_ge(na_done, s)

        def turn_heads(p, hh):
            s0 = p * 16 + hh * 8
            if hh:
                free_banks(s0)
            else:
                pe.wait_ge(rot_done, p + 1)
            sources = (lambda i: rot_k[:, i, hh, :, :].rearrange("p c n -> p (c n)"),
                       lambda i: rot_q[:, i, hh, :], lambda i: nrm[:, i, hh * HD:(hh + 1) * HD])
            for n, src in enumerate(sources):
                m = HD if n else P
                for half in range(2):
                    for e in range(4):
                        last = nc.tensor.transpose(bank[2 * n + half][0:m, e * P:(e + 1) * P],
                                                   src(4 * half + e), ident[:, :])
                    last.then_inc(t_ps, 1)
            for e in range(2):
                last = nc.tensor.transpose(bank[6][:, e * P:(e + 1) * P],
                                           kc2[:, e, hh, :, :].rearrange("p c n -> p (c n)"), ident[:, :])
            last.then_inc(t_ps, 1)

        def scores(p, hh, i):
            s = p * 16 + hh * 8 + i
            if i == 0:
                pe.wait_ge(t_done, p * 14 + hh * 7 + 7)
            elif i > 1:
                pe.wait_ge(exp_done, s - 1)
            b0 = 2 * (i % 2)
            q = slice(i * P, (i + 1) * P)
            k0 = key_tile(i) * P
            c0 = HD if inner(i) else 0
            mm(bank[b0], qrT[:, q], krT_hi[:, k0:k0 + HALF], start=True, stop=False)
            mm(bank[b0], qrT[:, q], krT_lo[:, k0:k0 + HALF], start=False, stop=True)
            if inner(i):
                k1 = slice(k0 + HALF, k0 + HALF + HD)
                mm(bank[b0 + 1][:, 0:HD], qrT[:, q], krT_hi[:, k1], start=True, stop=False)
                mm(bank[b0 + 1][:, 0:HD], qrT[:, q], krT_lo[:, k1], start=False, stop=True)
            o = bank[b0 + 1][:, c0:c0 + CTX]
            mm(o, qpT[:, q], kcT_hi[:, :], start=True, stop=False)
            mm(o, qpT[:, q], kcT_lo[:, :], start=False, stop=True).then_inc(s_ps, 1)

        def turn_probs(p, hh, i):
            s = p * 16 + hh * 8 + i
            pe.wait_ge(exp_done, s + 1)
            if i:
                pe.wait_ge(ptA_copied, s)
                pe.wait_ge(ptB_copied, s)
            pr = prob[:, i % 2, :]
            for e in range(4):
                last = nc.tensor.transpose(bank[4][:, e * P:(e + 1) * P], pr[:, e * P:(e + 1) * P], ident[:, :])
            c0 = HALF + (HD if inner(i) else 0)
            if inner(i):
                nc.tensor.transpose(bank[5][0:HD, CTX:CTX + P], pr[:, HALF:HALF + HD], ident[:, :])
            for e in range(2):
                last = nc.tensor.transpose(bank[5][:, e * P:(e + 1) * P], pr[:, c0 + e * P:c0 + (e + 1) * P],
                                           ident[:, :])
            last.then_inc(pt_ps, 1)

        def values(p, hh, i):
            s = p * 16 + hh * 8 + i
            pe.wait_ge(ptA_copied, s + 1)
            pe.wait_ge(ptB_copied, s + 1)
            if i:
                pe.wait_ge(na_done, s)
            v = slice(hh * HD, (hh + 1) * HD)
            o = bank[6][:, 0:HD]
            kt = key_tile(i)
            for e in range(4):
                mm(o, probT[:, e, :], vcur[:, kt + e, v], start=(e == 0), stop=False)
            if inner(i):
                mm(o, probT[0:HD, 6, :], vcur[0:HD, kt + 4, v], start=False, stop=False)
            for e in range(2):
                last = mm(o, probT[:, 4 + e, :], vcur[:, NT + e, v], start=False, stop=(e == 1))
            last.then_inc(pv_ps, 1)

        def attend(p, ahead):
            for hh in range(2):
                if ahead:
                    for t in range(3):
                        qkv(p + 1, 5 * hh + t)
                turn_heads(p, hh)
                scores(p, hh, 0)
                for i in range(8):
                    if i < 7:
                        scores(p, hh, i + 1)
                    if ahead and i in (1, 4):
                        qkv(p + 1, 5 * hh + 3 + i // 4)
                    turn_probs(p, hh, i)
                    if i:
                        values(p, hh, i - 1)
                values(p, hh, 7)
            free_banks(p * 16 + 16)
            for half in range(2):
                for e in range(4):
                    last = nc.tensor.transpose(bank[4 + half][:, e * P:(e + 1) * P], na_tok[:, 4 * half + e, :],
                                               ident[:, :])
                last.then_inc(nat_ps, 1)

        pe.wait_ge(sg_done, 32)
        pe.wait_ge(mp_done, 16)
        pe.wait_ge(mod2_done, 4)
        for t in range(NTA):
            qkv(0, t)
        with pe.Fori(0, PAIRS - 1) as p:
            attend(p, True)
        attend(PAIRS - 1, False)

        pe.wait_ge(nat_copied, 2 * PAIRS)
        for q in range(4):
            pe.wait_ge(split, U_NA + q + 1)
            for e in range(2):
                for half in range(2):
                    n = 4 * q + 2 * e + half
                    if n >= 8:
                        pe.wait_ge(m_done, n - 7)
                    x = slice(half * HALF, (half + 1) * HALF)
                    for k in range(PAIRS):
                        if n == 0:
                            pe.wait_ge(na_split, k + 1)
                        w = slice((4 * e + k) * P, (4 * e + k + 1) * P)
                        last = three(bank[n % 8], hi(q)[:, w], lo(q)[:, w], naT_hi[:, k, x], naT_lo[:, k, x],
                                     k == 0, k == PAIRS - 1)
                    last.then_inc(m2_ps, 1)
        pe.wait_ge(g_diag, 8)
        pe.wait_ge(m_done, 16)
        for k in range(KD):
            last = mm(psflat[:, (6 * HALF) + k * P:(6 * HALF) + (k + 1) * P], ones[:, :], gdiag[:, k, :],
                      start=True, stop=True)
        last.then_inc(g_ps, 1)
        for dh in range(2):
            pe.wait_ge(split, U_OUT + 4 * dh + 4)
            for t in range(NT):
                n = 8 * dh + t
                if n >= 4:
                    pe.wait_ge(xn_done, n - 3)
                x = slice(t * P, (t + 1) * P)
                for k in range(KD):
                    slot = O_SLOT[4 * dh + k // 2]
                    w = slice((k % 2) * HALF, (k % 2 + 1) * HALF)
                    last = three(bank[n % 4], mT_hi[:, k, x], mT_lo[:, k, x], hi(slot)[:, w], lo(slot)[:, w],
                                 k == 0, k == KD - 1)
                last.then_inc(o_ps, 1)
        pe.wait_ge(g_diag, 16)
        pe.wait_ge(xn_done, 16)
        for k in range(KD):
            last = mm(psflat[:, k * P:(k + 1) * P], ones[:, :], gdiag[:, k, :], start=True, stop=True)
        last.then_inc(g_ps, 1)
        for half in range(2):
            for k in range(KD):
                n = 8 * half + k
                if n >= 6:
                    pe.wait_ge(h2_full, n - 5)
                for e in range(4):
                    if k == 0:
                        pe.wait_ge(nx_done, 4 * half + e + 1)
                    last = nc.tensor.transpose(bank[2 + n % 6][:, e * P:(e + 1) * P],
                                               nx[half][:, e, k * P:(k + 1) * P], ident[:, :])
                last.then_inc(h2_ps, 1)
        pe.wait_ge(g_ready, 2)
        pe.wait_ge(h2_full, 16)

        def mlp_turn(g):
            first = isinstance(g, int)
            for f in range(FCH):
                slot = f % 2
                unit = U_MLP + g * 8 + (0, 1, 3, 5)[f]
                pe.wait_ge(split, unit + 1)
                for half in range(2):
                    n = 2 * f + half
                    if n >= 4 or not first:
                        pe.wait_ge(a_done, g * 8 + n - 3)
                    x = slice(half * HALF, (half + 1) * HALF)
                    for k in range(KD):
                        if first and f == 0:
                            pe.wait_ge(h2_done, 8 * half + k + 1)
                        w = slice(k * P, (k + 1) * P)
                        last = three(bank[n % 4], hi(slot)[:, w], lo(slot)[:, w], h2_hi[:, k, x], h2_lo[:, k, x],
                                     k == 0, k == KD - 1)
                    last.then_inc(f1_ps, 1)
            for dh in range(2):
                for t in range(NT):
                    n = 8 * dh + t
                    if n >= 4 or not first:
                        pe.wait_ge(x_done, g * 16 + n - 3)
                    x = slice(t * P, (t + 1) * P)
                    w = slice(dh * HALF, (dh + 1) * HALF)
                    for f in range(FCH):
                        if n == 0:
                            pe.wait_ge(a_done, g * 8 + 2 * f + 1)
                            pe.wait_ge(split, U_MLP + g * 8 + (2, 4, 6, 7)[f] + 1)
                        if n == 4:
                            pe.wait_ge(a_done, g * 8 + 2 * f + 2)
                        last = three(bank[4 + n % 4], aT_hi[:, f, x], aT_lo[:, f, x],
                                     hi(2 + f)[:, w], lo(2 + f)[:, w], f == 0, f == FCH - 1)
                    last.then_inc(f2_ps, 1)

        mlp_turn(0)
        with pe.Fori(1, NFG) as g:
            mlp_turn(g)

    @block.scalar
    def _(act):
        fn = nc.scalar.activation
        act.wait_ge(d_const, 8 * 16)
        fn(c_sig[:], c_col[:], ACT.Sigmoid).then_inc(sig_done, 1)
        for k in range(KD):
            act.wait_ge(d_x[k], 16)
            if k >= 2:
                act.wait_ge(ssq_ps, k - 1)
            fn(xsq[:, k % 2, :], xT[:, k, :], ACT.Square).then_inc(sq_done, 1)
        act.wait_ge(ms_ready, 1)
        fn(rt[:, 0:NTA], ms[:, 0:NTA], ACT.Sqrt).then_inc(sqrt_done, 1)
        for k in range(KD):
            act.wait_ge(xr_ready, k + 1)
            if k >= 2:
                act.wait_ge(h_done, k - 1)
            fn(hfull[:, k % 2, 0:L], xT[:, k, 0:L], ACT.Identity,
               bias=mod1[:, k, 0:1], scale=gain1[:, k, 0:1]).then_inc(a_own, 1)
            fn(hfull[:, k % 2, L:T], xT[:, k, L:T], ACT.Identity,
               bias=mod1[:, k, 1:2], scale=gain1[:, k, 1:2]).then_inc(a_own, 1)
            act.wait_ge(a_own, 2 * k + 2)
            fn(hT_hi[:, k, :], hfull[:, k % 2, :], ACT.Copy).then_inc(h_hi_done, 1)
        act.wait_ge(pads_done, 2)

        def u_out(g):
            for half in range(2):
                q = 2 * g + half
                act.wait_ge(u_ps, q + 1)
                if g:
                    act.wait_ge(d_made, g)
                fn(up[:, PAD + half * HALF:PAD + (half + 1) * HALF], bank[4 + q % 4], ACT.Copy)\
                    .then_inc(u_copied, 1)

        def d_out_hi(g):
            act.wait_ge(d_made, g + 1)
            if g:
                act.wait_ge(y_ps, 2 * g)
            fn(dT_hi[:, :], win[0][:, PAD:PAD + L], ACT.Copy).then_inc(d_hi_done, 1)

        def y_out(g):
            c = POOL_ORDER[g]
            for half in range(2):
                q = 2 * g + half
                act.wait_ge(y_ps, q + 1)
                fn(poolT_hi[:, c, half * HALF:(half + 1) * HALF], bank[q % 4], ACT.Copy,
                   scale=pscale[:, c:c + 1]).then_inc(y_hi_done, 1)

        for g in range(NG):
            u_out(g)
            d_out_hi(g)
            if g:
                y_out(g - 1)
        y_out(NG - 1)

        def gate_turn(j):
            first = isinstance(j, int)
            for e in range(2):
                for half in range(2):
                    d = j * 2 + e
                    for n in range(2):
                        u = 4 * e + 2 * half + n
                        if not first or u >= 2:
                            act.wait_ge(ada2_used, j * 8 + u - 1)
                        act.dma_start(ada2[:, n, :], a["ada2"][j * 8 + u]).then_inc(d_ada2[n], 16)
                    act.wait_ge(m1_ps, d * 6 + half * 3 + 1)
                    if not first or e:
                        act.wait_ge(mp_done, d * 2 + half - 1)
                        act.wait_ge(spill_g[half], d * 16)
                    fn(sgp[:, half, :], bank[3 * half], ACT.Sigmoid).then_inc(sg_done, 1)
                    act.wait_ge(m1_ps, d * 6 + half * 3 + 2)
                    fn(sgn[:, half, :], bank[3 * half + 1], ACT.Sigmoid).then_inc(sg_done, 1)
                    act.wait_ge(sg_done, d * 4 + half * 2 + 2)
                    act.dma_start(spill_m[0, d, half], sgn[:, half, :]).then_inc(spill_g[half], 16)
                    if not (first and e == 0 and half == 0):
                        act.wait_ge(mp_done, d * 2 + half)
                        act.dma_start(spill_m[1, d if half else d - 1, 1 - half], mpool[:, 1 - half, :])\
                            .then_inc(spill_p[1 - half], 16)

        act.wait_ge(y_ps, 8)
        act.wait_ge(y_done, 8)
        gate_turn(0)
        with act.Fori(1, 4) as j:
            gate_turn(j)
        act.wait_ge(mp_done, 16)
        act.dma_start(spill_m[1, KD - 1, 1], mpool[:, 1, :]).then_inc(spill_p[1], 16)

        act.wait_ge(m1_ps, 6 * KD)
        act.wait_ge(split, U_ATT)
        act.wait_ge(mod2_done, 4)
        for n in range(2):
            act.wait_ge(spill_g[n], 16 * KD)
            act.wait_ge(spill_p[n], 16 * KD)
        act.dma_start(rope_c[:], a["rope_c"]).then_inc(d_att, 16)
        act.dma_start(rope_s[:], a["rope_s"]).then_inc(d_att, 16)
        act.dma_start(qk_g[:], a["qk_g"]).then_inc(d_att, 16)
        act.dma_start(bias[:, :], a["bias"][0]).then_inc(d_bias, 16)

        def z_out(p, t):
            if t == 0 and not (isinstance(p, int) and p == 0):
                act.wait_ge(nrm_done, p)
            act.wait_ge(z_ps, p * NTA + t + 1)
            c = 0 if t < NT else P
            fn(z[:, t, c:384], bank[7][:, c:384], ACT.Copy).then_inc(z_copied, 1)

        def squares(p):
            act.wait_ge(z_copied, p * NTA + NTA)
            fn(nrm[:, :, :], z[:, :, 0:256], ACT.Square).then_inc(zsq_done, 1)

        def attend(p, ahead):
            act.wait_ge(qk_ms, p + 1)
            fn(rt[:, :], ms[:, :], ACT.Sqrt).then_inc(qk_sqrt, 1)
            for hh in range(2):
                if ahead:
                    for t in range(3):
                        z_out(p + 1, 5 * hh + t)
                dst = (krT_hi[:, 0:HALF], krT_hi[:, HALF:L], qrT[:, 0:HALF], qrT[:, HALF:L],
                       qpT[:, 0:HALF], qpT[:, HALF:L], kcT_hi[:, :])
                for n in range(7):
                    act.wait_ge(t_ps, p * 14 + hh * 7 + n + 1)
                    src = bank[n] if n < 6 else bank[6][:, 0:CTX]
                    m = HD if 2 <= n < 6 else P
                    fn(dst[n][0:m], src[0:m], ACT.Copy).then_inc(t_hi_done, 1)
                for i in range(8):
                    s = p * 16 + hh * 8 + i
                    n = i % 2
                    w = HALF + CTX + (HD if inner(i) else 0)
                    act.wait_ge(sm_ready, s + 1)
                    if i >= 2:
                        act.wait_ge(pt_ps, s - 1)
                        act.wait_ge(na_done, s - 1)
                    fn(prob[:, n, 0:w], psflat[:, 2 * n * HALF:2 * n * HALF + w], ACT.Exp,
                       bias=nmax[:, n:n + 1], accum_out=den[:, n:n + 1]).then_inc(exp_done, 1)
                    if ahead and i in (1, 4):
                        z_out(p + 1, 5 * hh + 3 + i // 4)
                    act.wait_ge(pt_ps, s + 1)
                    if i:
                        act.wait_ge(pv_ps, s)
                    fn(probT[:, 0:4, :], bank[4].rearrange("p (e n) -> p e n", n=P), ACT.Copy)\
                        .then_inc(ptA_copied, 1)
                if ahead or hh == 0:
                    act.dma_start(bias[:, :], a["bias"][p * 2 + hh + 1]).then_inc(d_bias, 16)
            for half in range(2):
                act.wait_ge(nat_ps, p * 2 + half + 1)
                fn(naT_out[:, half * HALF:(half + 1) * HALF], bank[4 + half], ACT.Copy).then_inc(nat_copied, 1)
            act.wait_ge(nat_copied, p * 2 + 2)
            act.dma_start(spill_na[p], naT_out[:, :]).then_inc(na_spilled, 16)
            if ahead:
                squares(p + 1)
                act.wait_ge(na_spilled, p * 16 + 16)

        for t in range(NTA):
            z_out(0, t)
        act.wait_ge(z_set, 1)
        squares(0)
        with act.Fori(0, PAIRS - 1) as p:
            attend(p, True)
        attend(PAIRS - 1, False)

        act.wait_ge(na_spilled, 16 * PAIRS)
        act.wait_ge(na_done, 8 * HEADS)
        for n in range(2):
            act.wait_ge(spill_p[n], 16 * KD)
        for k in range(PAIRS):
            act.dma_start(naT_in[:, k, :], spill_na[k]).then_inc(d_na[k], 16)

        def m_load(n):
            d, half, b = n // 2, n % 2, n % 2
            if n >= 2:
                act.wait_ge(m_done, n - 1)
            act.dma_start(gn_in[:, b, :], spill_m[0, d, half]).then_inc(d_m[b], 16)
            act.dma_start(mp_in[:, b, :], spill_m[1, d, half]).then_inc(d_m[b], 16)

        m_load(0)
        m_load(1)
        for k in range(PAIRS):
            act.wait_ge(d_na[k], 16)
            fn(naT_hi[:, k, :], naT_in[:, k, :], ACT.Copy).then_inc(na_hi_done, 1)
        for n in range(16):
            act.wait_ge(m_sum, n + 1)
            fn(mT_hi[:, n // 2, (n % 2) * HALF:(n % 2 + 1) * HALF], mp_in[:, n % 2, :], ACT.Copy)\
                .then_inc(m_hi_done, 1)
            if n + 2 < 16:
                m_load(n + 2)
        act.wait_ge(m2_ps, 16)
        for n in range(2):
            act.dma_start(xn[:, 4 * n:4 * n + 4, :],
                          a["x"].rearrange("(t p) d -> p t d", p=P)[:, 4 * n:4 * n + 4, :]).then_inc(d_xn[n], 16)
        act.wait_ge(g_ps, 1)
        for n in range(2):
            fn(gb[:, n * HALF:(n + 1) * HALF], bank[6 + n], ACT.Copy).then_inc(g_ready, 1)
        for t in range(NT):
            act.wait_ge(xn_done, 8 + t + 1)
            fn(nx[t // 4][:, t % 4, :], xn[:, t, :], ACT.Square, accum_out=row_ss[:, t:t + 1])\
                .then_inc(xss_done, 1)
            act.wait_ge(xms, t + 1)
            fn(rt[:, t:t + 1], ms[:, t:t + 1], ACT.Sqrt).then_inc(xsqrt, 1)
        act.wait_ge(g_ps, 2)
        for n in range(2):
            fn(gb[:, n * HALF:(n + 1) * HALF], bank[n], ACT.Copy).then_inc(g_ready, 1)
        for n in range(16):
            act.wait_ge(h2_ps, n + 1)
            if n >= 2:
                act.wait_ge(h2_done, n - 1)
            k = n % 8
            fn(otmp[:, n % 2, :], bank[2 + n % 6], ACT.Identity, bias=mod2[:, 1, k:k + 1],
               scale=gain2[:, k:k + 1]).then_inc(h2_full, 1)

        def mlp_turn(g):
            first = isinstance(g, int)
            for n in range(8):
                act.wait_ge(f1_ps, g * 8 + n + 1)
                if n >= 2 or not first:
                    act.wait_ge(a_done, g * 8 + n - 1)
                fn(relu[:, n % 2, :], bank[n % 4], ACT.Relu).then_inc(a_own, 1)
                act.wait_ge(a_own, 16 + g * 8 + n + 1)
                fn(relu[:, n % 2, :], relu[:, n % 2, :], ACT.Square).then_inc(relu_done, 1)

        act.wait_ge(h2_done, 16)
        mlp_turn(0)
        with act.Fori(1, NFG) as g:
            mlp_turn(g)

    @block.vector
    def _(dve):
        V = nc.vector
        own = Steps(dve, v_own)

        def rsqrt_begin(src, n, count, ready):
            V.tensor_scalar(ms[:, n], src, 1.0 / count, EPS, ALU.mult, ALU.add).then_inc(ready, 1)

        def rsqrt_end(n):
            own.link(V.reciprocal(rs[:, n], rt[:, n]))
            own.link(V.tensor_tensor(rt[:, n], rs[:, n], rs[:, n], ALU.mult))
            own.link(V.tensor_tensor(rt[:, n], rt[:, n], ms[:, n], ALU.mult))
            own.link(V.tensor_scalar(rt[:, n], rt[:, n], -0.5, 1.5, ALU.mult, ALU.add))
            own.link(V.tensor_tensor(rs[:, n], rs[:, n], rt[:, n], ALU.mult))

        dve.wait_ge(sig_done, 1)
        V.tensor_tensor(c_silu[:], c_col[:], c_sig[:], ALU.mult).then_inc(silu_done, 1)
        own.link(V.tensor_copy(pw_hi[:], pw_raw[:]))
        V.tensor_copy(edge_tmp[:, 0:1], ones[:, 0:1]).then_inc(pw_done, 1)
        dve.wait_ge(ssq_ps, KD)
        rsqrt_begin(bank[0][:, 0:NTA], slice(0, NTA), D, ms_ready)
        dve.wait_ge(sqrt_done, 1)
        dve.wait_ge(ms_ready, 1)
        rsqrt_end(slice(0, NTA))
        for t in range(NTA):
            V.tensor_scalar(diag[:, t, :], ident[:, :], rs[:, t:t + 1], None, ALU.mult).then_inc(diag_ready, 1)
        dve.wait_ge(mod1_ps, 1)
        own.link(V.tensor_tensor(mod1[:], bank[4][:, 0:32].rearrange("p (j c) -> p j c", c=2),
                                 ada_b[:, 0:16].unsqueeze(2).to_broadcast([P, 16, 2]), ALU.add))
        own.link(V.scalar_tensor_tensor(out=gain1[:], in0=mod1[:, 8:16, :], scalar=1.0,
                                        in1=norm_g[:, 0, :].unsqueeze(2).to_broadcast([P, KD, 2]),
                                        op0=ALU.add, op1=ALU.mult))
        dve.wait_ge(rb_ps, 1)

        def h_lo(k):
            dve.wait_ge(h_hi_done, k + 1)
            V.tensor_tensor(hT_lo[:, k, :], hfull[:, k % 2, :], hT_hi[:, k, :].bitcast(F32), ALU.subtract)\
                .then_inc(h_done, 1)

        for k in range(KD):
            V.tensor_tensor(xT[:, k, :], xT[:, k, :], psflat[:, HALF:HALF + T], ALU.mult).then_inc(xr_ready, 1)
            if k:
                h_lo(k - 1)
        h_lo(KD - 1)

        V.memset(up[:, 0:PAD], 0.0).then_inc(pads_done, 1)
        V.memset(up[:, PAD + L:W], 0.0).then_inc(pads_done, 1)
        V.tensor_tensor(pw_lo[:], pw_raw[:], pw_hi[:].bitcast(F32), ALU.subtract).then_inc(pw_done, 1)

        def y_lo(g):
            c = POOL_ORDER[g]
            for half in range(2):
                q = 2 * g + half
                dve.wait_ge(y_hi_done, q + 1)
                x = slice(half * HALF, (half + 1) * HALF)
                V.scalar_tensor_tensor(out=poolT_lo[:, c, x], in0=bank[q % 4], scalar=pscale[:, c:c + 1],
                                       in1=poolT_hi[:, c, x].bitcast(F32), op0=ALU.mult, op1=ALU.subtract)\
                    .then_inc(y_done, 1)

        for g in range(NG):
            w = WINDOWS[g]
            dve.wait_ge(u_copied, 2 * g + 2)
            dve.wait_ge(pads_done, 2)
            if g:
                dve.wait_ge(d_hi_done, g)
                dve.wait_ge(d_done, g)
            b = (w.bit_length() - 1) % 2
            own.link(V.tensor_tensor(win[b][:, 1:W - 1], up[:, 0:W - 2], up[:, 1:W - 1], ALU.add))
            src, step, lo_i = win[b], 1, 1
            while 2 * step < w:
                b = 1 - b
                lo_i += step
                hi_i = W - lo_i
                own.link(V.tensor_tensor(win[b][:, lo_i:hi_i], src[:, lo_i - step:hi_i - step],
                                         src[:, lo_i + step:hi_i + step], ALU.add))
                src, step = win[b], 2 * step
            assert b == 1
            own.link(V.scalar_tensor_tensor(out=win[0][:, PAD:PAD + L], in0=src[:, PAD:PAD + L], scalar=1.0 / w,
                                            in1=up[:, PAD:PAD + L], op0=ALU.mult, op1=ALU.subtract))
            for n, e0 in enumerate((PAD, L)):
                e = slice(e0, e0 + PAD)
                own.link(V.tensor_tensor(edge_tmp[:, :], src[:, e], edge_inv[:, POOL_ORDER[g], n * PAD:(n + 1) * PAD],
                                         ALU.mult))
                ins = V.tensor_tensor(win[0][:, e], edge_tmp[:, :], up[:, e], ALU.subtract)
                if n:
                    ins.then_inc(d_made, 1)
                else:
                    own.link(ins)
            dve.wait_ge(d_hi_done, g + 1)
            V.tensor_tensor(dT_lo[:, :], win[0][:, PAD:PAD + L], dT_hi[:, :].bitcast(F32), ALU.subtract)\
                .then_inc(d_done, 1)
            if g:
                y_lo(g - 1)
        y_lo(NG - 1)

        def gate_turn(j):
            first = isinstance(j, int)
            for e in range(2):
                for half in range(2):
                    d = j * 2 + e
                    for n in range(2):
                        k = 4 * e + 2 * half + n
                        dve.wait_ge(d_ada2[n], j * 64 + (k // 2) * 16 + 16)
                        if k == 0:
                            if not first:
                                dve.wait_ge(mod2_ps, j)
                            ins = V.tensor_scalar(acc[:, :], ada2[:, n, :], c_silu[:, k, 0:1], None, ALU.mult)
                        else:
                            dve.wait_ge(ada2_used, j * 8 + k)
                            ins = V.scalar_tensor_tensor(out=acc[:, :], in0=ada2[:, n, :], scalar=c_silu[:, k, 0:1],
                                                         in1=acc[:, :], op0=ALU.mult, op1=ALU.add)
                        ins.then_inc(ada2_used, 1)
                    dve.wait_ge(sg_done, d * 4 + half * 2 + 1)
                    dve.wait_ge(m1_ps, d * 6 + half * 3 + 3)
                    if not first or e:
                        dve.wait_ge(spill_p[half], d * 16)
                    V.tensor_tensor(mpool[:, half, :], sgp[:, half, :], bank[3 * half + 2], ALU.mult)\
                        .then_inc(mp_done, 1)
            dve.wait_ge(ada2_used, j * 8 + 8)
            V.tensor_copy(edge_tmp[:, 0:1], acc[:, 0:1]).then_inc(acc_ready, 1)
            dve.wait_ge(mod2_ps, j + 1)
            V.tensor_copy(mod2[:, j, :], bank[6][:, 0:KD]).then_inc(mod2_done, 1)

        gate_turn(0)
        with dve.Fori(1, 4) as j:
            gate_turn(j)

        dve.wait_ge(mod2_done, 4)
        own.link(V.tensor_tensor(mod2[:], mod2[:], ada_b[:, 16:48].rearrange("p (m k) -> p m k", k=KD), ALU.add))
        own.link(V.scalar_tensor_tensor(out=gain2[:, :], in0=mod2[:, 2, :], scalar=1.0, in1=norm_g[:, 1, :],
                                        op0=ALU.add, op1=ALU.mult))
        dve.wait_ge(m1_ps, 6 * KD)
        dve.wait_ge(sg_done, 4 * KD)
        V.memset(z[:, NT:NTA, 0:P], 1.0).then_inc(z_set, 1)
        dve.wait_ge(d_att, 48)
        own.link(V.tensor_scalar(qk_g[:, 0:P], qk_g[:, 0:P], HD ** -0.5, None, ALU.mult))

        def prepare(p):
            dve.wait_ge(z_copied, p * NTA + NTA)
            V.tensor_copy(vcur[:, :, :], z[:, :, 256:384]).then_inc(v_taken, 1)
            dve.wait_ge(zsq_done, p + 1)
            segs = nrm[:, :, :].rearrange("p t (s n) -> p (t s) n", n=HD)
            own.link(V.tensor_reduce(rs[:, :], segs, AX.X, ALU.add))
            rsqrt_begin(rs[:, :], slice(0, 40), HD, qk_ms)
            dve.wait_ge(qk_sqrt, p + 1)
            rsqrt_end(slice(0, 40))
            zseg = z[:, :, 0:256].rearrange("p t (s n) -> p t s n", n=HD)
            own.link(V.tensor_tensor(nrm[:, :, :].rearrange("p t (s n) -> p t s n", n=HD), zseg,
                                     rs[:, :].rearrange("p (t s) -> p t s", s=4).unsqueeze(3)
                                     .to_broadcast([P, NTA, 4, HD]), ALU.mult))
            V.tensor_tensor(nrm[:, :, :], nrm[:, :, :], qk_g[:, :].unsqueeze(1).to_broadcast([P, NTA, 256]),
                            ALU.mult).then_inc(nrm_done, 1)
            dve.wait_ge(nrm_done, p + 1)
            for e in range(2):
                own.done(V.tensor_copy(kc2[:, e, :, :, :],
                                       nrm[:, NT + e, P:2 * P].rearrange("p (h n) -> p h n", n=HD).unsqueeze(2)
                                       .to_broadcast([P, 2, 2, HD])))
            for s in range(4):
                x = slice(s * HD, (s + 1) * HD)
                prod = rot_q[:, :, s, :] if s < 2 else rot_k[:, :, s - 2, 1, :]
                own.link(V.tensor_tensor(prod, nrm[:, 0:NT, x], rope_c[:, :, :], ALU.mult))
                xh = nrm[:, 0:NT, x].rearrange("p t (c h n) -> p t c h n", h=2, n=HD // 4)
                sh = rope_s[:, :, :].rearrange("p t (c h n) -> p t c h n", h=2, n=HD // 4)
                th = rope_t[:, :, :].rearrange("p t (c h n) -> p t c h n", h=2, n=HD // 4)
                for h in range(2):
                    own.done(V.tensor_tensor(th[:, :, :, h, :], xh[:, :, :, 1 - h, :], sh[:, :, :, h, :], ALU.mult))
                own.wait()
                if s < 2:
                    own.link(V.tensor_tensor(prod, prod, rope_t[:, :, :], ALU.add))
                    continue
                both = [P, NT, 2, HD]
                ins = V.tensor_tensor(rot_k[:, :, s - 2, :, :], prod.unsqueeze(2).to_broadcast(both),
                                      rope_t[:, :, :].unsqueeze(2).to_broadcast(both), ALU.add)
                if s < 3:
                    own.link(ins)
                else:
                    ins.then_inc(rot_done, 1)

        def head_parts(p, hh):
            for n in range(7):
                dve.wait_ge(t_hi_done, p * 14 + hh * 7 + n + 1)
                if 2 <= n < 6:
                    q = (qrT, qpT)[n // 2 - 1][:, (n % 2) * HALF:(n % 2 + 1) * HALF]
                    ins = V.tensor_tensor(q[HD:P], bank[n][0:HD, :], q[0:HD].bitcast(F32), ALU.subtract)
                elif n < 2:
                    x = slice((n % 2) * HALF, (n % 2 + 1) * HALF)
                    ins = V.tensor_tensor(krT_lo[:, x], bank[n], krT_hi[:, x].bitcast(F32), ALU.subtract)
                else:
                    ins = V.tensor_tensor(kcT_lo[:, :], bank[6][:, 0:CTX], kcT_hi[:, :].bitcast(F32), ALU.subtract)
                ins.then_inc(t_done, 1)

        def soften(p, hh, i):
            s = p * 16 + hh * 8 + i
            n = i % 2
            w = HALF + (HD if inner(i) else 0)
            b0 = SLOTS_FULL * GRID_W if inner(i) else (2 * key_tile(i) - 2 * i + 6) * GRID_W
            flat = psflat[:, 2 * n * HALF:2 * n * HALF + w + CTX]
            dve.wait_ge(s_ps, s + 1)
            if i == 0:
                dve.wait_ge(d_bias, p * 32 + hh * 16 + 16)
            own.done(V.tensor_reduce(cmax[:, n:n + 1], flat[:, w:w + CTX], AX.X, ALU.max))
            own.link(V.tensor_tensor_reduce(flat[:, 0:w], flat[:, 0:w], bias[:, b0:b0 + w], 1.0,
                                            BIG, ALU.add, ALU.max, smax[:, n:n + 1]))
            V.tensor_scalar(nmax[:, n:n + 1], smax[:, n:n + 1], cmax[:, n:n + 1], -1.0, ALU.max, ALU.mult)\
                .then_inc(sm_ready, 1)

        def take_ctx_probs(p, hh, i):
            s = p * 16 + hh * 8 + i
            dve.wait_ge(pt_ps, s + 1)
            if i:
                dve.wait_ge(pv_ps, s)
            if inner(i):
                own.done(V.tensor_copy(probT[0:HD, 6, :], bank[5][0:HD, CTX:CTX + P]))
            else:
                own.done(V.tensor_copy(edge_tmp[:, 0:1], ones[:, 0:1]))
            own.wait()
            V.tensor_copy(probT[:, 4:6, :], bank[5][:, 0:CTX].rearrange("p (e n) -> p e n", n=P))\
                .then_inc(ptB_copied, 1)

        def take_values(p, hh, i):
            s = p * 16 + hh * 8 + i
            n = i % 2
            dve.wait_ge(exp_done, s + 1)
            own.link(V.reciprocal(rden[:, n:n + 1], den[:, n:n + 1]))
            dve.wait_ge(pv_ps, s + 1)
            V.tensor_scalar(na_tok[:, i, hh * HD:(hh + 1) * HD], bank[6][:, 0:HD], rden[:, n:n + 1], None,
                            ALU.mult).then_inc(na_done, 1)

        def attend(p):
            prepare(p)
            for hh in range(2):
                head_parts(p, hh)
                soften(p, hh, 0)
                for i in range(8):
                    if i < 7:
                        soften(p, hh, i + 1)
                    take_ctx_probs(p, hh, i)
                    if i:
                        take_values(p, hh, i - 1)
                take_values(p, hh, 7)

        PER = 7 + 2 + 15 + 2 * 8 * (2 + 1 + 1)
        with dve.Fori(0, PAIRS) as p:
            own.enter(p, 0, PER)
            attend(p)
        own.leave(PAIRS)

        dve.wait_ge(nat_ps, 2 * PAIRS)
        for k in range(KD):
            V.tensor_scalar(gdiag[:, k, :], ident[:, :], mod2[:, 0, k:k + 1], None, ALU.mult).then_inc(g_diag, 1)
        for k in range(PAIRS):
            dve.wait_ge(na_hi_done, k + 1)
            V.tensor_tensor(naT_lo[:, k, :], naT_in[:, k, :], naT_hi[:, k, :].bitcast(F32), ALU.subtract)\
                .then_inc(na_split, 1)
        for n in range(16):
            b = n % 2
            dve.wait_ge(m2_ps, n + 1)
            dve.wait_ge(d_m[b], 32 * (n // 2 + 1))
            own.link(V.tensor_tensor(gn_in[:, b, :], gn_in[:, b, :], bank[n % 8], ALU.mult))
            V.tensor_tensor(mp_in[:, b, :], mp_in[:, b, :], gn_in[:, b, :], ALU.add).then_inc(m_sum, 1)
            dve.wait_ge(m_hi_done, n + 1)
            x = slice((n % 2) * HALF, (n % 2 + 1) * HALF)
            V.tensor_tensor(mT_lo[:, n // 2, x], mp_in[:, b, :], mT_hi[:, n // 2, x].bitcast(F32), ALU.subtract)\
                .then_inc(m_done, 1)
        dve.wait_ge(g_ps, 1)
        dve.wait_ge(g_ready, 2)
        for k in range(KD):
            V.tensor_scalar(gdiag[:, k, :], ident[:, :], mod2[:, 3, k:k + 1], None, ALU.mult).then_inc(g_diag, 1)

        def renorm(t):
            dve.wait_ge(xss_done, t + 1)
            rsqrt_begin(row_ss[:, t:t + 1], slice(t, t + 1), D, xms)
            dve.wait_ge(xsqrt, t + 1)
            dve.wait_ge(xms, t + 1)
            rsqrt_end(slice(t, t + 1))
            V.tensor_scalar(nx[t // 4][:, t % 4, :], xn[:, t, :], rs[:, t:t + 1], None, ALU.mult)\
                .then_inc(nx_done, 1)

        for dh in range(2):
            for t in range(NT):
                n = 8 * dh + t
                dve.wait_ge(o_ps, n + 1)
                if dh == 0 and t % 4 == 0:
                    dve.wait_ge(d_xn[t // 4], 16)
                x = slice(dh * HALF, (dh + 1) * HALF)
                own.link(V.tensor_tensor(otmp[:, n % 2, :], gb[:, x], bank[n % 4], ALU.mult))
                V.tensor_tensor(xn[:, t, x], xn[:, t, x], otmp[:, n % 2, :], ALU.add).then_inc(xn_done, 1)
                if dh and t:
                    renorm(t - 1)
        renorm(NT - 1)
        for n in range(16):
            half, k = n // 8, n % 8
            x = slice(half * HALF, (half + 1) * HALF)
            dve.wait_ge(h2_full, n + 1)
            own.link(V.tensor_copy(h2_hi[:, k, x], otmp[:, n % 2, :]))
            V.tensor_tensor(h2_lo[:, k, x], otmp[:, n % 2, :], h2_hi[:, k, x].bitcast(F32), ALU.subtract)\
                .then_inc(h2_done, 1)

        def mlp_turn(g):
            first = isinstance(g, int)
            for n in range(8):
                f, x = n // 2, slice((n % 2) * HALF, (n % 2 + 1) * HALF)
                dve.wait_ge(relu_done, g * 8 + n + 1)
                if not first and n == 0:
                    dve.wait_ge(f2_ps, g * 16)
                own.link(V.tensor_copy(aT_hi[:, f, x], relu[:, n % 2, :]))
                V.tensor_tensor(aT_lo[:, f, x], relu[:, n % 2, :], aT_hi[:, f, x].bitcast(F32), ALU.subtract)\
                    .then_inc(a_done, 1)
            for n in range(16):
                dh, t = n // 8, n % 8
                x = slice(dh * HALF, (dh + 1) * HALF)
                dve.wait_ge(f2_ps, g * 16 + n + 1)
                if n == 0 and first:
                    dve.wait_ge(g_ready, 4)
                own.link(V.tensor_tensor(ytmp[:, n % 2, :], gb[:, x], bank[4 + n % 4], ALU.mult))
                V.tensor_tensor(xn[:, t, x], xn[:, t, x], ytmp[:, n % 2, :], ALU.add).then_inc(x_done, 1)

        mlp_turn(0)
        with dve.Fori(1, NFG) as g:
            own.enter(g, 1, 24)
            mlp_turn(g)
        own.leave(NFG - 1)


def shape_constants():
    t = np.arange(L)
    n_freq = HD // 4
    inv = np.float32(10000.0) ** (-np.arange(n_freq, dtype=np.float32) / np.float32(n_freq))
    ang = [(t // GRID_W).astype(np.float32)[:, None] * inv, (t % GRID_W).astype(np.float32)[:, None] * inv]
    cos = np.concatenate([f(x) for x in ang for f in (np.cos, np.cos)], 1)
    sin = np.concatenate([s * np.sin(x) for x in ang for s in (np.float32(-1), np.float32(1))], 1)
    tile = lambda m: np.ascontiguousarray(m.reshape(NT, P, HD).transpose(1, 0, 2).astype(np.float32))
    edge = np.zeros((NG, 2 * PAD), np.float32)
    for g, w in enumerate((2, 4, 8, 16)):
        pos = np.concatenate([np.arange(PAD), np.arange(L - PAD, L)])
        edge[g] = 1.0 / (np.minimum(pos + w // 2, L) - np.maximum(pos - w // 2, 0))
    return {"rope_c": tile(cos), "rope_s": tile(sin), "ident": np.eye(P, dtype=np.float32),
            "ones": np.ones((P, P), np.float32),
            "edge_inv": np.ascontiguousarray(np.broadcast_to(edge, (P, NG, 2 * PAD)))}


def bias_layout(rpb):
    q = np.arange(GRID_W)
    c0 = np.clip(q - NA_COLS // 2, 0, GRID_W - NA_COLS)
    rel = q[None, :] - q[:, None] + NA_COLS - 1
    seen = (q[None, :] >= c0[:, None]) & (q[None, :] < c0[:, None] + NA_COLS)
    rel = np.where(seen, rel, 0)
    out = np.full((HEADS, 2, GRID_W, SLOTS_FULL + SLOTS_INNER, GRID_W), BIG, np.float32)
    for odd in range(2):
        for s in range(SLOTS_FULL):
            out[:, odd, :, s, :] = np.where(seen[None], rpb[:, s + 1 - odd][:, rel], np.float32(BIG))
        for m in range(SLOTS_INNER):
            if m - odd in range(NA_ROWS):
                out[:, odd, :, SLOTS_FULL + m, :] = out[:, odd, :, m + 2, :]
    return out.reshape(HEADS, P, BIASW)


def by_k(w):
    return w.reshape(-1, P, w.shape[1]).transpose(1, 0, 2).reshape(P, -1)


def units_layout(i):
    w_in, w_bp, w_bn = i["w_in"][0], i["w_branch_pool"][0], i["w_branch_na"][0]
    w_out, w1, w2 = i["w_out"][0], i["mlp_w1"][0], i["mlp_w2"][0]
    u = np.zeros((UNITS, P, 1024), np.float32)
    for n, g in enumerate(POOL_ORDER):
        u[U_POOL + n] = by_k(w_in[:, g * P:(g + 1) * P])
    for d in range(KD):
        c = slice(d * P, (d + 1) * P)
        u[U_GATE + 3 * d] = by_k(w_in[:, 2048:3072][:, c])
        u[U_GATE + 3 * d + 1] = by_k(w_in[:, 3072:4096][:, c])
        u[U_GATE + 3 * d + 2, :, 0:512] = by_k(w_bp[:, c])
        u[U_NA + d // 2, :, (d % 2) * 512:(d % 2 + 1) * 512] = by_k(w_bn[:, c])
    for p in range(PAIRS):
        for n in range(3):
            u[U_ATT + 3 * p + n] = by_k(w_in[:, 512 * (n + 1) + p * P:512 * (n + 1) + (p + 1) * P])
    for dh in range(2):
        for n in range(4):
            u[U_OUT + 4 * dh + n] = by_k(w_out[n * 256:(n + 1) * 256, dh * HALF:(dh + 1) * HALF])
    for g in range(NFG):
        for r, (kind, c, _) in enumerate(MLP_ORDER):
            f = slice(g * FG + c * P, g * FG + (c + 1) * P)
            u[U_MLP + 8 * g + r] = by_k(w1[:, f]) if kind == "w1" else w2[f]
    return u


def lay_out(inputs):
    i = {k: np.asarray(v) for k, v in inputs.items()}
    x = i["x"][0]
    ada = i["ada_w"][0]
    col = lambda v: np.ascontiguousarray(v.reshape(-1, P).T)
    g = {
        "x": x,
        "xT": np.concatenate([x, i["ctx"][0]], 0).T.reshape(KD, P, T),
        "c_col": np.stack([col(i["c"][0]), col(i["c_ctx"])], -1),
        "norm_g": np.stack([col(i["norm1_g"][0]), col(i["norm2_g"][0])], 1),
        "ada_b": col(i["ada_b"][0]),
        "pscale": col(i["pool_scale"][0]),
        "pool_w": i["pool_w"][0].transpose(1, 0, 2),
        "qk_g": np.broadcast_to(np.concatenate([i["q_norm_g"][0]] * 2 + [i["k_norm_g"][0]] * 2), (P, 256)),
        "ada1": np.stack([by_k(ada[:, j * P:(j + 1) * P]) for j in range(16)]),
        "ada2": ada[:, 2048:].reshape(KD, P, 4, 1024).transpose(2, 0, 1, 3).reshape(32, P, 1024),
        "bias": bias_layout(i["rpb"][0]),
        "units": units_layout(i),
    }
    g.update(shape_constants())
    return {k: np.ascontiguousarray(v) for k, v in g.items()}


def kernel(**inputs):
    import concourse.bacc as bacc
    from concourse.bass_utils import run_bass_kernel_spmd

    nc = bacc.Bacc("TRN2", target_bir_lowering=False, num_devices=1)
    arrays = {f"in_{k}": v for k, v in lay_out(inputs).items()}
    a = {k[3:]: nc.dram_tensor(k, v.shape, F32, kind="ExternalInput").ap() for k, v in arrays.items()}
    out = nc.dram_tensor("x_out", (L, D), F32, kind="ExternalOutput").ap()
    build(nc, a, out)
    r = run_bass_kernel_spmd(nc, [arrays], core_ids=[0])
    return r.results[0]["x_out"].reshape(1, L, D)
```

```python
from contextlib import ExitStack

import numpy as np
import concourse.bass as bass
from concourse import mybir

P = 128
D = 1024
L = 1024
CTX = 256
T = L + CTX
KD = D // P
NT = L // P
NTA = T // P
GRID_W = 64
ROWS = L // GRID_W
WINDOWS = (16, 8, 4, 2)
POOL_ORDER = (3, 2, 1, 0)
NG = 4
PAD = 8
HD = 64
HEADS = 8
PAIRS = HEADS // 2
NA_ROWS, NA_COLS = 8, 16
D_FF = 4096
FG = 512
NFG = D_FF // FG
FCH = FG // P
EPS = 1e-6
HALF = 512
BIG = -1e30
SLOTS_FULL = 14
SLOTS_INNER = 9
BIASW = (SLOTS_FULL + SLOTS_INNER) * GRID_W

U_POOL = 0
U_GATE = U_POOL + NG
U_ATT = U_GATE + 3 * KD
U_NA = U_ATT + 3 * PAIRS
U_OUT = U_NA + 4
U_MLP = U_OUT + 8
UNITS = U_MLP + 8 * NFG
FIRST_ORDER = (0, 2, 1, 3, 4, 5, 6, 7)
MLP_ORDER = (("w1", 0, 0), ("w1", 1, 1), ("w2", 0, 2), ("w1", 2, 0),
             ("w2", 1, 3), ("w1", 3, 1), ("w2", 2, 4), ("w2", 3, 5))

F32 = mybir.dt.float32
F32R = mybir.dt.float32r
ALU = mybir.AluOpType
ACT = mybir.ActivationFunctionType
AX = mybir.AxisListType


def key_tile(i):
    return min(max(i - 2, 0), 4)


def inner(i):
    return 2 <= i <= 5


class Steps:

    def __init__(self, eng, sem):
        self.eng, self.sem, self.base, self.n = eng, sem, 0, 0

    def done(self, ins):
        ins.then_inc(self.sem, 1)
        self.n += 1

    def wait(self):
        self.eng.wait_ge(self.sem, self.base + self.n)

    def link(self, ins):
        self.done(ins)
        self.wait()

    def enter(self, i, first, per_turn):
        self.base, self.n, self.per, self.start = self.start_of(i, first, per_turn), 0, per_turn, self.base + self.n

    def start_of(self, i, first, per_turn):
        return (i - first) * per_turn + (self.base + self.n)

    def leave(self, turns):
        assert self.n == self.per, (self.n, self.per)
        self.base, self.n = self.start + self.per * turns, 0


def build(nc, a, out):
    with ExitStack() as ctx:
        build_in(nc, a, out, ctx)


def build_in(nc, a, out, ctx):
    KB = 1024
    CONST = 32 * KB
    H = 35 * KB
    R = H + 80 * KB
    base = 16 * KB + 512

    def at(name, shape, dt, off):
        return nc.alloc_sbuf_tensor_at(name, shape, dt, offset=base + off)

    ringA_hi = at("ringA_hi", [P, 3, 1024], F32R, 0)
    ringA_lo = at("ringA_lo", [P, 3, 1024], F32R, 12 * KB)
    rawA = at("rawA", [P, 2, 1024], F32, 24 * KB)
    off = CONST
    def const(name, shape, dt=F32):
        nonlocal off
        n = 4 * int(np.prod(shape[1:]))
        t = at(name, shape, dt, off)
        off += (n + 31) // 32 * 32
        assert off <= H
        return t
    ident = const("ident", [P, P])
    ones = const("ones", [P, P])
    c_col = const("c_col", [P, KD, 2])
    c_sig = const("c_sig", [P, KD, 2])
    c_silu = const("c_silu", [P, KD, 2])
    norm_g = const("norm_g", [P, 2, KD])
    ada_b = const("ada_b", [P, 48])
    pscale = const("pscale", [P, NG])
    edge_inv = const("edge_inv", [P, NG, 2 * PAD])
    edge_tmp = const("edge_tmp", [P, PAD])
    mod1 = const("mod1", [P, 16, 2])
    gain1 = const("gain1", [P, KD, 2])
    mod2 = const("mod2", [P, 4, KD])
    gain2 = const("gain2", [P, KD])
    ms = const("ms", [P, 40])
    rs = const("rs", [P, 40])
    rt = const("rt", [P, 40])
    row_ss = const("row_ss", [P, NT])
    cmax = const("cmax", [P, 2])
    smax = const("smax", [P, 2])
    nmax = const("nmax", [P, 2])
    den = const("den", [P, 4])
    rden = const("rden", [P, 4])
    ringB_hi = at("ringB_hi", [P, 3, 1024], F32R, R)
    ringB_lo = at("ringB_lo", [P, 3, 1024], F32R, R + 12 * KB)
    rawB = at("rawB", [P, 2, 1024], F32, R + 24 * KB)
    ada1 = at("ada1", [P, KD, 2048], F32, H)
    xsq = at("xsq", [P, 2, T], F32, H + 64 * KB)
    xsum = at("xsum", [P, T], F32, H + 74 * KB)
    xT = at("xT", [P, KD, T], F32, R + 32 * KB)
    hfull = at("hfull", [P, 2, L], F32, R + 72 * KB)
    mod_row = at("mod_row", [2, 2048], F32, R + 72 * KB)
    diag = at("diag", [P, NTA, P], F32, R + 82 * KB)
    rctx = diag[:, 0:CTX // P, :].rearrange("p t n -> p (t n)")
    hT_hi = at("hT_hi", [P, KD, T], F32R, H)
    hT_lo = at("hT_lo", [P, KD, T], F32R, H + 40 * KB)
    poolT_hi = at("poolT_hi", [P, NG, L], F32R, R + 32 * KB)
    poolT_lo = at("poolT_lo", [P, NG, L], F32R, R + 48 * KB)
    W = L + 2 * PAD
    up = at("up", [P, W], F32, R + 64 * KB)
    win = [at(f"win{n}", [P, W], F32, R + 64 * KB + 4160 * (n + 1)) for n in range(2)]
    dT_hi = at("dT_hi", [P, L], F32R, R + 64 * KB + 12480)
    dT_lo = at("dT_lo", [P, L], F32R, R + 64 * KB + 16576)
    pw_lo = at("pw_lo", [P, NG, P], F32R, R + 64 * KB + 20672)
    pw_raw = at("pw_raw", [P, NG, P], F32, R + 89088)
    pw_hi = at("pw_hi", [P, NG, P], F32R, R + 91136)
    sgp = at("sgp", [P, 2, HALF], F32, R + 64 * KB)
    sgn = at("sgn", [P, 2, HALF], F32, R + 68 * KB)
    mpool = at("mpool", [P, 2, HALF], F32, R + 72 * KB)
    acc = at("acc", [P, 1024], F32, R + 76 * KB)
    ada2 = at("ada2", [P, 2, 1024], F32, R + 80 * KB)
    qrT = at("qrT", [P, L], F32R, R)
    qpT = at("qpT", [P, L], F32R, R + 4 * KB)
    krT_hi = at("krT_hi", [P, L], F32R, R + 8 * KB)
    krT_lo = at("krT_lo", [P, L], F32R, R + 12 * KB)
    kcT_hi = at("kcT_hi", [P, CTX], F32R, R + 16 * KB)
    kcT_lo = at("kcT_lo", [P, CTX], F32R, R + 17 * KB)
    vcur = at("vcur", [P, NTA, P], F32, R + 18 * KB)
    probT = at("probT", [P, 7, P], F32, R + 23 * KB)
    rope_c = at("rope_c", [P, NT, HD], F32, R + 26 * KB + 512)
    rope_s = at("rope_s", [P, NT, HD], F32, R + 28 * KB + 512)
    qk_g = at("qk_g", [P, 256], F32, R + 30 * KB + 512)
    z = at("z", [P, NTA, 384], F32, R + 32 * KB)
    nrm = at("nrm", [P, NTA, 256], F32, R + 47 * KB)
    rot_q = at("rot_q", [P, NT, 2, HD], F32, R + 57 * KB)
    rot_k = at("rot_k", [P, NT, 2, 2, HD], F32, R + 61 * KB)
    kc2 = at("kc2", [P, 2, 2, 2, HD], F32, R + 69 * KB)
    rope_t = at("rope_t", [P, NT, HD], F32, R + 71 * KB)
    prob = at("prob", [P, 2, 832], F32, R + 73 * KB)
    bias = at("bias", [P, BIASW], F32, R + 73 * KB + 6656)
    na_tok = at("na_tok", [P, NT, P], F32, R + 73 * KB + 6656 + 4 * BIASW)
    rope_u = at("rope_u", [P, NT, HD], F32, R + 73 * KB + 6656 + 4 * BIASW + 4 * KB)
    sq = at("sq", [P, 2, 256], F32, R + 73 * KB + 6656 + 4 * BIASW + 4 * KB)
    na_in = at("na_in", [P, PAIRS - 1, NT, P], F32, H + 40 * KB)
    naT_hi = [at(f"naT_hi{k}", [P, L], F32R, R + (48 + 8 * k) * KB) for k in range(PAIRS)]
    naT_lo = [at(f"naT_lo{k}", [P, L], F32R, R + (52 + 8 * k) * KB) for k in range(PAIRS)]
    g1diag = at("g1diag", [P, KD, P], F32, H + 72 * KB)
    m_in = [at(f"m_in{n}", [P, 2, L], F32, H + kb * KB) for n, kb in enumerate((24, 56, 16, 64, 72))]
    mT_hi = at("mT_hi", [P, KD, L], F32R, H)
    mT_lo = at("mT_lo", [P, KD, L], F32R, H + 32 * KB)
    xn = at("xn", [P, NT, D], F32, R + 32 * KB)
    nx = [at("nx0", [P, 4, D], F32, R + 64 * KB), at("nx1", [P, 4, D], F32, H + 64 * KB)]
    gb = at("gb", [P, D], F32, R + 80 * KB)
    otmp = at("otmp", [P, 2, HALF], F32, R + 84 * KB)
    h2tmp = at("h2tmp", [P, 2, HALF], F32, R + 88 * KB)
    g2diag = at("g2diag", [P, KD, P], F32, R + 88 * KB)
    h2_hi = at("h2_hi", [P, KD, L], F32R, H)
    h2_lo = at("h2_lo", [P, KD, L], F32R, H + 32 * KB)
    aT_hi = at("aT_hi", [P, FCH, L], F32R, H + 64 * KB)
    aT_lo = at("aT_lo", [P, FCH, L], F32R, R + 64 * KB)
    relu = at("relu", [P, 2, HALF], F32, R + 84 * KB)
    ytmp = at("ytmp", [P, 2, HALF], F32, R + 88 * KB)

    ps = ctx.enter_context(nc.psum_tensor("ps", [P, 8, HALF], F32))
    bank = [ps[:, b, :] for b in range(8)]
    psflat = ps[:, :, :].rearrange("p b n -> p (b n)")

    spill_m = nc.dram_tensor("spill_m", (KD, P, 2, L), F32, kind="Internal").ap()
    spill_na = nc.dram_tensor("spill_na", (PAIRS - 1, P, NT, P), F32, kind="Internal").ap()

    def hi(s):
        return (ringA_hi if s < 3 else ringB_hi)[:, s % 3, :]

    def lo(s):
        return (ringA_lo if s < 3 else ringB_lo)[:, s % 3, :]

    def raw(r):
        return (rawA if r < 2 else rawB)[:, r % 2, :]

    def sem(name):
        return ctx.enter_context(nc.semaphore(name))

    d_const = sem("d_const")
    d_att = sem("d_att")
    d_x = [sem(f"d_x{k}") for k in range(KD)]
    d_c = sem("d_c")
    d_ada1 = [sem(f"d_ada1_{k}") for k in range(KD)]
    d_raw = [sem(f"d_raw{r}") for r in range(4)]
    p_own = sem("p_own")
    split_hi = sem("split_hi")
    split = sem("split")
    v_own = sem("v_own")
    a_own = sem("a_own")
    sig_done = sem("sig_done")
    silu_done = sem("silu_done")
    sq_done = sem("sq_done")
    row_ps = sem("row_ps")
    row_copied = sem("row_copied")
    xsum_done = sem("xsum_done")
    ssq_ps = sem("ssq_ps")
    ms_ready = sem("ms_ready")
    sqrt_done = sem("sqrt_done")
    diag_ready = sem("diag_ready")
    rb_ps = sem("rb_ps")
    mod1_ps = sem("mod1_ps")
    rctx_ready = sem("rctx_ready")
    xr_ready = sem("xr_ready")
    ctx_xr = sem("ctx_xr")
    ctx_hi_done = sem("ctx_hi_done")
    ctx_done = sem("ctx_done")
    h_hi_done = sem("h_hi_done")
    h_done = sem("h_done")
    pw_done = sem("pw_done")
    u_ps = sem("u_ps")
    pads_done = sem("pads_done")
    u_copied = sem("u_copied")
    d_made = sem("d_made")
    d_hi_done = sem("d_hi_done")
    d_done = sem("d_done")
    y_ps = sem("y_ps")
    y_hi_done = sem("y_hi_done")
    y_done = sem("y_done")
    m1_ps = sem("m1_ps")
    sg_done = sem("sg_done")
    mp_done = sem("mp_done")
    spill_g = [sem(f"spill_g{n}") for n in range(2)]
    spill_p = [sem(f"spill_p{n}") for n in range(2)]
    d_ada2 = [sem(f"d_ada2_{n}") for n in range(2)]
    ada2_used = sem("ada2_used")
    acc_ready = sem("acc_ready")
    mod2_ps = sem("mod2_ps")
    mod2_done = sem("mod2_done")
    z_ps = sem("z_ps")
    z_set = sem("z_set")
    z_copied = sem("z_copied")
    v_taken = sem("v_taken")
    zsq_done = sem("zsq_done")
    zsum_done = sem("zsum_done")
    gain_set = sem("gain_set")
    zg_done = sem("zg_done")
    qk_ms = sem("qk_ms")
    qk_sqrt = sem("qk_sqrt")
    nrm_done = sem("nrm_done")
    rotq_done = sem("rotq_done")
    rotk_done = sem("rotk_done")
    t_ps = sem("t_ps")
    t_hi_done = sem("t_hi_done")
    t_done = sem("t_done")
    s_ps = sem("s_ps")
    sm_ready = sem("sm_ready")
    exp_done = sem("exp_done")
    pt_ps = sem("pt_ps")
    ptA_copied = sem("ptA_copied")
    ptB_copied = sem("ptB_copied")
    pv_ps = sem("pv_ps")
    na_done = sem("na_done")
    nat_ps = sem("nat_ps")
    nat_hi_done = sem("nat_hi_done")
    nat_split = sem("nat_split")
    na_room = sem("na_room")
    d_bias = sem("d_bias")
    d_na = sem("d_na")
    d_m = [sem(f"d_m{n}") for n in range(5)]
    m2_ps = sem("m2_ps")
    m_sum = sem("m_sum")
    m_hi_done = sem("m_hi_done")
    m_done = sem("m_done")
    d_xn = [sem(f"d_xn{n}") for n in range(2)]
    g_diag = sem("g_diag")
    g_ps = sem("g_ps")
    g_ready = sem("g_ready")
    o_ps = sem("o_ps")
    o_part = sem("o_part")
    xn_done = sem("xn_done")
    xss_done = sem("xss_done")
    xms = sem("xms")
    xsqrt = sem("xsqrt")
    nx_done = sem("nx_done")
    h2_ps = sem("h2_ps")
    h2_full = sem("h2_full")
    h2_hi_done = sem("h2_hi_done")
    h2_done = sem("h2_done")
    f1_ps = sem("f1_ps")
    relu_done = sem("relu_done")
    a_done = sem("a_done")
    f2_ps = sem("f2_ps")
    x_done = sem("x_done")
    d_out = sem("d_out")

    G_RAW = (0, 1, 2, 3)
    M1_RAW = (0, 1, 2, 0, 1, 2)
    M1_SLOT = (1, 2, 0, 4, 5, 3)
    A_RAW = (0, 1, 0)
    N_RAW = (0, 1, 0, 1)
    O_RAW = (0, 1, 2, 3, 0, 1, 2, 3)
    O_SLOT = (4, 5, 0, 1, 2, 3, 4, 5)
    F_RAW = (0, 1, 2, 3, 0, 1, 2, 3)
    Y_BANK = (0, 1, 2, 3, 6, 7, 6, 7)
    M_SLOT = (0, 1, 2, 3, 4, 0, 3, 4)
    raws_before = {}
    seen = [0] * 4
    for name, table, turns in (("pool", G_RAW, 1), ("gate", M1_RAW, 4), ("att", A_RAW, PAIRS),
                               ("na", N_RAW, 1), ("out", O_RAW, 1), ("mlp", F_RAW, NFG)):
        raws_before[name] = (table, list(seen))
        for r in table:
            seen[r] += turns

    def landed(phase, turn, r):
        table, before = raws_before[phase]
        s = table[r]
        return s, 16 * (before[s] + turn * table.count(s) + table[:r + 1].count(s))

    block = ctx.enter_context(nc.Block())

    @block.sync
    def _(sp):
        sp.dma_start(c_col[:], a["c_col"]).then_inc(d_c, 16)
        for k in range(KD):
            sp.dma_start(ada1[:, k, :], a["ada1"][k]).then_inc(d_ada1[k], 16)
        consts = [(ident, "ident"), (ones, "ones"), (norm_g, "norm_g"),
                  (ada_b, "ada_b"), (pscale, "pscale"), (edge_inv, "edge_inv"), (pw_raw, "pool_w")]
        for t, name in consts:
            sp.dma_start(t[:], a[name]).then_inc(d_const, 16)
        for k in range(KD):
            sp.dma_start(xT[:, k, :], a["xT"][k]).then_inc(d_x[k], 16)

        def load(phase, turn, r, unit, cols=1024):
            s, _ = landed(phase, turn, r)
            sp.dma_start(raw(s)[:, 0:cols], a["units"][unit, :, 0:cols]).then_inc(d_raw[s], 16)

        for g in range(NG):
            load("pool", 0, g, U_POOL + g)
        with sp.Fori(0, 4) as j:
            for r in range(6):
                unit = U_GATE + j * 6 + r
                sp.wait_ge(split, unit - 2)
                load("gate", j, r, unit, 1024 if r % 3 < 2 else 512)
        with sp.Fori(0, PAIRS) as p:
            for r, back in ((0, 0), (1, 2), (2, 1)):
                unit = U_ATT + p * 3 + r
                sp.wait_ge(split, unit - back)
                load("att", p, r, unit)
        for r in range(4):
            sp.wait_ge(split, (U_NA, U_NA - 1, U_NA + 1, U_NA + 2)[r])
            load("na", 0, r, U_NA + r)
        for r in range(8):
            if r == 2:
                sp.wait_ge(pv_ps, 8 * HEADS)
            sp.wait_ge(split, U_OUT + (-1, 0, 0, 0, 1, 2, 3, 4)[r])
            load("out", 0, r, U_OUT + r)
        with sp.Fori(0, NFG) as g:
            for r in range(8):
                unit = U_MLP + g * 8 + r
                sp.wait_ge(split, unit - 3)
                load("mlp", g, r, unit)
        for dh in range(2):
            for t in range(NT):
                sp.wait_ge(x_done, 16 * (NFG - 1) + 8 * dh + t + 1)
                sp.dma_start(out[t * P:(t + 1) * P, dh * HALF:(dh + 1) * HALF],
                             xn[:, t, dh * HALF:(dh + 1) * HALF]).then_inc(d_out, 16)
        sp.wait_ge(d_out, 16 * 16)

    @block.gpsimd
    def _(pool):
        def split_unit(phase, turn, r, slot, unit, cols=1024):
            s, count = landed(phase, turn, r)
            pool.wait_ge(d_raw[s], count)
            h, l, w = hi(slot)[:, 0:cols], lo(slot)[:, 0:cols], raw(s)[:, 0:cols]
            nc.gpsimd.tensor_tensor(h, w, ones[:, 0:1].to_broadcast([P, cols]), ALU.mult).then_inc(split_hi, 1)
            pool.wait_ge(split_hi, unit + 1)
            nc.gpsimd.tensor_tensor(l, w, h.bitcast(F32), ALU.subtract).then_inc(split, 1)

        own = Steps(pool, p_own)
        pool.wait_ge(d_const, 7 * 16)
        for g in range(NG):
            split_unit("pool", 0, g, g, U_POOL + g)
        def gate_turn(j):
            for r in range(6):
                d = j * 2 + r // 3
                if isinstance(j, int) and j == 0:
                    if M1_SLOT[r] < NG:
                        pool.wait_ge(u_ps, 2 * M1_SLOT[r] + 2)
                else:
                    pool.wait_ge(m1_ps, (d - 2) * 6 + 4 + r % 3)
                split_unit("gate", j, r, M1_SLOT[r], U_GATE + j * 6 + r, 1024 if r % 3 < 2 else 512)
        gate_turn(0)
        with pool.Fori(1, 4) as j:
            gate_turn(j)
        for r in range(3):
            pool.wait_ge(m1_ps, 6 * (KD - 1))
            split_unit("att", 0, r, r, U_ATT + r)

        def gains(p):
            for t in range(NTA):
                pool.wait_ge(zsq_done, p * NTA + t + 1)
                x = slice(0 if t < NT else P, 256)
                nc.gpsimd.tensor_tensor(z[:, t, x], z[:, t, x], qk_g[:, x], ALU.mult).then_inc(zg_done, 1)

        def rotate_k(p):
            TT = nc.gpsimd.tensor_tensor
            pool.wait_ge(nrm_done, 2 * p + 2)
            for hh in range(2):
                x = slice(P + hh * HD, P + (hh + 1) * HD)
                prod = rot_k[:, :, hh, 1, :]
                own.done(TT(prod, nrm[:, 0:NT, x], rope_c[:, :, :], ALU.mult))
                xh = nrm[:, 0:NT, x].rearrange("p t (c h n) -> p t c h n", h=2, n=HD // 4)
                sh = rope_s[:, :, :].rearrange("p t (c h n) -> p t c h n", h=2, n=HD // 4)
                th = rope_t[:, :, :].rearrange("p t (c h n) -> p t c h n", h=2, n=HD // 4)
                for h in range(2):
                    own.done(TT(th[:, :, :, h, :], xh[:, :, :, 1 - h, :], sh[:, :, :, h, :], ALU.mult))
                own.wait()
                both = [P, NT, 2, HD]
                own.link(TT(rot_k[:, :, hh, :, :], prod.unsqueeze(2).to_broadcast(both),
                            rope_t[:, :, :].unsqueeze(2).to_broadcast(both), ALU.add))
                both = [P, 2, 2, HD]
                TT(kc2[:, :, hh, :, :], nrm[:, NT:NTA, x].unsqueeze(2).to_broadcast(both),
                   ones[:, 0:HD].unsqueeze(1).unsqueeze(1).to_broadcast(both), ALU.mult).then_inc(rotk_done, 1)

        pool.wait_ge(gain_set, 1)
        pool.wait_ge(mp_done, 2 * KD)
        for n in range(2):
            pool.wait_ge(spill_g[n], 16 * KD)
            pool.wait_ge(spill_p[n], 16 * KD)
        with pool.Fori(0, PAIRS - 1) as p:
            own.enter(p, 0, 8)
            gains(p)
            pool.wait_ge(z_ps, p * NTA + NTA)
            split_unit("att", p + 1, 0, 0, U_ATT + p * 3 + 3)
            rotate_k(p)
            for r in range(1, 3):
                split_unit("att", p + 1, r, r, U_ATT + p * 3 + 3 + r)
        own.leave(PAIRS - 1)
        gains(PAIRS - 1)
        rotate_k(PAIRS - 1)
        pool.wait_ge(z_ps, PAIRS * NTA)
        for r in range(4):
            if r == 3:
                pool.wait_ge(pv_ps, 8 * HEADS)
            split_unit("na", 0, r, r, U_NA + r)
        for r in range(8):
            if 2 <= r < 6:
                pool.wait_ge(m2_ps, 4 * (r - 1))
            if r >= 6:
                pool.wait_ge(o_part, r - 5)
            split_unit("out", 0, r, O_SLOT[r], U_OUT + r)
        def mlp_turn(g):
            first = isinstance(g, int)
            for r, (kind, c, slot) in enumerate(MLP_ORDER):
                if kind == "w1" and c >= 2:
                    pool.wait_ge(f1_ps, g * 8 + ((3, 4)[c - 2] if first else 2 * (c - 2) + 2))
                elif kind == "w1":
                    if first:
                        pool.wait_ge(o_ps, 8)
                    else:
                        pool.wait_ge(f1_ps, (g - 1) * 8 + 2 * (c + 2) + 2)
                elif first:
                    pool.wait_ge(o_ps, 16)
                else:
                    pool.wait_ge(f2_ps, g * 16)
                split_unit("mlp", g, r, slot, U_MLP + g * 8 + r)
        mlp_turn(0)
        with pool.Fori(1, NFG) as g:
            mlp_turn(g)

    @block.tensor
    def _(pe):
        mm = nc.tensor.matmul

        def three(o, wh, wl, xh, xl, first, last):
            mm(o, wh, xh, start=first, stop=False)
            mm(o, wh, xl, start=False, stop=False)
            return mm(o, wl, xh, start=False, stop=last)

        pe.wait_ge(silu_done, 1)
        for k in range(KD):
            pe.wait_ge(d_ada1[k], 16)
            for j in range(4):
                last = mm(bank[4 + j][0:2, :], c_silu[:, k, :], ada1[:, k, j * HALF:(j + 1) * HALF],
                          start=(k == 0), stop=(k == KD - 1))
        last.then_inc(row_ps, 1)
        pe.wait_ge(d_const, 7 * 16)
        pe.wait_ge(row_copied, 4)
        for j in range(16):
            last = mm(bank[0][:, 2 * j:2 * j + 2], mod_row[:, j * P:(j + 1) * P], ident[0:2, 0:2],
                      start=True, stop=True)
        last.then_inc(mod1_ps, 1)
        pe.wait_ge(xsum_done, KD - 1)
        for t in range(NTA):
            last = mm(bank[3][:, t:t + 1], xsum[:, t * P:(t + 1) * P], ones[:, 0:1], start=True, stop=True)
        last.then_inc(ssq_ps, 1)
        for t in range(NTA):
            pe.wait_ge(diag_ready, t + 1)
            last = mm(psflat[:, HALF + t * P:HALF + (t + 1) * P], ones[:, :], diag[:, t, :],
                      start=True, stop=True)
        last.then_inc(rb_ps, 1)

        def pool_part(q, k):
            g, x = q // 2, slice((q % 2) * HALF, (q % 2 + 1) * HALF)
            last = three(bank[4 + q % 4], hi(g)[:, k * P:(k + 1) * P], lo(g)[:, k * P:(k + 1) * P],
                         hT_hi[:, k, x], hT_lo[:, k, x], k == 0, k == KD - 1)
            if k == KD - 1:
                last.then_inc(u_ps, 1)

        def pool_u(g):
            pe.wait_ge(split, U_POOL + g + 1)
            for half in range(2):
                pe.wait_ge(u_copied, 2 * g + half - 3)
                for k in range(KD):
                    pool_part(2 * g + half, k)

        def pool_y(g):
            if g == 0:
                pe.wait_ge(pw_done, 1)
            pe.wait_ge(d_done, g + 1)
            for half in range(2):
                q = 2 * g + half
                if g == 3:
                    pe.wait_ge(y_done, q - 1)
                elif g == 2:
                    pe.wait_ge(u_copied, 8)
                x = slice(half * HALF, (half + 1) * HALF)
                c = POOL_ORDER[g]
                three(bank[Y_BANK[q]], pw_hi[:, c, :], pw_lo[:, c, :], dT_hi[:, x], dT_lo[:, x],
                      True, True).then_inc(y_ps, 1)

        pe.wait_ge(split, U_POOL + 2)
        for k in range(KD):
            pe.wait_ge(h_done, k + 1)
            for q in range(4):
                pool_part(q, k)
        pool_u(2)
        pool_y(0)
        pool_u(3)
        pool_y(1)

        def gate_turn(j):
            for e in range(2):
                d = j * 2 + e
                sg, sn, sb = M1_SLOT[3 * e:3 * e + 3]
                for half in range(2):
                    x = slice(half * HALF, (half + 1) * HALF)
                    for n, slot in enumerate((sg, sn)):
                        if half == 0:
                            pe.wait_ge(split, U_GATE + d * 3 + n + 1)
                        if isinstance(j, int) and j == 0 and e == 0:
                            if half == 0 and n == 0:
                                pe.wait_ge(y_done, 2)
                        else:
                            pe.wait_ge(sg_done, d * 4 + half * 2 + n - 3)
                        for k in range(KD):
                            w = slice(k * P, (k + 1) * P)
                            last = three(bank[3 * half + n], hi(slot)[:, w], lo(slot)[:, w],
                                         hT_hi[:, k, x], hT_lo[:, k, x], k == 0, k == KD - 1)
                        last.then_inc(m1_ps, 1)
                        if not isinstance(j, int) and e == half == n == 0:
                            modulation(j - 1)
                    if half == 0:
                        pe.wait_ge(split, U_GATE + d * 3 + 3)
                    if isinstance(j, int) and j == 0 and e == half == 0:
                        pool_y(2)
                        pool_y(3)
                        pe.wait_ge(y_done, 8)
                    if not (isinstance(j, int) and j == 0 and e == 0):
                        pe.wait_ge(mp_done, d * 2 + half - 1)
                    for k in range(NG):
                        w = slice(k * P, (k + 1) * P)
                        last = three(bank[3 * half + 2], hi(sb)[:, w], lo(sb)[:, w],
                                     poolT_hi[:, k, x], poolT_lo[:, k, x], k == 0, k == NG - 1)
                    last.then_inc(m1_ps, 1)

        def modulation(j):
            pe.wait_ge(acc_ready, j + 1)
            for k in range(KD):
                last = mm(bank[6][:, k:k + 1], acc[:, k * P:(k + 1) * P], ones[:, 0:1],
                          start=True, stop=True)
            last.then_inc(mod2_ps, 1)

        gate_turn(0)
        with pe.Fori(1, 4) as j:
            gate_turn(j)

        def qkv(p, t):
            first = isinstance(p, int)
            if t == 0:
                pe.wait_ge(split, U_ATT + p * 3 + 3)
            if not first:
                pe.wait_ge(z_copied, p * NTA + t)
            elif t >= 2:
                pe.wait_ge(z_copied, t - 1)
            elif t == 1:
                pe.wait_ge(mp_done, 2 * KD)
            zb = bank[5 if first and t % 2 else 7]
            c = 0 if t < NT else 1
            for k in range(KD):
                w = slice(k * P, (k + 1) * P)
                x = slice(t * P, (t + 1) * P)
                last = three(zb[:, c * P:384].rearrange("p (u n) -> p u n", n=P),
                             hT_hi[:, k, x], hT_lo[:, k, x],
                             ringA_hi[:, c:3, w], ringA_lo[:, c:3, w], k == 0, k == KD - 1)
            last.then_inc(z_ps, 1)

        def free_banks(s):
            pe.wait_ge(exp_done, s)
            pe.wait_ge(ptA_copied, s)
            pe.wait_ge(ptB_copied, s)
            pe.wait_ge(na_done, s)

        def turn_heads(p, hh):
            s0 = p * 16 + hh * 8
            if hh:
                free_banks(s0)
            pe.wait_ge(rotq_done, p * 2 + hh + 1)
            pe.wait_ge(rotk_done, p * 2 + hh + 1)
            sources = (lambda i: rot_k[:, i, hh, :, :].rearrange("p c n -> p (c n)"),
                       lambda i: rot_q[:, i, hh, :], lambda i: nrm[:, i, hh * HD:(hh + 1) * HD])
            for n, src in enumerate(sources):
                m = HD if n else P
                for half in range(2):
                    for e in range(4):
                        last = nc.tensor.transpose(bank[2 * n + half][0:m, e * P:(e + 1) * P],
                                                   src(4 * half + e), ident[:, :])
                    last.then_inc(t_ps, 1)
            for e in range(2):
                last = nc.tensor.transpose(bank[6][:, e * P:(e + 1) * P],
                                           kc2[:, e, hh, :, :].rearrange("p c n -> p (c n)"), ident[:, :])
            last.then_inc(t_ps, 1)

        def scores(p, hh, i):
            s = p * 16 + hh * 8 + i
            if i == 0:
                pe.wait_ge(t_done, p * 14 + hh * 7 + 7)
            elif i > 1:
                pe.wait_ge(exp_done, s - 1)
            b0 = 2 * (i % 2)
            q = slice(i * P, (i + 1) * P)
            k0 = key_tile(i) * P
            c0 = HD if inner(i) else 0
            mm(bank[b0], qrT[:, q], krT_hi[:, k0:k0 + HALF], start=True, stop=False)
            mm(bank[b0], qrT[:, q], krT_lo[:, k0:k0 + HALF], start=False, stop=True)
            if inner(i):
                k1 = slice(k0 + HALF, k0 + HALF + HD)
                mm(bank[b0 + 1][:, 0:HD], qrT[:, q], krT_hi[:, k1], start=True, stop=False)
                mm(bank[b0 + 1][:, 0:HD], qrT[:, q], krT_lo[:, k1], start=False, stop=True)
            o = bank[b0 + 1][:, c0:c0 + CTX]
            mm(o, qpT[:, q], kcT_hi[:, :], start=True, stop=False)
            mm(o, qpT[:, q], kcT_lo[:, :], start=False, stop=True).then_inc(s_ps, 1)

        def turn_probs(p, hh, i):
            s = p * 16 + hh * 8 + i
            pe.wait_ge(exp_done, s + 1)
            if i:
                pe.wait_ge(ptA_copied, s)
                pe.wait_ge(ptB_copied, s)
            pr = prob[:, i % 2, :]
            for e in range(4):
                last = nc.tensor.transpose(bank[4][:, e * P:(e + 1) * P], pr[:, e * P:(e + 1) * P], ident[:, :])
            c0 = HALF + (HD if inner(i) else 0)
            if inner(i):
                nc.tensor.transpose(bank[5][0:HD, CTX:CTX + P], pr[:, HALF:HALF + HD], ident[:, :])
            for e in range(2):
                last = nc.tensor.transpose(bank[5][:, e * P:(e + 1) * P], pr[:, c0 + e * P:c0 + (e + 1) * P],
                                           ident[:, :])
            last.then_inc(pt_ps, 1)

        def values(p, hh, i):
            s = p * 16 + hh * 8 + i
            pe.wait_ge(ptA_copied, s + 1)
            pe.wait_ge(ptB_copied, s + 1)
            if i:
                pe.wait_ge(na_done, s)
            v = slice(hh * HD, (hh + 1) * HD)
            o = bank[6][:, 0:HD]
            kt = key_tile(i)
            for e in range(4):
                mm(o, probT[:, e, :], vcur[:, kt + e, v], start=(e == 0), stop=False)
            if inner(i):
                mm(o, probT[0:HD, 6, :], vcur[0:HD, kt + 4, v], start=False, stop=False)
            for e in range(2):
                last = mm(o, probT[:, 4 + e, :], vcur[:, NT + e, v], start=False, stop=(e == 1))
            last.then_inc(pv_ps, 1)

        def attend(p, ahead):
            for hh in range(2):
                if ahead and hh == 0:
                    qkv(p + 1, 0)
                turn_heads(p, hh)
                if ahead:
                    qkv(p + 1, 9 if hh else 1)
                if hh == 0:
                    pe.wait_ge(v_taken, p + 1)
                scores(p, hh, 0)
                for i in range(8):
                    if i < 7:
                        scores(p, hh, i + 1)
                    if ahead and hh == 0 and i < 7:
                        qkv(p + 1, i + 2)
                    if not ahead and hh and i < 6:
                        turn_result(i // 2, i % 2)
                    turn_probs(p, hh, i)
                    if i:
                        values(p, hh, i - 1)
                values(p, hh, 7)
            free_banks(p * 16 + 16)

        def turn_result(k, half):
            n = 2 * k + half
            if n == 0:
                pe.wait_ge(z_copied, PAIRS * NTA)
                pe.wait_ge(d_na, 16 * (PAIRS - 1))
            elif k < PAIRS - 1:
                pe.wait_ge(nat_split, n)
            for e in range(4):
                t = 4 * half + e
                src, b = (na_in[:, k, t, :], 7) if k < PAIRS - 1 else (na_tok[:, t, :], 4 + half)
                last = nc.tensor.transpose(bank[b][:, e * P:(e + 1) * P], src, ident[:, :])
            last.then_inc(nat_ps, 1)

        qkv(0, 0)
        modulation(3)
        for t in range(1, NTA):
            qkv(0, t)
        pe.wait_ge(sg_done, 4 * KD)
        pe.wait_ge(z_copied, NTA)
        pe.wait_ge(mod2_done, 4)
        with pe.Fori(0, PAIRS - 1) as p:
            attend(p, True)
        attend(PAIRS - 1, False)

        for half in range(2):
            turn_result(PAIRS - 1, half)
        pe.wait_ge(g_diag, 8)
        pe.wait_ge(nat_split, 6)
        for k in range(KD):
            last = mm(psflat[:, (6 * HALF) + k * P:(6 * HALF) + (k + 1) * P], ones[:, :], g1diag[:, k, :],
                      start=True, stop=True)
        last.then_inc(g_ps, 1)
        for q in range(4):
            pe.wait_ge(split, U_NA + q + 1)
            for e in range(2):
                for half in range(2):
                    n = 4 * q + 2 * e + half
                    if n >= 6:
                        pe.wait_ge(m_done, n - 5)
                    x = slice(half * HALF, (half + 1) * HALF)
                    for k in range(PAIRS):
                        if n < 2 and k == PAIRS - 1:
                            pe.wait_ge(nat_split, 7 + n)
                        w = slice((4 * e + k) * P, (4 * e + k + 1) * P)
                        last = three(bank[n % 6], hi(q)[:, w], lo(q)[:, w], naT_hi[k][:, x], naT_lo[k][:, x],
                                     k == 0, k == PAIRS - 1)
                    last.then_inc(m2_ps, 1)
        def project(dh, t):
            n = 8 * dh + t
            if n >= 4:
                pe.wait_ge(xn_done, n - 3)
            else:
                pe.wait_ge(m_done, 13 + n)
            if n == 4:
                pe.wait_ge(m_done, 16)
            x = slice(t * P, (t + 1) * P)
            for k in range(KD):
                if n == 0 and k == KD - 1:
                    pe.wait_ge(m_done, 2 * k + 1)
                if t == 0 and k % 2 == 0:
                    pe.wait_ge(split, U_OUT + 4 * dh + k // 2 + 1)
                slot = O_SLOT[4 * dh + k // 2]
                w = slice((k % 2) * HALF, (k % 2 + 1) * HALF)
                last = three(bank[n % 4], mT_hi[:, k, x], mT_lo[:, k, x], hi(slot)[:, w], lo(slot)[:, w],
                             k == 0, k == KD - 1)
                if n == 7 and k in (1, 3):
                    last.then_inc(o_part, 1)
            last.then_inc(o_ps, 1)

        def turn_norm(half, k0):
            for k in range(k0, k0 + 4):
                n = 8 * half + k
                if n >= 4:
                    pe.wait_ge(h2_full, n - 3)
                else:
                    pe.wait_ge(g_ready, 2)
                for e in range(4):
                    if k == 0:
                        pe.wait_ge(nx_done, 4 * half + e + 1)
                    last = nc.tensor.transpose(bank[4 + n % 4][:, e * P:(e + 1) * P],
                                               nx[half][:, e, k * P:(k + 1) * P], ident[:, :])
                last.then_inc(h2_ps, 1)

        for n in range(16):
            project(n // 8, n % 8)
            if n >= 13:
                turn_norm(0, 4 * (n - 13)) if n < 15 else None

        def hidden(g, n, pos):
            first = isinstance(g, int)
            f, half = n // 2, n % 2
            slot = f % 2
            unit = U_MLP + g * 8 + (0, 1, 3, 5)[f]
            if half == 0:
                pe.wait_ge(split, unit + 1)
            if n >= 4 or not first:
                pe.wait_ge(a_done, g * 8 + (FIRST_ORDER.index(n - 4) + 1 if first else n - 3))
            elif pos == 0:
                pe.wait_ge(xn_done, 16)
            x = slice(half * HALF, (half + 1) * HALF)
            for k in range(KD):
                if first and f == 0:
                    pe.wait_ge(h2_done, 8 * half + k + 1)
                w = slice(k * P, (k + 1) * P)
                last = three(bank[n % 4], hi(slot)[:, w], lo(slot)[:, w], h2_hi[:, k, x], h2_lo[:, k, x],
                             k == 0, k == KD - 1)
            last.then_inc(f1_ps, 1)

        def mlp_turn(g):
            first = isinstance(g, int)
            for pos in range(8):
                hidden(g, FIRST_ORDER[pos] if first else pos, pos)
                if first and pos < 2:
                    turn_norm(1, 4 * pos)
                if first and pos == 3:
                    pe.wait_ge(g_diag, 16)
                    pe.wait_ge(h2_full, 16)
                    for k in range(KD):
                        last = mm(psflat[:, 4 * HALF + k * P:4 * HALF + (k + 1) * P], ones[:, :], g2diag[:, k, :],
                                  start=True, stop=True)
                    last.then_inc(g_ps, 1)
            for dh in range(2):
                for t in range(NT):
                    n = 8 * dh + t
                    if n >= 4 or not first:
                        pe.wait_ge(x_done, g * 16 + n - 3)
                    x = slice(t * P, (t + 1) * P)
                    w = slice(dh * HALF, (dh + 1) * HALF)
                    for f in range(FCH):
                        if n == 0 and first and f == 0:
                            pe.wait_ge(g_ready, 4)
                        if n == 0:
                            pe.wait_ge(a_done, g * 8 + (FIRST_ORDER.index(2 * f) if first else 2 * f) + 1)
                            pe.wait_ge(split, U_MLP + g * 8 + (2, 4, 6, 7)[f] + 1)
                        if n == 4:
                            pe.wait_ge(a_done, g * 8 + (FIRST_ORDER.index(2 * f + 1) if first else 2 * f + 1) + 1)
                        last = three(bank[4 + n % 4], aT_hi[:, f, x], aT_lo[:, f, x],
                                     hi(2 + f)[:, w], lo(2 + f)[:, w], f == 0, f == FCH - 1)
                    last.then_inc(f2_ps, 1)

        mlp_turn(0)
        with pe.Fori(1, NFG) as g:
            mlp_turn(g)

    @block.scalar
    def _(act):
        fn = nc.scalar.activation
        act.wait_ge(d_c, 16)
        fn(c_sig[:], c_col[:], ACT.Sigmoid).then_inc(sig_done, 1)
        for k in range(KD):
            if k == 5:
                act.wait_ge(row_ps, 1)
                for j in range(4):
                    fn(mod_row[:, j * HALF:(j + 1) * HALF], bank[4 + j][0:2, :], ACT.Copy)\
                        .then_inc(row_copied, 1)
            act.wait_ge(d_x[k], 16)
            if k >= 3:
                act.wait_ge(xsum_done, k - 2)
            fn(xsq[:, k % 2, :] if k else xsum[:, :], xT[:, k, :], ACT.Square).then_inc(sq_done, 1)
        act.wait_ge(ms_ready, 1)
        fn(rt[:, 0:NTA], ms[:, 0:NTA], ACT.Sqrt).then_inc(sqrt_done, 1)
        act.wait_ge(rb_ps, 1)
        fn(rctx, bank[3][:, 0:CTX], ACT.Copy).then_inc(rctx_ready, 1)
        for k in range(KD):
            act.wait_ge(xr_ready, k + 1)
            if k >= 2:
                act.wait_ge(h_done, k - 1)
            fn(hfull[:, k % 2, :], xT[:, k, 0:L], ACT.Identity,
               bias=mod1[:, k, 0:1], scale=gain1[:, k, 0:1]).then_inc(a_own, 1)
            act.wait_ge(a_own, k + 1)
            fn(hT_hi[:, k, 0:L], hfull[:, k % 2, :], ACT.Copy).then_inc(h_hi_done, 1)
        act.wait_ge(ctx_xr, 1)
        for k in range(KD):
            fn(xT[:, k, L:T], xT[:, k, L:T], ACT.Identity,
               bias=mod1[:, k, 1:2], scale=gain1[:, k, 1:2]).then_inc(a_own, 1)
        act.wait_ge(a_own, 2 * KD)
        fn(hT_hi[:, :, L:T], xT[:, :, L:T], ACT.Copy).then_inc(ctx_hi_done, 1)
        act.wait_ge(pads_done, 2)

        def u_out(g):
            for half in range(2):
                q = 2 * g + half
                act.wait_ge(u_ps, q + 1)
                if g:
                    act.wait_ge(d_made, g)
                fn(up[:, PAD + half * HALF:PAD + (half + 1) * HALF], bank[4 + q % 4], ACT.Copy)\
                    .then_inc(u_copied, 1)

        def d_out_hi(g):
            act.wait_ge(d_made, g + 1)
            if g:
                act.wait_ge(y_ps, 2 * g)
            fn(dT_hi[:, :], win[0][:, PAD:PAD + L], ACT.Copy).then_inc(d_hi_done, 1)

        def y_out(g):
            c = POOL_ORDER[g]
            for half in range(2):
                q = 2 * g + half
                act.wait_ge(y_ps, q + 1)
                fn(poolT_hi[:, c, half * HALF:(half + 1) * HALF], bank[Y_BANK[q]], ACT.Copy,
                   scale=pscale[:, c:c + 1]).then_inc(y_hi_done, 1)

        for g in range(NG):
            u_out(g)
            d_out_hi(g)
            if g:
                y_out(g - 1)
        y_out(NG - 1)

        def gate_turn(j):
            first = isinstance(j, int)
            for e in range(2):
                for half in range(2):
                    d = j * 2 + e
                    for n in range(2):
                        u = 4 * e + 2 * half + n
                        if not first or u >= 2:
                            act.wait_ge(ada2_used, j * 8 + u - 1)
                        act.dma_start(ada2[:, n, :], a["ada2"][j * 8 + u]).then_inc(d_ada2[n], 16)
                    act.wait_ge(m1_ps, d * 6 + half * 3 + 1)
                    if not first or e:
                        act.wait_ge(mp_done, d * 2 + half - 1)
                        act.wait_ge(spill_g[half], d * 16)
                    fn(sgp[:, half, :], bank[3 * half], ACT.Sigmoid).then_inc(sg_done, 1)
                    act.wait_ge(m1_ps, d * 6 + half * 3 + 2)
                    fn(sgn[:, half, :], bank[3 * half + 1], ACT.Sigmoid).then_inc(sg_done, 1)
                    act.wait_ge(sg_done, d * 4 + half * 2 + 2)
                    act.dma_start(spill_m[d, :, 0, half * HALF:(half + 1) * HALF], sgn[:, half, :])\
                        .then_inc(spill_g[half], 16)
                    if not (first and e == 0 and half == 0):
                        act.wait_ge(mp_done, d * 2 + half)
                        act.dma_start(spill_m[d if half else d - 1, :, 1, (1 - half) * HALF:(2 - half) * HALF],
                                      mpool[:, 1 - half, :]).then_inc(spill_p[1 - half], 16)

        act.wait_ge(y_ps, 8)
        act.wait_ge(y_done, 8)
        gate_turn(0)
        with act.Fori(1, 4) as j:
            gate_turn(j)
        act.wait_ge(mp_done, 16)
        act.dma_start(spill_m[KD - 1, :, 1, HALF:L], mpool[:, 1, :]).then_inc(spill_p[1], 16)

        act.wait_ge(m1_ps, 6 * KD)
        act.wait_ge(split, U_ATT)
        act.dma_start(qk_g[:], a["qk_g"]).then_inc(d_att, 16)
        act.dma_start(rope_c[:], a["rope_c"]).then_inc(d_att, 16)
        act.dma_start(rope_s[:], a["rope_s"]).then_inc(d_att, 16)

        def z_out(p, t):
            first = isinstance(p, int)
            if t == 0 and not first:
                act.wait_ge(nrm_done, 2 * p)
                act.wait_ge(v_taken, p)
            act.wait_ge(z_ps, p * NTA + t + 1)
            if first and t == NT:
                act.wait_ge(z_set, 1)
            c = 0 if t < NT else P
            fn(z[:, t, c:384], bank[5 if first and t % 2 else 7][:, c:384], ACT.Copy).then_inc(z_copied, 1)
            act.wait_ge(z_copied, p * NTA + t + 1)
            if t >= 2:
                act.wait_ge(zsum_done, p * NTA + t - 1)
            elif not first:
                act.wait_ge(rotq_done, 2 * p)
            fn(sq[:, t % 2, :], z[:, t, 0:256], ACT.Square).then_inc(zsq_done, 1)

        def qk_root(p):
            act.wait_ge(qk_ms, p + 1)
            fn(rt[:, :], ms[:, :], ACT.Sqrt).then_inc(qk_sqrt, 1)

        def attend(p, ahead):
            if not ahead:
                act.wait_ge(z_ps, PAIRS * NTA)
                act.wait_ge(na_room, 16 * PAIRS)
                for k in range(PAIRS - 1):
                    act.dma_start(na_in[:, k, :, :], spill_na[k]).then_inc(d_na, 16)
                for d in range(4):
                    act.dma_start(m_in[M_SLOT[d]][:, :, :], spill_m[d]).then_inc(d_m[M_SLOT[d]], 16)
            for hh in range(2):
                if ahead and hh == 0:
                    z_out(p + 1, 0)
                dst = (krT_hi[:, 0:HALF], krT_hi[:, HALF:L], qrT[:, 0:HALF], qrT[:, HALF:L],
                       qpT[:, 0:HALF], qpT[:, HALF:L], kcT_hi[:, :])
                for n in range(7):
                    act.wait_ge(t_ps, p * 14 + hh * 7 + n + 1)
                    src = bank[n] if n < 6 else bank[6][:, 0:CTX]
                    m = HD if 2 <= n < 6 else P
                    fn(dst[n][0:m], src[0:m], ACT.Copy).then_inc(t_hi_done, 1)
                if ahead:
                    z_out(p + 1, 9 if hh else 1)
                    if hh:
                        qk_root(p + 1)
                elif hh:
                    act.dma_start(xn[:, 0:4, :], x_tiles[:, 0:4, :]).then_inc(d_xn[0], 16)
                exponents(p, hh, 0)
                for i in range(8):
                    s = p * 16 + hh * 8 + i
                    if i < 7:
                        exponents(p, hh, i + 1)
                    if i == 6 and (ahead or hh == 0):
                        act.dma_start(bias[:, :], a["bias"][p * 2 + hh + 1]).then_inc(d_bias, 16)
                    if ahead and hh == 0 and i < 7:
                        z_out(p + 1, i + 2)
                    if not ahead and hh and i < 6:
                        result_hi(i // 2, i % 2)
                    act.wait_ge(pt_ps, s + 1)
                    if i:
                        act.wait_ge(pv_ps, s)
                    fn(probT[:, 0:4, :], bank[4].rearrange("p (e n) -> p e n", n=P), ACT.Copy)\
                        .then_inc(ptA_copied, 1)
            if ahead:
                act.wait_ge(na_done, p * 16 + 16)
                act.dma_start(spill_na[p], na_tok[:, :, :]).then_inc(na_room, 16)

        def exponents(p, hh, i):
            s = p * 16 + hh * 8 + i
            n = i % 2
            w = HALF + CTX + (HD if inner(i) else 0)
            act.wait_ge(sm_ready, s + 1)
            if i >= 2:
                act.wait_ge(pt_ps, s - 1)
            if i >= 4:
                act.wait_ge(na_done, s - 3)
            fn(prob[:, n, 0:w], psflat[:, 2 * n * HALF:2 * n * HALF + w], ACT.Exp,
               bias=nmax[:, n:n + 1], accum_out=den[:, i % 4:i % 4 + 1]).then_inc(exp_done, 1)

        def result_hi(k, half):
            act.wait_ge(nat_ps, 2 * k + half + 1)
            b = 7 if k < PAIRS - 1 else 4 + half
            fn(naT_hi[k][:, half * HALF:(half + 1) * HALF], bank[b], ACT.Copy).then_inc(nat_hi_done, 1)

        x_tiles = a["x"].rearrange("(t p) d -> p t d", p=P)
        z_out(0, 0)
        z_out(0, 1)
        act.wait_ge(mod2_done, 4)
        for n in range(2):
            act.wait_ge(spill_g[n], 16 * KD)
            act.wait_ge(spill_p[n], 16 * KD)
        act.dma_start(bias[:, :], a["bias"][0]).then_inc(d_bias, 16)
        for t in range(2, NTA):
            z_out(0, t)
        qk_root(0)
        with act.Fori(0, PAIRS - 1) as p:
            attend(p, True)
        attend(PAIRS - 1, False)

        for half in range(2):
            result_hi(PAIRS - 1, half)
        act.wait_ge(g_ps, 1)
        for n in range(2):
            fn(gb[:, n * HALF:(n + 1) * HALF], bank[6 + n], ACT.Copy).then_inc(g_ready, 1)
        act.dma_start(m_in[4][:, :, :], spill_m[4]).then_inc(d_m[4], 16)
        for d in range(KD):
            for half in range(2):
                x = slice(half * HALF, (half + 1) * HALF)
                act.wait_ge(m_sum, 2 * d + half + 1)
                fn(mT_hi[:, d, x], m_in[M_SLOT[d]][:, 1, x], ACT.Copy).then_inc(m_hi_done, 1)
            if d in M_SLOT[5:]:
                after = 5 + M_SLOT[5:].index(d)
                act.wait_ge(m_done, 2 * d + 2)
                act.dma_start(m_in[d][:, :, :], spill_m[after]).then_inc(d_m[d], 16)
        act.wait_ge(m2_ps, 16)
        act.dma_start(xn[:, 4:8, :], x_tiles[:, 4:8, :]).then_inc(d_xn[1], 16)
        def row_squares(t):
            act.wait_ge(xn_done, 8 + t + 1)
            fn(nx[t // 4][:, t % 4, :], xn[:, t, :], ACT.Square, accum_out=row_ss[:, t:t + 1])\
                .then_inc(xss_done, 1)
            act.wait_ge(xms, t + 1)
            fn(rt[:, t:t + 1], ms[:, t:t + 1], ACT.Sqrt).then_inc(xsqrt, 1)

        def h2_out(n):
            act.wait_ge(h2_ps, n + 1)
            if n >= 2:
                act.wait_ge(h2_done, n - 1)
            k = n % 8
            fn(h2tmp[:, n % 2, :], bank[4 + n % 4], ACT.Identity, bias=mod2[:, 1, k:k + 1],
               scale=gain2[:, k:k + 1]).then_inc(h2_full, 1)
            act.wait_ge(h2_full, n + 1)
            fn(h2_hi[:, k, (n // 8) * HALF:(n // 8 + 1) * HALF], h2tmp[:, n % 2, :], ACT.Copy)\
                .then_inc(h2_hi_done, 1)

        for t in range(5):
            row_squares(t)
        for n in range(4):
            h2_out(n)
        row_squares(5)
        for n in range(4, 8):
            h2_out(n)
        row_squares(6)
        row_squares(7)
        for n in range(8, 16):
            h2_out(n)

        def mlp_turn(g):
            first = isinstance(g, int)
            for pos in range(8):
                n = FIRST_ORDER[pos] if first else pos
                act.wait_ge(f1_ps, g * 8 + pos + 1)
                if pos >= 2 or not first:
                    act.wait_ge(a_done, g * 8 + pos - 1)
                fn(relu[:, pos % 2, :], bank[n % 4], ACT.Relu).then_inc(a_own, 1)
                act.wait_ge(a_own, 16 + g * 8 + pos + 1)
                fn(relu[:, pos % 2, :], relu[:, pos % 2, :], ACT.Square).then_inc(relu_done, 1)
                if first and pos == 3:
                    act.wait_ge(g_ps, 2)
                    for e in range(2):
                        fn(gb[:, e * HALF:(e + 1) * HALF], bank[4 + e], ACT.Copy).then_inc(g_ready, 1)

        mlp_turn(0)
        with act.Fori(1, NFG) as g:
            mlp_turn(g)

    @block.vector
    def _(dve):
        V = nc.vector
        own = Steps(dve, v_own)

        def rsqrt_begin(src, n, count, ready):
            V.tensor_scalar(ms[:, n], src, 1.0 / count, EPS, ALU.mult, ALU.add).then_inc(ready, 1)

        def rsqrt_end(n):
            own.link(V.reciprocal(rs[:, n], rt[:, n]))
            own.link(V.tensor_tensor(rt[:, n], rs[:, n], rs[:, n], ALU.mult))
            own.link(V.tensor_tensor(rt[:, n], rt[:, n], ms[:, n], ALU.mult))
            own.link(V.tensor_scalar(rt[:, n], rt[:, n], -0.5, 1.5, ALU.mult, ALU.add))
            own.link(V.tensor_tensor(rs[:, n], rs[:, n], rt[:, n], ALU.mult))

        dve.wait_ge(sig_done, 1)
        V.tensor_tensor(c_silu[:], c_col[:], c_sig[:], ALU.mult).then_inc(silu_done, 1)
        dve.wait_ge(d_const, 7 * 16)
        own.link(V.tensor_copy(pw_hi[:], pw_raw[:]))
        for k in range(1, KD):
            dve.wait_ge(sq_done, k + 1)
            if k > 1:
                dve.wait_ge(xsum_done, k - 1)
            V.tensor_tensor(xsum[:, :], xsum[:, :], xsq[:, k % 2, :], ALU.add).then_inc(xsum_done, 1)
        dve.wait_ge(mod1_ps, 1)
        own.link(V.tensor_tensor(mod1[:], bank[0][:, 0:32].rearrange("p (j c) -> p j c", c=2),
                                 ada_b[:, 0:16].unsqueeze(2).to_broadcast([P, 16, 2]), ALU.add))
        own.link(V.scalar_tensor_tensor(out=gain1[:], in0=mod1[:, 8:16, :], scalar=1.0,
                                        in1=norm_g[:, 0, :].unsqueeze(2).to_broadcast([P, KD, 2]),
                                        op0=ALU.add, op1=ALU.mult))
        dve.wait_ge(ssq_ps, 1)
        rsqrt_begin(bank[3][:, 0:NTA], slice(0, NTA), D, ms_ready)
        dve.wait_ge(sqrt_done, 1)
        dve.wait_ge(ms_ready, 1)
        rsqrt_end(slice(0, NTA))
        for t in range(NTA):
            V.tensor_scalar(diag[:, t, :], ident[:, :], rs[:, t:t + 1], None, ALU.mult).then_inc(diag_ready, 1)
        dve.wait_ge(rb_ps, 1)

        def h_lo(k):
            dve.wait_ge(h_hi_done, k + 1)
            V.tensor_tensor(hT_lo[:, k, 0:L], hfull[:, k % 2, :], hT_hi[:, k, 0:L].bitcast(F32), ALU.subtract)\
                .then_inc(h_done, 1)

        for k in range(KD):
            V.tensor_tensor(xT[:, k, 0:L], xT[:, k, 0:L], psflat[:, HALF:HALF + L], ALU.mult)\
                .then_inc(xr_ready, 1)
            if k:
                h_lo(k - 1)
        dve.wait_ge(rctx_ready, 1)
        V.tensor_tensor(xT[:, :, L:T], xT[:, :, L:T], rctx.unsqueeze(1).to_broadcast([P, KD, CTX]), ALU.mult)\
            .then_inc(ctx_xr, 1)
        h_lo(KD - 1)

        dve.wait_ge(ctx_hi_done, 1)
        V.tensor_tensor(hT_lo[:, :, L:T], xT[:, :, L:T], hT_hi[:, :, L:T].bitcast(F32), ALU.subtract)\
            .then_inc(ctx_done, 1)
        dve.wait_ge(ctx_done, 1)
        V.tensor_tensor(pw_lo[:], pw_raw[:], pw_hi[:].bitcast(F32), ALU.subtract).then_inc(pw_done, 1)
        V.memset(up[:, 0:PAD], 0.0).then_inc(pads_done, 1)
        V.memset(up[:, PAD + L:W], 0.0).then_inc(pads_done, 1)

        def y_lo(g):
            c = POOL_ORDER[g]
            for half in range(2):
                q = 2 * g + half
                dve.wait_ge(y_hi_done, q + 1)
                x = slice(half * HALF, (half + 1) * HALF)
                V.scalar_tensor_tensor(out=poolT_lo[:, c, x], in0=bank[Y_BANK[q]], scalar=pscale[:, c:c + 1],
                                       in1=poolT_hi[:, c, x].bitcast(F32), op0=ALU.mult, op1=ALU.subtract)\
                    .then_inc(y_done, 1)

        for g in range(NG):
            w = WINDOWS[g]
            dve.wait_ge(u_copied, 2 * g + 2)
            dve.wait_ge(pads_done, 2)
            if g:
                dve.wait_ge(d_hi_done, g)
                dve.wait_ge(d_done, g)
            b = (w.bit_length() - 1) % 2
            own.link(V.tensor_tensor(win[b][:, 1:W - 1], up[:, 0:W - 2], up[:, 1:W - 1], ALU.add))
            src, step, lo_i = win[b], 1, 1
            while 2 * step < w:
                b = 1 - b
                lo_i += step
                hi_i = W - lo_i
                own.link(V.tensor_tensor(win[b][:, lo_i:hi_i], src[:, lo_i - step:hi_i - step],
                                         src[:, lo_i + step:hi_i + step], ALU.add))
                src, step = win[b], 2 * step
            assert b == 1
            own.link(V.scalar_tensor_tensor(out=win[0][:, PAD:PAD + L], in0=src[:, PAD:PAD + L], scalar=1.0 / w,
                                            in1=up[:, PAD:PAD + L], op0=ALU.mult, op1=ALU.subtract))
            for n, e0 in enumerate((PAD, L)):
                e = slice(e0, e0 + PAD)
                own.link(V.tensor_tensor(edge_tmp[:, :], src[:, e], edge_inv[:, POOL_ORDER[g], n * PAD:(n + 1) * PAD],
                                         ALU.mult))
                ins = V.tensor_tensor(win[0][:, e], edge_tmp[:, :], up[:, e], ALU.subtract)
                if n:
                    ins.then_inc(d_made, 1)
                else:
                    own.link(ins)
            dve.wait_ge(d_hi_done, g + 1)
            V.tensor_tensor(dT_lo[:, :], win[0][:, PAD:PAD + L], dT_hi[:, :].bitcast(F32), ALU.subtract)\
                .then_inc(d_done, 1)
            if g:
                y_lo(g - 1)
        y_lo(NG - 1)

        def gate_turn(j):
            first = isinstance(j, int)
            for e in range(2):
                for half in range(2):
                    d = j * 2 + e
                    for n in range(2):
                        k = 4 * e + 2 * half + n
                        dve.wait_ge(d_ada2[n], j * 64 + (k // 2) * 16 + 16)
                        if k == 0:
                            if not first:
                                dve.wait_ge(mod2_ps, j)
                            ins = V.tensor_scalar(acc[:, :], ada2[:, n, :], c_silu[:, k, 0:1], None, ALU.mult)
                        else:
                            dve.wait_ge(ada2_used, j * 8 + k)
                            ins = V.scalar_tensor_tensor(out=acc[:, :], in0=ada2[:, n, :], scalar=c_silu[:, k, 0:1],
                                                         in1=acc[:, :], op0=ALU.mult, op1=ALU.add)
                        ins.then_inc(ada2_used, 1)
                    dve.wait_ge(sg_done, d * 4 + half * 2 + 1)
                    dve.wait_ge(m1_ps, d * 6 + half * 3 + 3)
                    if not first or e:
                        dve.wait_ge(spill_p[half], d * 16)
                    V.tensor_tensor(mpool[:, half, :], sgp[:, half, :], bank[3 * half + 2], ALU.mult)\
                        .then_inc(mp_done, 1)
            dve.wait_ge(ada2_used, j * 8 + 8)
            V.tensor_copy(edge_tmp[:, 0:1], acc[:, 0:1]).then_inc(acc_ready, 1)
            dve.wait_ge(mod2_ps, j + 1)
            V.tensor_copy(mod2[:, j, :], bank[6][:, 0:KD]).then_inc(mod2_done, 1)

        gate_turn(0)
        with dve.Fori(1, 4) as j:
            gate_turn(j)

        dve.wait_ge(mod2_done, 4)
        own.link(V.tensor_tensor(mod2[:], mod2[:], ada_b[:, 16:48].rearrange("p (m k) -> p m k", k=KD), ALU.add))
        own.link(V.scalar_tensor_tensor(out=gain2[:, :], in0=mod2[:, 2, :], scalar=1.0, in1=norm_g[:, 1, :],
                                        op0=ALU.add, op1=ALU.mult))
        dve.wait_ge(m1_ps, 6 * KD)
        dve.wait_ge(sg_done, 4 * KD)
        V.memset(z[:, NT:NTA, 0:P], 1.0).then_inc(z_set, 1)
        V.memset(na_tok[:, 0, 0:1], 0.0).then_inc(na_room, 16)
        dve.wait_ge(d_att, 48)
        V.tensor_scalar(qk_g[:, 0:P], qk_g[:, 0:P], HD ** -0.5, None, ALU.mult).then_inc(gain_set, 1)

        def sum_squares(p, t):
            dve.wait_ge(zsq_done, p * NTA + t + 1)
            V.tensor_reduce(rs[:, 4 * t:4 * t + 4], sq[:, t % 2, :].rearrange("p (s n) -> p s n", n=HD),
                            AX.X, ALU.add).then_inc(zsum_done, 1)

        def qk_mean(p):
            dve.wait_ge(zsum_done, p * NTA + NTA)
            rsqrt_begin(rs[:, :], slice(0, 40), HD, qk_ms)

        def qk_rsqrt(p):
            dve.wait_ge(qk_sqrt, p + 1)
            rsqrt_end(slice(0, 40))

        def normalise(p, half):
            ts = slice(5 * half, 5 * half + 5)
            dve.wait_ge(zg_done, p * NTA + NTA)
            V.tensor_tensor(nrm[:, ts, :].rearrange("p t (s n) -> p t s n", n=HD),
                            z[:, ts, 0:256].rearrange("p t (s n) -> p t s n", n=HD),
                            rs[:, 20 * half:20 * half + 20].rearrange("p (t s) -> p t s", s=4).unsqueeze(3)
                            .to_broadcast([P, 5, 4, HD]), ALU.mult).then_inc(nrm_done, 1)

        def rotate_q(p, hh):
            x = slice(hh * HD, (hh + 1) * HD)
            prod = rot_q[:, :, hh, :]
            if hh:
                dve.wait_ge(rotq_done, 2 * p + 1)
            else:
                dve.wait_ge(nrm_done, 2 * p + 2)
            own.done(V.tensor_tensor(prod, nrm[:, 0:NT, x], rope_c[:, :, :], ALU.mult))
            xh = nrm[:, 0:NT, x].rearrange("p t (c h n) -> p t c h n", h=2, n=HD // 4)
            sh = rope_s[:, :, :].rearrange("p t (c h n) -> p t c h n", h=2, n=HD // 4)
            th = rope_u[:, :, :].rearrange("p t (c h n) -> p t c h n", h=2, n=HD // 4)
            for h in range(2):
                own.done(V.tensor_tensor(th[:, :, :, h, :], xh[:, :, :, 1 - h, :], sh[:, :, :, h, :], ALU.mult))
            own.wait()
            V.tensor_tensor(prod, prod, rope_u[:, :, :], ALU.add).then_inc(rotq_done, 1)

        def take_v(p):
            dve.wait_ge(z_copied, p * NTA + NTA)
            V.tensor_copy(vcur[:, :, :], z[:, :, 256:384]).then_inc(v_taken, 1)

        def head_parts(p, hh):
            for n in range(7):
                dve.wait_ge(t_hi_done, p * 14 + hh * 7 + n + 1)
                if 2 <= n < 6:
                    q = (qrT, qpT)[n // 2 - 1][:, (n % 2) * HALF:(n % 2 + 1) * HALF]
                    ins = V.tensor_tensor(q[HD:P], bank[n][0:HD, :], q[0:HD].bitcast(F32), ALU.subtract)
                elif n < 2:
                    x = slice((n % 2) * HALF, (n % 2 + 1) * HALF)
                    ins = V.tensor_tensor(krT_lo[:, x], bank[n], krT_hi[:, x].bitcast(F32), ALU.subtract)
                else:
                    ins = V.tensor_tensor(kcT_lo[:, :], bank[6][:, 0:CTX], kcT_hi[:, :].bitcast(F32), ALU.subtract)
                ins.then_inc(t_done, 1)

        def soften(p, hh, i):
            s = p * 16 + hh * 8 + i
            n = i % 2
            w = HALF + (HD if inner(i) else 0)
            b0 = SLOTS_FULL * GRID_W if inner(i) else (2 * key_tile(i) - 2 * i + 6) * GRID_W
            flat = psflat[:, 2 * n * HALF:2 * n * HALF + w + CTX]
            dve.wait_ge(s_ps, s + 1)
            if i == 0:
                dve.wait_ge(d_bias, p * 32 + hh * 16 + 16)
            own.done(V.tensor_reduce(cmax[:, n:n + 1], flat[:, w:w + CTX], AX.X, ALU.max))
            own.link(V.tensor_tensor_reduce(flat[:, 0:w], flat[:, 0:w], bias[:, b0:b0 + w], 1.0,
                                            BIG, ALU.add, ALU.max, smax[:, n:n + 1]))
            V.tensor_scalar(nmax[:, n:n + 1], smax[:, n:n + 1], cmax[:, n:n + 1], -1.0, ALU.max, ALU.mult)\
                .then_inc(sm_ready, 1)

        def take_ctx_probs(p, hh, i):
            s = p * 16 + hh * 8 + i
            dve.wait_ge(pt_ps, s + 1)
            if i:
                dve.wait_ge(pv_ps, s)
            if inner(i):
                own.done(V.tensor_copy(probT[0:HD, 6, :], bank[5][0:HD, CTX:CTX + P]))
            else:
                own.done(V.tensor_copy(edge_tmp[:, 0:1], ones[:, 0:1]))
            own.wait()
            V.tensor_copy(probT[:, 4:6, :], bank[5][:, 0:CTX].rearrange("p (e n) -> p e n", n=P))\
                .then_inc(ptB_copied, 1)

        def take_values(p, hh, i):
            s = p * 16 + hh * 8 + i
            c = slice(i % 4, i % 4 + 1)
            dve.wait_ge(exp_done, s + 1)
            own.link(V.reciprocal(rden[:, c], den[:, c]))
            dve.wait_ge(pv_ps, s + 1)
            V.tensor_scalar(na_tok[:, i, hh * HD:(hh + 1) * HD], bank[6][:, 0:HD],
                            rden[:, c], None, ALU.mult).then_inc(na_done, 1)

        def attend(p, ahead):
            for hh in range(2):
                if ahead and hh == 0:
                    sum_squares(p + 1, 0)
                head_parts(p, hh)
                if ahead:
                    sum_squares(p + 1, 9 if hh else 1)
                if ahead and hh:
                    qk_mean(p + 1)
                soften(p, hh, 0)
                for i in range(8):
                    if i == 2 and hh == 0:
                        dve.wait_ge(na_room, p * 16 + 16)
                    if i >= 2:
                        take_values(p, hh, i - 2)
                    if i < 7:
                        soften(p, hh, i + 1)
                    take_ctx_probs(p, hh, i)
                    if ahead and hh == 0 and i < 7:
                        sum_squares(p + 1, i + 2)
                    if ahead and hh:
                        if i == 0:
                            qk_rsqrt(p + 1)
                        elif i < 3:
                            normalise(p + 1, i - 1)
                        elif i < 5:
                            rotate_q(p + 1, i - 3)
                    if not ahead and hh and i < 6:
                        result_lo(i // 2, i % 2)
                take_values(p, hh, 6)
                take_values(p, hh, 7)
            if ahead:
                take_v(p + 1)

        def result_lo(k, half):
            n = 2 * k + half
            x = slice(half * HALF, (half + 1) * HALF)
            b = 7 if k < PAIRS - 1 else 4 + half
            dve.wait_ge(nat_hi_done, n + 1)
            V.tensor_tensor(naT_lo[k][:, x], bank[b], naT_hi[k][:, x].bitcast(F32), ALU.subtract)\
                .then_inc(nat_split, 1)

        for t in range(NTA):
            sum_squares(0, t)
        qk_mean(0)
        take_v(0)
        qk_rsqrt(0)
        for half in range(2):
            normalise(0, half)
        for hh in range(2):
            rotate_q(0, hh)
        PER = 2 * 8 * (2 + 1 + 1) + 5 + 2 * 3
        with dve.Fori(0, PAIRS - 1) as p:
            own.enter(p, 0, PER)
            attend(p, True)
        own.leave(PAIRS - 1)
        dve.wait_ge(z_ps, PAIRS * NTA)
        for k in range(KD):
            V.tensor_scalar(g1diag[:, k, :], ident[:, :], mod2[:, 0, k:k + 1], None, ALU.mult).then_inc(g_diag, 1)
        attend(PAIRS - 1, False)

        for half in range(2):
            result_lo(PAIRS - 1, half)
        for n in range(16):
            d, x = n // 2, slice((n % 2) * HALF, (n % 2 + 1) * HALF)
            m = m_in[M_SLOT[d]]
            dve.wait_ge(m2_ps, n + 1)
            if n % 2 == 0:
                dve.wait_ge(d_m[M_SLOT[d]], 16 * M_SLOT[:d + 1].count(M_SLOT[d]))
            own.link(V.tensor_tensor(m[:, 0, x], m[:, 0, x], bank[n % 6], ALU.mult))
            V.tensor_tensor(m[:, 1, x], m[:, 1, x], m[:, 0, x], ALU.add).then_inc(m_sum, 1)
            dve.wait_ge(m_hi_done, n + 1)
            V.tensor_tensor(mT_lo[:, d, x], m[:, 1, x], mT_hi[:, d, x].bitcast(F32), ALU.subtract)\
                .then_inc(m_done, 1)
        dve.wait_ge(g_ready, 2)

        def renorm(t):
            dve.wait_ge(xss_done, t + 1)
            rsqrt_begin(row_ss[:, t:t + 1], slice(t, t + 1), D, xms)
            dve.wait_ge(xsqrt, t + 1)
            dve.wait_ge(xms, t + 1)
            rsqrt_end(slice(t, t + 1))
            V.tensor_scalar(nx[t // 4][:, t % 4, :], xn[:, t, :], rs[:, t:t + 1], None, ALU.mult)\
                .then_inc(nx_done, 1)

        def h2_lo_part(n):
            k, x = n % 8, slice((n // 8) * HALF, (n // 8 + 1) * HALF)
            dve.wait_ge(h2_hi_done, n + 1)
            V.tensor_tensor(h2_lo[:, k, x], h2tmp[:, n % 2, :], h2_hi[:, k, x].bitcast(F32), ALU.subtract)\
                .then_inc(h2_done, 1)

        for dh in range(2):
            for t in range(NT):
                n = 8 * dh + t
                dve.wait_ge(o_ps, n + 1)
                if dh == 0 and t % 4 == 0:
                    dve.wait_ge(d_xn[t // 4], 16)
                x = slice(dh * HALF, (dh + 1) * HALF)
                own.link(V.tensor_tensor(otmp[:, n % 2, :], gb[:, x], bank[n % 4], ALU.mult))
                V.tensor_tensor(xn[:, t, x], xn[:, t, x], otmp[:, n % 2, :], ALU.add).then_inc(xn_done, 1)
                if dh and 1 <= t < 7:
                    renorm(t - 1)
                if dh and t in (5, 6):
                    for k in range(4 * (t - 5), 4 * (t - 4)):
                        h2_lo_part(k)
        renorm(6)
        renorm(7)
        for n in range(8, 16):
            h2_lo_part(n)
        dve.wait_ge(h2_done, 16)
        for k in range(KD):
            V.tensor_scalar(g2diag[:, k, :], ident[:, :], mod2[:, 3, k:k + 1], None, ALU.mult).then_inc(g_diag, 1)

        def mlp_turn(g):
            first = isinstance(g, int)
            for pos in range(8):
                n = FIRST_ORDER[pos] if first else pos
                f, x = n // 2, slice((n % 2) * HALF, (n % 2 + 1) * HALF)
                dve.wait_ge(relu_done, g * 8 + pos + 1)
                if not first and n == 0:
                    dve.wait_ge(f2_ps, g * 16)
                own.link(V.tensor_copy(aT_hi[:, f, x], relu[:, pos % 2, :]))
                V.tensor_tensor(aT_lo[:, f, x], relu[:, pos % 2, :], aT_hi[:, f, x].bitcast(F32), ALU.subtract)\
                    .then_inc(a_done, 1)
            for n in range(16):
                dh, t = n // 8, n % 8
                x = slice(dh * HALF, (dh + 1) * HALF)
                dve.wait_ge(f2_ps, g * 16 + n + 1)
                if n == 0 and first:
                    dve.wait_ge(g_ready, 4)
                own.link(V.tensor_tensor(ytmp[:, n % 2, :], gb[:, x], bank[4 + n % 4], ALU.mult))
                V.tensor_tensor(xn[:, t, x], xn[:, t, x], ytmp[:, n % 2, :], ALU.add).then_inc(x_done, 1)

        mlp_turn(0)
        with dve.Fori(1, NFG) as g:
            own.enter(g, 1, 24)
            mlp_turn(g)
        own.leave(NFG - 1)


def shape_constants():
    t = np.arange(L)
    n_freq = HD // 4
    inv = np.float32(10000.0) ** (-np.arange(n_freq, dtype=np.float32) / np.float32(n_freq))
    ang = [(t // GRID_W).astype(np.float32)[:, None] * inv, (t % GRID_W).astype(np.float32)[:, None] * inv]
    cos = np.concatenate([f(x) for x in ang for f in (np.cos, np.cos)], 1)
    sin = np.concatenate([s * np.sin(x) for x in ang for s in (np.float32(-1), np.float32(1))], 1)
    tile = lambda m: np.ascontiguousarray(m.reshape(NT, P, HD).transpose(1, 0, 2).astype(np.float32))
    edge = np.zeros((NG, 2 * PAD), np.float32)
    for g, w in enumerate((2, 4, 8, 16)):
        pos = np.concatenate([np.arange(PAD), np.arange(L - PAD, L)])
        edge[g] = 1.0 / (np.minimum(pos + w // 2, L) - np.maximum(pos - w // 2, 0))
    return {"rope_c": tile(cos), "rope_s": tile(sin), "ident": np.eye(P, dtype=np.float32),
            "ones": np.ones((P, P), np.float32),
            "edge_inv": np.ascontiguousarray(np.broadcast_to(edge, (P, NG, 2 * PAD)))}


def bias_layout(rpb):
    q = np.arange(GRID_W)
    c0 = np.clip(q - NA_COLS // 2, 0, GRID_W - NA_COLS)
    rel = q[None, :] - q[:, None] + NA_COLS - 1
    seen = (q[None, :] >= c0[:, None]) & (q[None, :] < c0[:, None] + NA_COLS)
    rel = np.where(seen, rel, 0)
    out = np.full((HEADS, 2, GRID_W, SLOTS_FULL + SLOTS_INNER, GRID_W), BIG, np.float32)
    for odd in range(2):
        for s in range(SLOTS_FULL):
            out[:, odd, :, s, :] = np.where(seen[None], rpb[:, s + 1 - odd][:, rel], np.float32(BIG))
        for m in range(SLOTS_INNER):
            if m - odd in range(NA_ROWS):
                out[:, odd, :, SLOTS_FULL + m, :] = out[:, odd, :, m + 2, :]
    return out.reshape(HEADS, P, BIASW)


def by_k(w):
    return w.reshape(-1, P, w.shape[1]).transpose(1, 0, 2).reshape(P, -1)


def units_layout(i):
    w_in, w_bp, w_bn = i["w_in"][0], i["w_branch_pool"][0], i["w_branch_na"][0]
    w_out, w1, w2 = i["w_out"][0], i["mlp_w1"][0], i["mlp_w2"][0]
    u = np.zeros((UNITS, P, 1024), np.float32)
    for n, g in enumerate(POOL_ORDER):
        u[U_POOL + n] = by_k(w_in[:, g * P:(g + 1) * P])
    for d in range(KD):
        c = slice(d * P, (d + 1) * P)
        u[U_GATE + 3 * d] = by_k(w_in[:, 2048:3072][:, c])
        u[U_GATE + 3 * d + 1] = by_k(w_in[:, 3072:4096][:, c])
        u[U_GATE + 3 * d + 2, :, 0:512] = by_k(w_bp[:, c])
        u[U_NA + d // 2, :, (d % 2) * 512:(d % 2 + 1) * 512] = by_k(w_bn[:, c])
    for p in range(PAIRS):
        for n in range(3):
            u[U_ATT + 3 * p + n] = by_k(w_in[:, 512 * (n + 1) + p * P:512 * (n + 1) + (p + 1) * P])
    for dh in range(2):
        for n in range(4):
            u[U_OUT + 4 * dh + n] = by_k(w_out[n * 256:(n + 1) * 256, dh * HALF:(dh + 1) * HALF])
    for g in range(NFG):
        for r, (kind, c, _) in enumerate(MLP_ORDER):
            f = slice(g * FG + c * P, g * FG + (c + 1) * P)
            u[U_MLP + 8 * g + r] = by_k(w1[:, f]) if kind == "w1" else w2[f]
    return u


def lay_out(inputs):
    i = {k: np.asarray(v) for k, v in inputs.items()}
    x = i["x"][0]
    ada = i["ada_w"][0]
    col = lambda v: np.ascontiguousarray(v.reshape(-1, P).T)
    g = {
        "x": x,
        "xT": np.concatenate([x, i["ctx"][0]], 0).T.reshape(KD, P, T),
        "c_col": np.stack([col(i["c"][0]), col(i["c_ctx"])], -1),
        "norm_g": np.stack([col(i["norm1_g"][0]), col(i["norm2_g"][0])], 1),
        "ada_b": col(i["ada_b"][0]),
        "pscale": col(i["pool_scale"][0]),
        "pool_w": i["pool_w"][0].transpose(1, 0, 2),
        "qk_g": np.broadcast_to(np.concatenate([i["q_norm_g"][0]] * 2 + [i["k_norm_g"][0]] * 2), (P, 256)),
        "ada1": ada[:, 0:2048].reshape(KD, P, 2048),
        "ada2": ada[:, 2048:].reshape(KD, P, 4, 1024).transpose(2, 0, 1, 3).reshape(32, P, 1024),
        "bias": bias_layout(i["rpb"][0]),
        "units": units_layout(i),
    }
    g.update(shape_constants())
    return {k: np.ascontiguousarray(v) for k, v in g.items()}


def kernel(**inputs):
    import concourse.bacc as bacc
    from concourse.bass_utils import run_bass_kernel_spmd

    nc = bacc.Bacc("TRN2", target_bir_lowering=False, num_devices=1)
    arrays = {f"in_{k}": v for k, v in lay_out(inputs).items()}
    a = {k[3:]: nc.dram_tensor(k, v.shape, F32, kind="ExternalInput").ap() for k, v in arrays.items()}
    out = nc.dram_tensor("x_out", (L, D), F32, kind="ExternalOutput").ap()
    build(nc, a, out)
    r = run_bass_kernel_spmd(nc, [arrays], core_ids=[0])
    return r.results[0]["x_out"].reshape(1, L, D)
```

```python
from contextlib import ExitStack

import numpy as np
import concourse.bass as bass
from concourse import mybir

P = 128
D = 1024
L = 1024
CTX = 256
T = L + CTX
KD = D // P
NT = L // P
NTA = T // P
GRID_W = 64
ROWS = L // GRID_W
WINDOWS = (16, 8, 4, 2)
POOL_ORDER = (3, 2, 1, 0)
NG = 4
PAD = 8
HD = 64
HEADS = 8
PAIRS = HEADS // 2
NA_ROWS, NA_COLS = 8, 16
D_FF = 4096
FG = 512
NFG = D_FF // FG
FCH = FG // P
EPS = 1e-6
HALF = 512
BIG = -1e30
SLOTS_FULL = 14
SLOTS_INNER = 9
BIASW = (SLOTS_FULL + SLOTS_INNER) * GRID_W

U_POOL = 0
U_GATE = U_POOL + NG
U_ATT = U_GATE + 3 * KD
U_NA = U_ATT + 3 * PAIRS
U_OUT = U_NA + 4
U_MLP = U_OUT + 8
UNITS = U_MLP + 8 * NFG
FIRST_ORDER = (0, 2, 1, 3, 4, 5, 6, 7)
MLP_ORDER = (("w1", 0, 0), ("w1", 1, 1), ("w2", 0, 2), ("w1", 2, 0),
             ("w2", 1, 3), ("w1", 3, 1), ("w2", 2, 4), ("w2", 3, 5))

F32 = mybir.dt.float32
F32R = mybir.dt.float32r
ALU = mybir.AluOpType
ACT = mybir.ActivationFunctionType
AX = mybir.AxisListType


def key_tile(i):
    return min(max(i - 2, 0), 4)


def inner(i):
    return 2 <= i <= 5


class Steps:

    def __init__(self, eng, sem):
        self.eng, self.sem, self.base, self.n = eng, sem, 0, 0

    def done(self, ins):
        ins.then_inc(self.sem, 1)
        self.n += 1

    def wait(self):
        self.eng.wait_ge(self.sem, self.base + self.n)

    def link(self, ins):
        self.done(ins)
        self.wait()

    def enter(self, i, first, per_turn):
        self.base, self.n, self.per, self.start = self.start_of(i, first, per_turn), 0, per_turn, self.base + self.n

    def start_of(self, i, first, per_turn):
        return (i - first) * per_turn + (self.base + self.n)

    def leave(self, turns):
        assert self.n == self.per, (self.n, self.per)
        self.base, self.n = self.start + self.per * turns, 0


def build(nc, a, out):
    with ExitStack() as ctx:
        build_in(nc, a, out, ctx)


def build_in(nc, a, out, ctx):
    KB = 1024
    CONST = 32 * KB
    H = 35 * KB
    R = H + 80 * KB
    base = 16 * KB + 512

    def at(name, shape, dt, off):
        return nc.alloc_sbuf_tensor_at(name, shape, dt, offset=base + off)

    ringA_hi = at("ringA_hi", [P, 3, 1024], F32R, 0)
    ringA_lo = at("ringA_lo", [P, 3, 1024], F32R, 12 * KB)
    rawA = at("rawA", [P, 2, 1024], F32, 24 * KB)
    off = CONST
    def const(name, shape, dt=F32):
        nonlocal off
        n = 4 * int(np.prod(shape[1:]))
        t = at(name, shape, dt, off)
        off += (n + 31) // 32 * 32
        assert off <= H
        return t
    ident = const("ident", [P, P])
    ones = const("ones", [P, P])
    c_col = const("c_col", [P, KD, 2])
    c_sig = const("c_sig", [P, KD, 2])
    c_silu = const("c_silu", [P, KD, 2])
    norm_g = const("norm_g", [P, 2, KD])
    ada_b = const("ada_b", [P, 48])
    pscale = const("pscale", [P, NG])
    edge_inv = const("edge_inv", [P, NG, 2 * PAD])
    edge_tmp = const("edge_tmp", [P, PAD])
    mod1 = const("mod1", [P, 16, 2])
    gain1 = const("gain1", [P, KD, 2])
    mod2 = const("mod2", [P, 4, KD])
    gain2 = const("gain2", [P, KD])
    ms = const("ms", [P, 40])
    rs = const("rs", [P, 40])
    rt = const("rt", [P, 40])
    row_ss = const("row_ss", [P, NT])
    cmax = const("cmax", [P, 2])
    smax = const("smax", [P, 2])
    nmax = const("nmax", [P, 2])
    den = const("den", [P, 4])
    rden = const("rden", [P, 4])
    ringB_hi = at("ringB_hi", [P, 3, 1024], F32R, R)
    ringB_lo = at("ringB_lo", [P, 3, 1024], F32R, R + 12 * KB)
    rawB = at("rawB", [P, 2, 1024], F32, R + 24 * KB)
    ada1 = at("ada1", [P, KD, 2048], F32, H)
    xsq = at("xsq", [P, 2, T], F32, H + 64 * KB)
    xsum = at("xsum", [P, T], F32, H + 74 * KB)
    xT = at("xT", [P, KD, T], F32, R + 32 * KB)
    hfull = at("hfull", [P, 2, L], F32, R + 72 * KB)
    mod_row = at("mod_row", [2, 2048], F32, R + 72 * KB)
    diag = at("diag", [P, NTA, P], F32, R + 82 * KB)
    rctx = diag[:, 0:CTX // P, :].rearrange("p t n -> p (t n)")
    hT_hi = at("hT_hi", [P, KD, T], F32R, H)
    hT_lo = at("hT_lo", [P, KD, T], F32R, H + 40 * KB)
    poolT_hi = at("poolT_hi", [P, NG, L], F32R, R + 32 * KB)
    poolT_lo = at("poolT_lo", [P, NG, L], F32R, R + 48 * KB)
    W = L + 2 * PAD
    up = at("up", [P, W], F32, R + 64 * KB)
    win = [at(f"win{n}", [P, W], F32, R + 64 * KB + 4160 * (n + 1)) for n in range(2)]
    dT_hi = at("dT_hi", [P, L], F32R, R + 64 * KB + 12480)
    dT_lo = at("dT_lo", [P, L], F32R, R + 64 * KB + 16576)
    pw_lo = at("pw_lo", [P, NG, P], F32R, R + 64 * KB + 20672)
    pw_raw = at("pw_raw", [P, NG, P], F32, R + 89088)
    pw_hi = at("pw_hi", [P, NG, P], F32R, R + 91136)
    sgp = at("sgp", [P, 2, HALF], F32, R + 64 * KB)
    sgn = at("sgn", [P, 2, HALF], F32, R + 68 * KB)
    mpool = at("mpool", [P, 2, HALF], F32, R + 72 * KB)
    acc = at("acc", [P, 1024], F32, R + 76 * KB)
    ada2 = at("ada2", [P, 2, 1024], F32, R + 80 * KB)
    sgp_late = at("sgp_late", [P, HALF], F32, R + 80 * KB)
    sgn_late = at("sgn_late", [P, HALF], F32, R + 82 * KB)
    mpool_late = at("mpool_late", [P, HALF], F32, R + 86 * KB)
    qrT = at("qrT", [P, L], F32R, R)
    qpT = at("qpT", [P, L], F32R, R + 4 * KB)
    krT_hi = at("krT_hi", [P, L], F32R, R + 8 * KB)
    krT_lo = at("krT_lo", [P, L], F32R, R + 12 * KB)
    kcT_hi = at("kcT_hi", [P, CTX], F32R, R + 16 * KB)
    kcT_lo = at("kcT_lo", [P, CTX], F32R, R + 17 * KB)
    vcur = at("vcur", [P, NTA, P], F32, R + 18 * KB)
    probT = at("probT", [P, 7, P], F32, R + 23 * KB)
    rope_c = at("rope_c", [P, NT, HD], F32, R + 26 * KB + 512)
    rope_s = at("rope_s", [P, NT, HD], F32, R + 28 * KB + 512)
    qk_g = at("qk_g", [P, 256], F32, R + 30 * KB + 512)
    z = at("z", [P, NTA, 384], F32, R + 32 * KB)
    nrm = at("nrm", [P, NTA, 256], F32, R + 47 * KB)
    rot_q = at("rot_q", [P, NT, 2, HD], F32, R + 57 * KB)
    rot_k = at("rot_k", [P, NT, 2, 2, HD], F32, R + 61 * KB)
    kc2 = at("kc2", [P, 2, 2, 2, HD], F32, R + 69 * KB)
    rope_t = at("rope_t", [P, NT, HD], F32, R + 71 * KB)
    prob = at("prob", [P, 2, 832], F32, R + 73 * KB)
    bias = at("bias", [P, BIASW], F32, R + 73 * KB + 6656)
    na_tok = at("na_tok", [P, NT, P], F32, R + 73 * KB + 6656 + 4 * BIASW)
    rope_u = at("rope_u", [P, NT, HD], F32, R + 73 * KB + 6656 + 4 * BIASW + 4 * KB)
    sq = at("sq", [P, 2, 256], F32, R + 73 * KB + 6656 + 4 * BIASW + 4 * KB)
    na_in = at("na_in", [P, PAIRS - 1, NT, P], F32, H + 40 * KB)
    naT_hi = [at(f"naT_hi{k}", [P, L], F32R, R + (48 + 8 * k) * KB) for k in range(PAIRS)]
    naT_lo = [at(f"naT_lo{k}", [P, L], F32R, R + (52 + 8 * k) * KB) for k in range(PAIRS)]
    g1diag = at("g1diag", [P, KD, P], F32, H + 72 * KB)
    m_in = [at(f"m_in{n}", [P, 2, L], F32, H + kb * KB) for n, kb in enumerate((24, 56, 16, 64, 72))]
    mT_hi = at("mT_hi", [P, KD, L], F32R, H)
    mT_lo = at("mT_lo", [P, KD, L], F32R, H + 32 * KB)
    xn = at("xn", [P, NT, D], F32, R + 32 * KB)
    nx = [at("nx0", [P, 4, D], F32, R + 64 * KB), at("nx1", [P, 4, D], F32, H + 64 * KB)]
    gb = at("gb", [P, D], F32, R + 80 * KB)
    otmp = at("otmp", [P, 2, HALF], F32, R + 84 * KB)
    h2tmp = at("h2tmp", [P, 2, HALF], F32, R + 88 * KB)
    g2diag = at("g2diag", [P, KD, P], F32, R + 88 * KB)
    h2_hi = at("h2_hi", [P, KD, L], F32R, H)
    h2_lo = at("h2_lo", [P, KD, L], F32R, H + 32 * KB)
    aT_hi = at("aT_hi", [P, FCH, L], F32R, H + 64 * KB)
    aT_lo = at("aT_lo", [P, FCH, L], F32R, R + 64 * KB)
    relu = at("relu", [P, 2, HALF], F32, R + 84 * KB)
    ytmp = at("ytmp", [P, 2, HALF], F32, R + 88 * KB)

    ps = ctx.enter_context(nc.psum_tensor("ps", [P, 8, HALF], F32))
    bank = [ps[:, b, :] for b in range(8)]
    psflat = ps[:, :, :].rearrange("p b n -> p (b n)")

    spill_m = nc.dram_tensor("spill_m", (KD, P, 2, L), F32, kind="Internal").ap()
    spill_na = nc.dram_tensor("spill_na", (PAIRS - 1, P, NT, P), F32, kind="Internal").ap()

    def hi(s):
        return (ringA_hi if s < 3 else ringB_hi)[:, s % 3, :]

    def lo(s):
        return (ringA_lo if s < 3 else ringB_lo)[:, s % 3, :]

    def raw(r):
        return (rawA if r < 2 else rawB)[:, r % 2, :]

    def sem(name):
        return ctx.enter_context(nc.semaphore(name))

    d_const = sem("d_const")
    d_att = sem("d_att")
    d_x = [sem(f"d_x{k}") for k in range(KD)]
    d_c = sem("d_c")
    d_ada1 = [sem(f"d_ada1_{k}") for k in range(KD)]
    d_raw = [sem(f"d_raw{r}") for r in range(4)]
    p_own = sem("p_own")
    split_hi = sem("split_hi")
    split = sem("split")
    v_own = sem("v_own")
    a_own = sem("a_own")
    sig_done = sem("sig_done")
    silu_done = sem("silu_done")
    sq_done = sem("sq_done")
    row_ps = sem("row_ps")
    row_copied = sem("row_copied")
    xsum_done = sem("xsum_done")
    ssq_ps = sem("ssq_ps")
    ms_ready = sem("ms_ready")
    sqrt_done = sem("sqrt_done")
    diag_ready = sem("diag_ready")
    rb_ps = sem("rb_ps")
    mod1_ps = sem("mod1_ps")
    rctx_ready = sem("rctx_ready")
    xr_ready = sem("xr_ready")
    ctx_xr = sem("ctx_xr")
    ctx_hi_done = sem("ctx_hi_done")
    ctx_done = sem("ctx_done")
    h_hi_done = sem("h_hi_done")
    h_done = sem("h_done")
    pw_done = sem("pw_done")
    u_ps = sem("u_ps")
    pads_done = sem("pads_done")
    u_copied = sem("u_copied")
    d_made = sem("d_made")
    d_hi_done = sem("d_hi_done")
    d_done = sem("d_done")
    y_ps = sem("y_ps")
    y_hi_done = sem("y_hi_done")
    y_done = sem("y_done")
    m1_ps = sem("m1_ps")
    late_ps = sem("late_ps")
    sg_done = sem("sg_done")
    mp_done = sem("mp_done")
    spill_g = [sem(f"spill_g{n}") for n in range(2)]
    spill_p = [sem(f"spill_p{n}") for n in range(2)]
    d_ada2 = [sem(f"d_ada2_{n}") for n in range(2)]
    ada2_used = sem("ada2_used")
    acc_ready = sem("acc_ready")
    mod2_ps = sem("mod2_ps")
    mod2_done = sem("mod2_done")
    z_ps = sem("z_ps")
    z_set = sem("z_set")
    z_copied = sem("z_copied")
    v_taken = sem("v_taken")
    zsq_done = sem("zsq_done")
    zsum_done = sem("zsum_done")
    gain_set = sem("gain_set")
    zg_done = sem("zg_done")
    qk_ms = sem("qk_ms")
    qk_sqrt = sem("qk_sqrt")
    nrm_done = sem("nrm_done")
    rotq_done = sem("rotq_done")
    rotk_done = sem("rotk_done")
    t_ps = sem("t_ps")
    t_hi_done = sem("t_hi_done")
    t_done = sem("t_done")
    s_ps = sem("s_ps")
    sm_ready = sem("sm_ready")
    exp_done = sem("exp_done")
    pt_ps = sem("pt_ps")
    ptA_copied = sem("ptA_copied")
    ptB_copied = sem("ptB_copied")
    pv_ps = sem("pv_ps")
    na_done = sem("na_done")
    nat_ps = sem("nat_ps")
    nat_hi_done = sem("nat_hi_done")
    nat_split = sem("nat_split")
    na_room = sem("na_room")
    d_bias = sem("d_bias")
    d_na = sem("d_na")
    d_m = [sem(f"d_m{n}") for n in range(5)]
    m2_ps = sem("m2_ps")
    m_sum = sem("m_sum")
    m_hi_done = sem("m_hi_done")
    m_done = sem("m_done")
    d_xn = [sem(f"d_xn{n}") for n in range(2)]
    g_diag = sem("g_diag")
    g_ps = sem("g_ps")
    g_ready = sem("g_ready")
    o_ps = sem("o_ps")
    o_part = sem("o_part")
    xn_done = sem("xn_done")
    xss_done = sem("xss_done")
    xms = sem("xms")
    xsqrt = sem("xsqrt")
    nx_done = sem("nx_done")
    h2_ps = sem("h2_ps")
    h2_full = sem("h2_full")
    h2_hi_done = sem("h2_hi_done")
    h2_done = sem("h2_done")
    f1_ps = sem("f1_ps")
    relu_done = sem("relu_done")
    a_done = sem("a_done")
    f2_ps = sem("f2_ps")
    x_done = sem("x_done")
    d_out = sem("d_out")

    G_RAW = (0, 1, 2, 3)
    M1_RAW = (0, 1, 2, 0, 1, 2)
    M1_SLOT = (1, 2, 0, 4, 5, 3)
    A_RAW = (0, 1, 0)
    N_RAW = (0, 1, 0, 1)
    O_RAW = (0, 1, 2, 3, 0, 1, 2, 3)
    O_SLOT = (4, 5, 0, 1, 2, 3, 4, 5)
    F_RAW = (0, 1, 2, 3, 0, 1, 2, 3)
    M1_LAST = 6 * KD - 2
    def late(j, e, half):
        return isinstance(j, int) and 2 * j + e == KD - 1 and half == 1

    NORM_STEPS = (1, 2, 3, 5)
    T_BANK = (0, 1, 2, 3, 0, 1, 6)
    Y_BANK = (0, 1, 2, 3, 6, 7, 6, 7)
    M_SLOT = (0, 1, 2, 3, 4, 0, 3, 4)
    raws_before = {}
    seen = [0] * 4
    for name, table, turns in (("pool", G_RAW, 1), ("gate", M1_RAW, 4), ("att", A_RAW, PAIRS),
                               ("na", N_RAW, 1), ("out", O_RAW, 1), ("mlp", F_RAW, NFG)):
        raws_before[name] = (table, list(seen))
        for r in table:
            seen[r] += turns

    def landed(phase, turn, r):
        table, before = raws_before[phase]
        s = table[r]
        return s, 16 * (before[s] + turn * table.count(s) + table[:r + 1].count(s))

    block = ctx.enter_context(nc.Block())

    @block.sync
    def _(sp):
        sp.dma_start(c_col[:], a["c_col"]).then_inc(d_c, 16)
        for k in range(KD):
            sp.dma_start(ada1[:, k, :], a["ada1"][k]).then_inc(d_ada1[k], 16)
        consts = [(ident, "ident"), (ones, "ones"), (norm_g, "norm_g"),
                  (ada_b, "ada_b"), (pscale, "pscale"), (edge_inv, "edge_inv"), (pw_raw, "pool_w")]
        for t, name in consts:
            sp.dma_start(t[:], a[name]).then_inc(d_const, 16)
        for k in range(KD):
            sp.dma_start(xT[:, k, :], a["xT"][k]).then_inc(d_x[k], 16)

        def load(phase, turn, r, unit, cols=1024):
            s, _ = landed(phase, turn, r)
            sp.dma_start(raw(s)[:, 0:cols], a["units"][unit, :, 0:cols]).then_inc(d_raw[s], 16)

        for g in range(NG):
            load("pool", 0, g, U_POOL + g)
        with sp.Fori(0, 4) as j:
            for r in range(6):
                unit = U_GATE + j * 6 + r
                sp.wait_ge(split, unit - 2)
                load("gate", j, r, unit, 1024 if r % 3 < 2 else 512)
        with sp.Fori(0, PAIRS) as p:
            for r, back in ((0, 0), (1, 2), (2, 1)):
                unit = U_ATT + p * 3 + r
                sp.wait_ge(split, unit - back)
                load("att", p, r, unit)
        for r in range(4):
            sp.wait_ge(split, (U_NA, U_NA - 1, U_NA + 1, U_NA + 2)[r])
            load("na", 0, r, U_NA + r)
        for r in range(8):
            if r == 2:
                sp.wait_ge(pv_ps, 8 * HEADS)
            sp.wait_ge(split, U_OUT + (-1, 0, 0, 0, 1, 2, 3, 4)[r])
            load("out", 0, r, U_OUT + r)
        with sp.Fori(0, NFG) as g:
            for r in range(8):
                unit = U_MLP + g * 8 + r
                sp.wait_ge(split, unit - 3)
                load("mlp", g, r, unit)
        for dh in range(2):
            for t in range(NT):
                sp.wait_ge(x_done, 16 * (NFG - 1) + 8 * dh + t + 1)
                sp.dma_start(out[t * P:(t + 1) * P, dh * HALF:(dh + 1) * HALF],
                             xn[:, t, dh * HALF:(dh + 1) * HALF]).then_inc(d_out, 16)
        sp.wait_ge(d_out, 16 * 16)

    @block.gpsimd
    def _(pool):
        def split_unit(phase, turn, r, slot, unit, cols=1024, lo_only=False):
            s, count = landed(phase, turn, r)
            pool.wait_ge(d_raw[s], count)
            h, l, w = hi(slot)[:, 0:cols], lo(slot)[:, 0:cols], raw(s)[:, 0:cols]
            if lo_only:
                pool.wait_ge(split_hi, unit + 1)
                nc.gpsimd.tensor_tensor(l, w, h.bitcast(F32), ALU.subtract).then_inc(split, 1)
                return
            nc.gpsimd.tensor_tensor(h, w, ones[:, 0:1].to_broadcast([P, cols]), ALU.mult).then_inc(split_hi, 1)
            pool.wait_ge(split_hi, unit + 1)
            nc.gpsimd.tensor_tensor(l, w, h.bitcast(F32), ALU.subtract).then_inc(split, 1)

        own = Steps(pool, p_own)
        pool.wait_ge(d_const, 7 * 16)
        for g in range(NG):
            split_unit("pool", 0, g, g, U_POOL + g)
        def gate_turn(j):
            for r in range(6):
                d = j * 2 + r // 3
                if isinstance(j, int) and j == 0:
                    if M1_SLOT[r] < NG:
                        pool.wait_ge(u_ps, 2 * M1_SLOT[r] + 2)
                else:
                    pool.wait_ge(m1_ps, (d - 2) * 6 + 4 + r % 3)
                split_unit("gate", j, r, M1_SLOT[r], U_GATE + j * 6 + r, 1024 if r % 3 < 2 else 512)
        gate_turn(0)
        with pool.Fori(1, 4) as j:
            gate_turn(j)
        for r in range(3):
            pool.wait_ge(m1_ps, 6 * (KD - 1))
            split_unit("att", 0, r, r, U_ATT + r)

        def gains(p, tiles=range(NTA)):
            for t in tiles:
                pool.wait_ge(zsq_done, p * NTA + t + 1)
                x = slice(0 if t < NT else P, 256)
                nc.gpsimd.tensor_tensor(z[:, t, x], z[:, t, x], qk_g[:, x], ALU.mult).then_inc(zg_done, 1)

        def rotate_k(p, t0=0, t1=NT):
            TT = nc.gpsimd.tensor_tensor
            pool.wait_ge(nrm_done, 2 * p + (2 if t1 == NT else 1))
            for hh in range(2):
                x, ts = slice(P + hh * HD, P + (hh + 1) * HD), slice(t0, t1)
                prod = rot_k[:, ts, hh, 1, :]
                own.done(TT(prod, nrm[:, ts, x], rope_c[:, ts, :], ALU.mult))
                xh = nrm[:, ts, x].rearrange("p t (c h n) -> p t c h n", h=2, n=HD // 4)
                sh = rope_s[:, ts, :].rearrange("p t (c h n) -> p t c h n", h=2, n=HD // 4)
                th = rope_t[:, ts, :].rearrange("p t (c h n) -> p t c h n", h=2, n=HD // 4)
                for h in range(2):
                    own.done(TT(th[:, :, :, h, :], xh[:, :, :, 1 - h, :], sh[:, :, :, h, :], ALU.mult))
                own.wait()
                both = [P, t1 - t0, 2, HD]
                own.link(TT(rot_k[:, ts, hh, :, :], prod.unsqueeze(2).to_broadcast(both),
                            rope_t[:, ts, :].unsqueeze(2).to_broadcast(both), ALU.add))
                if t1 < NT:
                    continue
                both = [P, 2, 2, HD]
                TT(kc2[:, :, hh, :, :], nrm[:, NT:NTA, x].unsqueeze(2).to_broadcast(both),
                   ones[:, 0:HD].unsqueeze(1).unsqueeze(1).to_broadcast(both), ALU.mult).then_inc(rotk_done, 1)

        pool.wait_ge(gain_set, 1)
        pool.wait_ge(mp_done, 2 * KD - 1)
        for n in range(2):
            pool.wait_ge(spill_g[n], 16 * (KD - n))
            pool.wait_ge(spill_p[n], 16 * (KD - n))
        gains(0, range(5))
        rotate_k(0, 0, 5)
        gains(0, range(5, NTA))
        split_unit("att", 1, 0, 0, U_ATT + 3, lo_only=True)
        rotate_k(0, 5, NT)
        for r in range(1, 3):
            split_unit("att", 1, r, r, U_ATT + 3 + r, lo_only=True)
        with pool.Fori(1, PAIRS - 1) as p:
            own.enter(p, 1, 8)
            gains(p)
            pool.wait_ge(z_ps, p * NTA + NTA)
            split_unit("att", p + 1, 0, 0, U_ATT + p * 3 + 3)
            rotate_k(p)
            for r in range(1, 3):
                split_unit("att", p + 1, r, r, U_ATT + p * 3 + 3 + r, lo_only=True)
        own.leave(PAIRS - 2)
        gains(PAIRS - 1)
        rotate_k(PAIRS - 1)
        pool.wait_ge(z_ps, PAIRS * NTA)
        for r in range(4):
            if r == 3:
                pool.wait_ge(pv_ps, 8 * HEADS)
            split_unit("na", 0, r, r, U_NA + r)
        for r in range(8):
            if 2 <= r < 6:
                pool.wait_ge(m2_ps, 4 * (r - 1))
            if r >= 6:
                pool.wait_ge(o_part, r - 5)
            split_unit("out", 0, r, O_SLOT[r], U_OUT + r)
        def mlp_turn(g):
            first = isinstance(g, int)
            for r, (kind, c, slot) in enumerate(MLP_ORDER):
                if kind == "w1" and c >= 2:
                    pool.wait_ge(f1_ps, g * 8 + ((3, 4)[c - 2] if first else 2 * (c - 2) + 2))
                elif kind == "w1":
                    if first:
                        pool.wait_ge(o_ps, 8)
                    else:
                        pool.wait_ge(f1_ps, (g - 1) * 8 + 2 * (c + 2) + 2)
                elif first:
                    pool.wait_ge(o_ps, 16)
                else:
                    pool.wait_ge(f2_ps, g * 16)
                split_unit("mlp", g, r, slot, U_MLP + g * 8 + r)
        mlp_turn(0)
        with pool.Fori(1, NFG) as g:
            mlp_turn(g)

    @block.tensor
    def _(pe):
        mm = nc.tensor.matmul

        def three(o, wh, wl, xh, xl, first, last):
            mm(o, wh, xh, start=first, stop=False)
            mm(o, wh, xl, start=False, stop=False)
            return mm(o, wl, xh, start=False, stop=last)

        pe.wait_ge(silu_done, 1)
        for k in range(KD):
            pe.wait_ge(d_ada1[k], 16)
            for j in range(4):
                last = mm(bank[4 + j][0:2, :], c_silu[:, k, :], ada1[:, k, j * HALF:(j + 1) * HALF],
                          start=(k == 0), stop=(k == KD - 1))
        last.then_inc(row_ps, 1)
        pe.wait_ge(d_const, 7 * 16)
        pe.wait_ge(row_copied, 4)
        for j in range(16):
            last = mm(bank[0][:, 2 * j:2 * j + 2], mod_row[:, j * P:(j + 1) * P], ident[0:2, 0:2],
                      start=True, stop=True)
        last.then_inc(mod1_ps, 1)
        pe.wait_ge(xsum_done, KD - 1)
        for t in range(NTA):
            last = mm(bank[3][:, t:t + 1], xsum[:, t * P:(t + 1) * P], ones[:, 0:1], start=True, stop=True)
        last.then_inc(ssq_ps, 1)
        for t in range(NTA):
            pe.wait_ge(diag_ready, t + 1)
            last = mm(psflat[:, HALF + t * P:HALF + (t + 1) * P], ones[:, :], diag[:, t, :],
                      start=True, stop=True)
        last.then_inc(rb_ps, 1)

        def pool_part(q, k):
            g, x = q // 2, slice((q % 2) * HALF, (q % 2 + 1) * HALF)
            last = three(bank[4 + q % 4], hi(g)[:, k * P:(k + 1) * P], lo(g)[:, k * P:(k + 1) * P],
                         hT_hi[:, k, x], hT_lo[:, k, x], k == 0, k == KD - 1)
            if k == KD - 1:
                last.then_inc(u_ps, 1)

        def pool_u(g):
            pe.wait_ge(split, U_POOL + g + 1)
            for half in range(2):
                pe.wait_ge(u_copied, 2 * g + half - 3)
                for k in range(KD):
                    pool_part(2 * g + half, k)

        def pool_y(g):
            if g == 0:
                pe.wait_ge(pw_done, 1)
            pe.wait_ge(d_done, g + 1)
            for half in range(2):
                q = 2 * g + half
                if g == 3:
                    pe.wait_ge(y_done, q - 1)
                elif g == 2:
                    pe.wait_ge(u_copied, 8)
                x = slice(half * HALF, (half + 1) * HALF)
                c = POOL_ORDER[g]
                three(bank[Y_BANK[q]], pw_hi[:, c, :], pw_lo[:, c, :], dT_hi[:, x], dT_lo[:, x],
                      True, True).then_inc(y_ps, 1)

        pe.wait_ge(split, U_POOL + 2)
        for k in range(KD):
            pe.wait_ge(h_done, k + 1)
            for q in range(4):
                pool_part(q, k)
        pool_u(2)
        pool_y(0)
        pool_u(3)
        pool_y(1)

        def gate(slot, b, x):
            for k in range(KD):
                w = slice(k * P, (k + 1) * P)
                last = three(bank[b], hi(slot)[:, w], lo(slot)[:, w],
                             hT_hi[:, k, x], hT_lo[:, k, x], k == 0, k == KD - 1)
            last.then_inc(m1_ps, 1)

        def gate_turn(j):
            for e in range(2):
                d = j * 2 + e
                sg, sn, sb = M1_SLOT[3 * e:3 * e + 3]
                for half in range(2):
                    x = slice(half * HALF, (half + 1) * HALF)
                    for n, slot in enumerate((sg, sn)):
                        if late(j, e, half) or (isinstance(j, int) and d == n == 0 and half == 1):
                            continue
                        if half == 0:
                            pe.wait_ge(split, U_GATE + d * 3 + n + 1)
                        if isinstance(j, int) and j == 0 and e == 0:
                            if half == 0 and n == 0:
                                pe.wait_ge(y_done, 2)
                        else:
                            pe.wait_ge(sg_done, d * 4 + half * 2 + n - 3)
                        gate(slot, 3 * half + n, x)
                        if not (isinstance(j, int) and j == 0) and e == half == n == 0:
                            modulation(j - 1)
                    if half == 0:
                        pe.wait_ge(split, U_GATE + d * 3 + 3)
                    if isinstance(j, int) and j == 0 and e == half == 0:
                        pe.wait_ge(y_done, 4)
                        gate(sg, 3, slice(HALF, L))
                        pool_y(2)
                        pool_y(3)
                        pe.wait_ge(y_done, 8)
                    if not (isinstance(j, int) and j == 0 and e == 0):
                        pe.wait_ge(mp_done, d * 2 + half - 1)
                    for k in range(NG):
                        w = slice(k * P, (k + 1) * P)
                        last = three(bank[3 * half + 2], hi(sb)[:, w], lo(sb)[:, w],
                                     poolT_hi[:, k, x], poolT_lo[:, k, x], k == 0, k == NG - 1)
                    last.then_inc(m1_ps, 1)

        def modulation(j):
            pe.wait_ge(acc_ready, j + 1)
            for k in range(KD):
                last = mm(bank[6][:, k:k + 1], acc[:, k * P:(k + 1) * P], ones[:, 0:1],
                          start=True, stop=True)
            last.then_inc(mod2_ps, 1)

        def gates_late():
            _, _, _, sg, sn, _ = M1_SLOT
            for n, slot in enumerate((sg, sn)):
                pe.wait_ge(sg_done, 4 * KD - 5 + n)
                for k in range(KD):
                    w = slice(k * P, (k + 1) * P)
                    last = three(bank[3 + n], hi(slot)[:, w], lo(slot)[:, w],
                                 hT_hi[:, k, HALF:L], hT_lo[:, k, HALF:L], k == 0, k == KD - 1)
                last.then_inc(late_ps, 1)

        gate_turn(0)
        with pe.Fori(1, 3) as j:
            gate_turn(j)
        gate_turn(3)

        def qkv(p, t):
            first = isinstance(p, int) and p == 0
            if t == 0:
                pe.wait_ge(split, U_ATT + p * 3 + 3)
            if not first:
                pe.wait_ge(z_copied, p * NTA + t)
            elif t >= 2:
                pe.wait_ge(z_copied, t - 1)
            elif t == 1:
                pe.wait_ge(mp_done, 2 * KD - 1)
            zb = bank[2 if first and t % 2 else 7]
            c = 0 if t < NT else 1
            for k in range(KD):
                w = slice(k * P, (k + 1) * P)
                x = slice(t * P, (t + 1) * P)
                last = three(zb[:, c * P:384].rearrange("p (u n) -> p u n", n=P),
                             hT_hi[:, k, x], hT_lo[:, k, x],
                             ringA_hi[:, c:3, w], ringA_lo[:, c:3, w], k == 0, k == KD - 1)
            last.then_inc(z_ps, 1)

        def turn_head(p, hh, n):
            s0 = p * 16 + hh * 8
            first = isinstance(p, int) and s0 == 0
            if n == 0:
                if not first:
                    pe.wait_ge(exp_done, s0 - 1)
                pe.wait_ge(rotq_done, p * 2 + 2)
                pe.wait_ge(rotk_done, p * 2 + hh + 1)
            elif n == 1 and not first:
                pe.wait_ge(exp_done, s0)
            elif n == 2:
                pe.wait_ge(t_done, p * 14 + hh * 7 + 2)
            elif n == 3 and not first:
                pe.wait_ge(na_done, s0)
            if n < 3:
                src = (lambda i: rot_k[:, i, hh, :, :].rearrange("p c n -> p (c n)"),
                       lambda i: rot_q[:, i, :, :].rearrange("p c n -> p (c n)"), lambda i: nrm[:, i, 0:P])[n]
                for half in range(2):
                    for e in range(4):
                        last = nc.tensor.transpose(bank[T_BANK[2 * n + half]][:, e * P:(e + 1) * P],
                                                   src(4 * half + e), ident[:, :])
                    last.then_inc(t_ps, 1)
                return
            for e in range(2):
                last = nc.tensor.transpose(bank[6][:, e * P:(e + 1) * P],
                                           kc2[:, e, hh, :, :].rearrange("p c n -> p (c n)"), ident[:, :])
            last.then_inc(t_ps, 1)

        def scores(p, hh, i):
            s = p * 16 + hh * 8 + i
            if i == 0:
                pe.wait_ge(t_done, p * 14 + hh * 7 + 7)
            elif i > 1:
                pe.wait_ge(exp_done, s - 1)
            b0 = 2 * (i % 2)
            q = slice(i * P, (i + 1) * P)
            k0 = key_tile(i) * P
            c0 = HD if inner(i) else 0
            mm(bank[b0], qrT[:, q], krT_hi[:, k0:k0 + HALF], start=True, stop=False)
            mm(bank[b0], qrT[:, q], krT_lo[:, k0:k0 + HALF], start=False, stop=True)
            if inner(i):
                k1 = slice(k0 + HALF, k0 + HALF + HD)
                mm(bank[b0 + 1][:, 0:HD], qrT[:, q], krT_hi[:, k1], start=True, stop=False)
                mm(bank[b0 + 1][:, 0:HD], qrT[:, q], krT_lo[:, k1], start=False, stop=True)
            o = bank[b0 + 1][:, c0:c0 + CTX]
            mm(o, qpT[:, q], kcT_hi[:, :], start=True, stop=False)
            mm(o, qpT[:, q], kcT_lo[:, :], start=False, stop=True).then_inc(s_ps, 1)

        def turn_probs(p, hh, i):
            s = p * 16 + hh * 8 + i
            pe.wait_ge(exp_done, s + 1)
            if i:
                pe.wait_ge(ptA_copied, s)
                pe.wait_ge(ptB_copied, s)
            pr = prob[:, i % 2, :]
            for e in range(4):
                last = nc.tensor.transpose(bank[4][:, e * P:(e + 1) * P], pr[:, e * P:(e + 1) * P], ident[:, :])
            c0 = HALF + (HD if inner(i) else 0)
            if inner(i):
                nc.tensor.transpose(bank[5][0:HD, CTX:CTX + P], pr[:, HALF:HALF + HD], ident[:, :])
            for e in range(2):
                last = nc.tensor.transpose(bank[5][:, e * P:(e + 1) * P], pr[:, c0 + e * P:c0 + (e + 1) * P],
                                           ident[:, :])
            last.then_inc(pt_ps, 1)

        def values(p, hh, i):
            s = p * 16 + hh * 8 + i
            pe.wait_ge(ptA_copied, s + 1)
            pe.wait_ge(ptB_copied, s + 1)
            if i:
                pe.wait_ge(na_done, s)
            v = slice(hh * HD, (hh + 1) * HD)
            o = bank[6][:, 0:HD]
            kt = key_tile(i)
            for e in range(4):
                mm(o, probT[:, e, :], vcur[:, kt + e, v], start=(e == 0), stop=False)
            if inner(i):
                mm(o, probT[0:HD, 6, :], vcur[0:HD, kt + 4, v], start=False, stop=False)
            for e in range(2):
                last = mm(o, probT[:, 4 + e, :], vcur[:, NT + e, v], start=False, stop=(e == 1))
            last.then_inc(pv_ps, 1)

        def attend(p, ahead):
            for hh in range(2):
                if ahead:
                    qkv(p + 1, 9 if hh else 0)
                if hh == 0:
                    pe.wait_ge(v_taken, p + 1)
                scores(p, hh, 0)
                for i in range(8):
                    if i < 7:
                        scores(p, hh, i + 1)
                    if ahead and hh == 0 and i < 7:
                        qkv(p + 1, i + 1)
                    if not ahead and hh and i < 6:
                        turn_result(i // 2, i % 2)
                    if i == 7 and hh == 0:
                        turn_head(p, 1, 0)
                    if i:
                        values(p, hh, i - 1)
                    turn_probs(p, hh, i)
                if hh == 0:
                    turn_head(p, 1, 1)
                    if ahead:
                        qkv(p + 1, 8)
                values(p, hh, 7)
                if hh == 0:
                    turn_head(p, 1, 2)
                    turn_head(p, 1, 3)
                elif ahead:
                    for n in range(4):
                        turn_head(p + 1, 0, n)

        def turn_result(k, half):
            n = 2 * k + half
            if n == 0:
                pe.wait_ge(z_copied, PAIRS * NTA)
                pe.wait_ge(d_na, 16 * (PAIRS - 1))
            elif k < PAIRS - 1:
                pe.wait_ge(nat_split, n)
            for e in range(4):
                t = 4 * half + e
                src, b = (na_in[:, k, t, :], 7) if k < PAIRS - 1 else (na_tok[:, t, :], 4 + half)
                last = nc.tensor.transpose(bank[b][:, e * P:(e + 1) * P], src, ident[:, :])
            last.then_inc(nat_ps, 1)

        qkv(0, 0)
        modulation(3)
        for t in range(1, NTA):
            qkv(0, t)
        gates_late()
        pe.wait_ge(z_copied, NTA)
        pe.wait_ge(mod2_done, 4)
        turn_head(0, 0, 0)
        pe.wait_ge(sg_done, 4 * KD)
        for n in range(1, 4):
            turn_head(0, 0, n)
        pe.wait_ge(mp_done, 2 * KD)
        with pe.Fori(0, PAIRS - 1) as p:
            attend(p, True)
        attend(PAIRS - 1, False)
        pe.wait_ge(na_done, 8 * HEADS)

        for half in range(2):
            turn_result(PAIRS - 1, half)
        pe.wait_ge(g_diag, 8)
        pe.wait_ge(nat_split, 6)
        for k in range(KD):
            last = mm(psflat[:, (6 * HALF) + k * P:(6 * HALF) + (k + 1) * P], ones[:, :], g1diag[:, k, :],
                      start=True, stop=True)
        last.then_inc(g_ps, 1)
        for q in range(4):
            pe.wait_ge(split, U_NA + q + 1)
            for e in range(2):
                for half in range(2):
                    n = 4 * q + 2 * e + half
                    if n >= 6:
                        pe.wait_ge(m_done, n - 5)
                    x = slice(half * HALF, (half + 1) * HALF)
                    for k in range(PAIRS):
                        if n < 2 and k == PAIRS - 1:
                            pe.wait_ge(nat_split, 7 + n)
                        w = slice((4 * e + k) * P, (4 * e + k + 1) * P)
                        last = three(bank[n % 6], hi(q)[:, w], lo(q)[:, w], naT_hi[k][:, x], naT_lo[k][:, x],
                                     k == 0, k == PAIRS - 1)
                    last.then_inc(m2_ps, 1)
        def project(dh, t):
            n = 8 * dh + t
            if n >= 4:
                pe.wait_ge(xn_done, n - 3)
            else:
                pe.wait_ge(m_done, 13 + n)
            if n == 4:
                pe.wait_ge(m_done, 16)
            x = slice(t * P, (t + 1) * P)
            for k in range(KD):
                if n == 0 and k == KD - 1:
                    pe.wait_ge(m_done, 2 * k + 1)
                if t == 0 and k % 2 == 0:
                    pe.wait_ge(split, U_OUT + 4 * dh + k // 2 + 1)
                slot = O_SLOT[4 * dh + k // 2]
                w = slice((k % 2) * HALF, (k % 2 + 1) * HALF)
                last = three(bank[n % 4], mT_hi[:, k, x], mT_lo[:, k, x], hi(slot)[:, w], lo(slot)[:, w],
                             k == 0, k == KD - 1)
                if n == 7 and k in (1, 3):
                    last.then_inc(o_part, 1)
            last.then_inc(o_ps, 1)

        def turn_norm(half, k0):
            for k in range(k0, k0 + 4):
                n = 8 * half + k
                if n >= 4:
                    pe.wait_ge(h2_full, n - 3)
                else:
                    pe.wait_ge(g_ready, 2)
                for e in range(4):
                    if k == 0:
                        pe.wait_ge(nx_done, 4 * half + e + 1)
                    last = nc.tensor.transpose(bank[4 + n % 4][:, e * P:(e + 1) * P],
                                               nx[half][:, e, k * P:(k + 1) * P], ident[:, :])
                last.then_inc(h2_ps, 1)

        for n in range(16):
            project(n // 8, n % 8)
            if n in (13, 14):
                turn_norm(0, 4 * (n - 13))

        def hidden(g, n, pos):
            first = isinstance(g, int)
            f, half = n // 2, n % 2
            slot = f % 2
            unit = U_MLP + g * 8 + (0, 1, 3, 5)[f]
            if half == 0:
                pe.wait_ge(split, unit + 1)
            if n >= 4 or not first:
                pe.wait_ge(a_done, g * 8 + (FIRST_ORDER.index(n - 4) + 1 if first else n - 3))
            else:
                pe.wait_ge(xn_done, 13 + n)
            x = slice(half * HALF, (half + 1) * HALF)
            for k in range(KD):
                if first and f == 0:
                    pe.wait_ge(h2_done, 8 * half + k + 1)
                w = slice(k * P, (k + 1) * P)
                last = three(bank[n % 4], hi(slot)[:, w], lo(slot)[:, w], h2_hi[:, k, x], h2_lo[:, k, x],
                             k == 0, k == KD - 1)
            last.then_inc(f1_ps, 1)

        def mlp_turn(g):
            first = isinstance(g, int)
            for pos in range(8):
                hidden(g, FIRST_ORDER[pos] if first else pos, pos)
                if first and pos < 2:
                    turn_norm(1, 4 * pos)
                if first and pos == 3:
                    pe.wait_ge(g_diag, 16)
                    pe.wait_ge(h2_full, 16)
                    for k in range(KD):
                        last = mm(psflat[:, 4 * HALF + k * P:4 * HALF + (k + 1) * P], ones[:, :], g2diag[:, k, :],
                                  start=True, stop=True)
                    last.then_inc(g_ps, 1)
            for dh in range(2):
                for t in range(NT):
                    n = 8 * dh + t
                    if n >= 4 or not first:
                        pe.wait_ge(x_done, g * 16 + n - 3)
                    x = slice(t * P, (t + 1) * P)
                    w = slice(dh * HALF, (dh + 1) * HALF)
                    for f in range(FCH):
                        if n == 0 and first and f == 0:
                            pe.wait_ge(g_ready, 4)
                        if n == 0:
                            pe.wait_ge(a_done, g * 8 + (FIRST_ORDER.index(2 * f) if first else 2 * f) + 1)
                            pe.wait_ge(split, U_MLP + g * 8 + (2, 4, 6, 7)[f] + 1)
                        if n == 4:
                            pe.wait_ge(a_done, g * 8 + (FIRST_ORDER.index(2 * f + 1) if first else 2 * f + 1) + 1)
                        last = three(bank[4 + n % 4], aT_hi[:, f, x], aT_lo[:, f, x],
                                     hi(2 + f)[:, w], lo(2 + f)[:, w], f == 0, f == FCH - 1)
                    last.then_inc(f2_ps, 1)

        mlp_turn(0)
        with pe.Fori(1, NFG) as g:
            mlp_turn(g)

    @block.scalar
    def _(act):
        fn = nc.scalar.activation
        act.wait_ge(d_c, 16)
        fn(c_sig[:], c_col[:], ACT.Sigmoid).then_inc(sig_done, 1)
        for k in range(KD):
            if k == 6:
                act.wait_ge(row_ps, 1)
                for j in (1, 3):
                    fn(mod_row[:, j * HALF:(j + 1) * HALF], bank[4 + j][0:2, :], ACT.Copy)\
                        .then_inc(row_copied, 1)
            act.wait_ge(d_x[k], 16)
            if k >= 3:
                act.wait_ge(xsum_done, k - 2)
            fn(xsq[:, k % 2, :] if k else xsum[:, :], xT[:, k, :], ACT.Square).then_inc(sq_done, 1)
        act.wait_ge(ms_ready, 1)
        fn(rt[:, 0:NTA], ms[:, 0:NTA], ACT.Sqrt).then_inc(sqrt_done, 1)
        act.wait_ge(rb_ps, 1)
        fn(rctx, bank[3][:, 0:CTX], ACT.Copy).then_inc(rctx_ready, 1)
        for k in range(KD):
            act.wait_ge(xr_ready, k + 1)
            if k >= 2:
                act.wait_ge(h_done, k - 1)
            fn(hfull[:, k % 2, :], xT[:, k, 0:L], ACT.Identity,
               bias=mod1[:, k, 0:1], scale=gain1[:, k, 0:1]).then_inc(a_own, 1)
            act.wait_ge(a_own, k + 1)
            fn(hT_hi[:, k, 0:L], hfull[:, k % 2, :], ACT.Copy).then_inc(h_hi_done, 1)
        act.wait_ge(ctx_xr, 1)
        for k in range(KD):
            fn(xT[:, k, L:T], xT[:, k, L:T], ACT.Identity,
               bias=mod1[:, k, 1:2], scale=gain1[:, k, 1:2]).then_inc(a_own, 1)
        act.wait_ge(a_own, 2 * KD)
        fn(hT_hi[:, :, L:T], xT[:, :, L:T], ACT.Copy).then_inc(ctx_hi_done, 1)
        act.wait_ge(pads_done, 2)

        def u_out(g):
            for half in range(2):
                q = 2 * g + half
                act.wait_ge(u_ps, q + 1)
                if g:
                    act.wait_ge(d_made, g)
                fn(up[:, PAD + half * HALF:PAD + (half + 1) * HALF], bank[4 + q % 4], ACT.Copy)\
                    .then_inc(u_copied, 1)

        def d_out_hi(g):
            act.wait_ge(d_made, g + 1)
            if g:
                act.wait_ge(y_ps, 2 * g)
            fn(dT_hi[:, :], win[0][:, PAD:PAD + L], ACT.Copy).then_inc(d_hi_done, 1)

        def y_out(g):
            c = POOL_ORDER[g]
            for half in range(2):
                q = 2 * g + half
                act.wait_ge(y_ps, q + 1)
                fn(poolT_hi[:, c, half * HALF:(half + 1) * HALF], bank[Y_BANK[q]], ACT.Copy,
                   scale=pscale[:, c:c + 1]).then_inc(y_hi_done, 1)

        for g in range(NG):
            u_out(g)
            d_out_hi(g)
            if g:
                y_out(g - 1)
        y_out(NG - 1)

        def gate_turn(j):
            first = isinstance(j, int) and j == 0
            for e in range(2):
                for half in range(2):
                    d = j * 2 + e
                    for n in range(2):
                        u = 4 * e + 2 * half + n
                        if not first or u >= 2:
                            act.wait_ge(ada2_used, j * 8 + u - 1)
                        act.dma_start(ada2[:, n, :], a["ada2"][j * 8 + u]).then_inc(d_ada2[n], 16)
                    if late(j, e, half):
                        continue
                    act.wait_ge(m1_ps, d * 6 + half * 3 + 1)
                    if not first or e:
                        act.wait_ge(mp_done, d * 2 + half - 1)
                        act.wait_ge(spill_g[half], d * 16)
                    fn(sgp[:, half, :], bank[3 * half], ACT.Sigmoid).then_inc(sg_done, 1)
                    act.wait_ge(m1_ps, d * 6 + half * 3 + 2)
                    fn(sgn[:, half, :], bank[3 * half + 1], ACT.Sigmoid).then_inc(sg_done, 1)
                    act.wait_ge(sg_done, d * 4 + half * 2 + 2)
                    act.dma_start(spill_m[d, :, 0, half * HALF:(half + 1) * HALF], sgn[:, half, :])\
                        .then_inc(spill_g[half], 16)
                    if not (first and e == 0 and half == 0):
                        act.wait_ge(mp_done, d * 2 + half)
                        act.dma_start(spill_m[d if half else d - 1, :, 1, (1 - half) * HALF:(2 - half) * HALF],
                                      mpool[:, 1 - half, :]).then_inc(spill_p[1 - half], 16)

        act.wait_ge(y_ps, 8)
        act.wait_ge(y_done, 8)
        gate_turn(0)
        with act.Fori(1, 3) as j:
            gate_turn(j)
        gate_turn(3)
        act.wait_ge(mp_done, 2 * KD - 1)
        act.dma_start(spill_m[KD - 1, :, 1, 0:HALF], mpool[:, 0, :]).then_inc(spill_p[0], 16)

        act.wait_ge(split, U_ATT)
        act.dma_start(qk_g[:], a["qk_g"]).then_inc(d_att, 16)
        act.dma_start(rope_c[:], a["rope_c"]).then_inc(d_att, 16)
        act.dma_start(rope_s[:], a["rope_s"]).then_inc(d_att, 16)

        def z_out(p, t):
            first = isinstance(p, int) and p == 0
            if t == 0 and not first:
                act.wait_ge(nrm_done, 2 * p)
                act.wait_ge(v_taken, p)
            act.wait_ge(z_ps, p * NTA + t + 1)
            if first and t == NT:
                act.wait_ge(z_set, 1)
            c = 0 if t < NT else P
            fn(z[:, t, c:384], bank[2 if first and t % 2 else 7][:, c:384], ACT.Copy).then_inc(z_copied, 1)
            act.wait_ge(z_copied, p * NTA + t + 1)
            if t >= 2:
                act.wait_ge(zsum_done, p * NTA + t - 1)
            elif not first:
                act.wait_ge(rotq_done, 2 * p)
            fn(sq[:, t % 2, :], z[:, t, 0:256], ACT.Square).then_inc(zsq_done, 1)

        def qk_root(n, part=slice(0, 40)):
            act.wait_ge(qk_ms, n)
            fn(rt[:, part], ms[:, part], ACT.Sqrt).then_inc(qk_sqrt, 1)

        def unit_hi(p, r):
            s, count = landed("att", p, r)
            act.wait_ge(d_raw[s], count)
            fn(hi(r), raw(s), ACT.Copy).then_inc(split_hi, 1)

        def load_merge():
            act.wait_ge(z_ps, PAIRS * NTA)
            act.wait_ge(na_room, 16 * PAIRS)
            for k in range(PAIRS - 1):
                act.dma_start(na_in[:, k, :, :], spill_na[k]).then_inc(d_na, 16)
            for d in range(4):
                act.dma_start(m_in[M_SLOT[d]][:, :, :], spill_m[d]).then_inc(d_m[M_SLOT[d]], 16)

        def head_hi(p, hh, n0, n1):
            dst = (krT_hi[:, 0:HALF], krT_hi[:, HALF:L], qrT[:, 0:HALF], qrT[:, HALF:L],
                   qpT[:, 0:HALF], qpT[:, HALF:L], kcT_hi[:, :])
            for n in range(n0, n1):
                act.wait_ge(t_ps, p * 14 + hh * 7 + n + 1)
                src = bank[T_BANK[n]][:, 0:CTX if n == 6 else HALF]
                rows = slice(hh * HD, (hh + 1) * HD) if 2 <= n < 6 else slice(0, P)
                fn(dst[n][rows], src[rows], ACT.Copy).then_inc(t_hi_done, 1)

        def attend(p, ahead, units=False):
            for hh in range(2):
                if ahead:
                    z_out(p + 1, 9 if hh else 0)
                    if hh:
                        qk_root(p + 3)
                elif hh == 0:
                    load_merge()
                else:
                    act.dma_start(xn[:, 0:4, :], x_tiles[:, 0:4, :]).then_inc(d_xn[0], 16)
                exponents(p, hh, 0)
                for i in range(8):
                    s = p * 16 + hh * 8 + i
                    if i < 7:
                        exponents(p, hh, i + 1)
                    if i == 6 and (ahead or hh == 0):
                        act.dma_start(bias[:, :], a["bias"][p * 2 + hh + 1]).then_inc(d_bias, 16)
                    if ahead and hh == 0 and i < 7:
                        z_out(p + 1, i + 1)
                    if not ahead and hh and i < 6:
                        result_hi(i // 2, i % 2)
                    if i == 7 and hh == 0:
                        head_hi(p, 1, 0, 2)
                    act.wait_ge(pt_ps, s + 1)
                    if i:
                        act.wait_ge(pv_ps, s)
                    fn(probT[:, 0:4, :], bank[4].rearrange("p (e n) -> p e n", n=P), ACT.Copy)\
                        .then_inc(ptA_copied, 1)
                    if ahead and hh and i in NORM_STEPS:
                        if inner(i):
                            fn(probT[0:HD, 6, :], bank[5][0:HD, CTX:CTX + P], ACT.Copy)
                        fn(probT[:, 4:6, :], bank[5][:, 0:CTX].rearrange("p (e n) -> p e n", n=P), ACT.Copy)\
                            .then_inc(ptB_copied, 1)
                    if units and hh and i in (5, 6):
                        act.wait_ge(split, U_ATT + p * 3 + 7)
                        unit_hi(p + 2, i - 4)
                if hh == 0:
                    head_hi(p, 1, 2, 4)
                    if ahead:
                        z_out(p + 1, 8)
                    head_hi(p, 1, 4, 7)
            if ahead:
                head_hi(p + 1, 0, 0, 2)
                act.wait_ge(na_done, p * 16 + 16)
                act.dma_start(spill_na[p], na_tok[:, :, :]).then_inc(na_room, 16)
                head_hi(p + 1, 0, 2, 7)

        def exponents(p, hh, i):
            s = p * 16 + hh * 8 + i
            n = i % 2
            w = HALF + CTX + (HD if inner(i) else 0)
            act.wait_ge(sm_ready, s + 1)
            if i >= 2:
                act.wait_ge(pt_ps, s - 1)
            if i >= 4:
                act.wait_ge(na_done, s - 3)
            fn(prob[:, n, 0:w], psflat[:, 2 * n * HALF:2 * n * HALF + w], ACT.Exp,
               bias=nmax[:, n:n + 1], accum_out=den[:, i % 4:i % 4 + 1]).then_inc(exp_done, 1)

        def result_hi(k, half):
            act.wait_ge(nat_ps, 2 * k + half + 1)
            b = 7 if k < PAIRS - 1 else 4 + half
            fn(naT_hi[k][:, half * HALF:(half + 1) * HALF], bank[b], ACT.Copy).then_inc(nat_hi_done, 1)

        x_tiles = a["x"].rearrange("(t p) d -> p t d", p=P)
        for t in range(NTA):
            z_out(0, t)
            if t == 5:
                qk_root(1, slice(0, 20))
        qk_root(2, slice(20, 40))
        unit_hi(1, 0)
        unit_hi(1, 1)
        act.wait_ge(ada2_used, 32)
        for n, sg in enumerate((sgp_late, sgn_late)):
            act.wait_ge(late_ps, n + 1)
            fn(sg[:, :], bank[3 + n], ACT.Sigmoid).then_inc(sg_done, 1)
            if n == 0:
                unit_hi(1, 2)
        act.wait_ge(sg_done, 4 * KD)
        act.dma_start(spill_m[KD - 1, :, 0, HALF:L], sgn_late[:, :]).then_inc(spill_g[1], 16)
        head_hi(0, 0, 0, 2)
        act.wait_ge(mp_done, 2 * KD)
        act.dma_start(spill_m[KD - 1, :, 1, HALF:L], mpool_late[:, :]).then_inc(spill_p[1], 16)
        head_hi(0, 0, 2, 7)
        for n in range(2):
            act.wait_ge(spill_g[n], 16 * KD)
            act.wait_ge(spill_p[n], 16 * KD)
        act.dma_start(bias[:, :], a["bias"][0]).then_inc(d_bias, 16)
        with act.Fori(0, PAIRS - 2) as p:
            attend(p, True, units=True)
        attend(PAIRS - 2, True)
        attend(PAIRS - 1, False)

        for half in range(2):
            result_hi(PAIRS - 1, half)
        act.wait_ge(g_ps, 1)
        for n in range(2):
            fn(gb[:, n * HALF:(n + 1) * HALF], bank[6 + n], ACT.Copy).then_inc(g_ready, 1)
        act.dma_start(m_in[4][:, :, :], spill_m[4]).then_inc(d_m[4], 16)
        for d in range(KD):
            for half in range(2):
                x = slice(half * HALF, (half + 1) * HALF)
                act.wait_ge(m_sum, 2 * d + half + 1)
                fn(mT_hi[:, d, x], m_in[M_SLOT[d]][:, 1, x], ACT.Copy).then_inc(m_hi_done, 1)
            if d in M_SLOT[5:]:
                after = 5 + M_SLOT[5:].index(d)
                act.wait_ge(m_done, 2 * d + 2)
                act.dma_start(m_in[d][:, :, :], spill_m[after]).then_inc(d_m[d], 16)
        act.wait_ge(m2_ps, 16)
        act.dma_start(xn[:, 4:8, :], x_tiles[:, 4:8, :]).then_inc(d_xn[1], 16)
        def row_squares(t):
            act.wait_ge(xn_done, 8 + t + 1)
            fn(nx[t // 4][:, t % 4, :], xn[:, t, :], ACT.Square, accum_out=row_ss[:, t:t + 1])\
                .then_inc(xss_done, 1)
            act.wait_ge(xms, t + 1)
            fn(rt[:, t:t + 1], ms[:, t:t + 1], ACT.Sqrt).then_inc(xsqrt, 1)

        def h2_out(n):
            act.wait_ge(h2_ps, n + 1)
            if n >= 2:
                act.wait_ge(h2_done, n - 1)
            k = n % 8
            fn(h2tmp[:, n % 2, :], bank[4 + n % 4], ACT.Identity, bias=mod2[:, 1, k:k + 1],
               scale=gain2[:, k:k + 1]).then_inc(h2_full, 1)
            act.wait_ge(h2_full, n + 1)
            fn(h2_hi[:, k, (n // 8) * HALF:(n // 8 + 1) * HALF], h2tmp[:, n % 2, :], ACT.Copy)\
                .then_inc(h2_hi_done, 1)

        for t in range(5):
            row_squares(t)
        for n in range(4):
            h2_out(n)
        row_squares(5)
        for n in range(4, 8):
            h2_out(n)
        row_squares(6)
        row_squares(7)
        for n in range(8, 16):
            h2_out(n)

        def mlp_turn(g):
            first = isinstance(g, int)
            for pos in range(8):
                n = FIRST_ORDER[pos] if first else pos
                act.wait_ge(f1_ps, g * 8 + pos + 1)
                if pos >= 2 or not first:
                    act.wait_ge(a_done, g * 8 + pos - 1)
                fn(relu[:, pos % 2, :], bank[n % 4], ACT.Relu).then_inc(a_own, 1)
                act.wait_ge(a_own, 16 + g * 8 + pos + 1)
                fn(relu[:, pos % 2, :], relu[:, pos % 2, :], ACT.Square).then_inc(relu_done, 1)
                if first and pos == 3:
                    act.wait_ge(g_ps, 2)
                    for e in range(2):
                        fn(gb[:, e * HALF:(e + 1) * HALF], bank[4 + e], ACT.Copy).then_inc(g_ready, 1)

        mlp_turn(0)
        with act.Fori(1, NFG) as g:
            mlp_turn(g)

    @block.vector
    def _(dve):
        V = nc.vector
        own = Steps(dve, v_own)

        def rsqrt_begin(src, n, count, ready):
            V.tensor_scalar(ms[:, n], src, 1.0 / count, EPS, ALU.mult, ALU.add).then_inc(ready, 1)

        def rsqrt_end(n):
            own.link(V.reciprocal(rs[:, n], rt[:, n]))
            own.link(V.tensor_tensor(rt[:, n], rs[:, n], rs[:, n], ALU.mult))
            own.link(V.tensor_tensor(rt[:, n], rt[:, n], ms[:, n], ALU.mult))
            own.link(V.tensor_scalar(rt[:, n], rt[:, n], -0.5, 1.5, ALU.mult, ALU.add))
            own.link(V.tensor_tensor(rs[:, n], rs[:, n], rt[:, n], ALU.mult))

        dve.wait_ge(sig_done, 1)
        V.tensor_tensor(c_silu[:], c_col[:], c_sig[:], ALU.mult).then_inc(silu_done, 1)
        dve.wait_ge(d_const, 7 * 16)
        own.link(V.tensor_copy(pw_hi[:], pw_raw[:]))
        for k in range(1, KD):
            dve.wait_ge(sq_done, k + 1)
            if k > 1:
                dve.wait_ge(xsum_done, k - 1)
            V.tensor_tensor(xsum[:, :], xsum[:, :], xsq[:, k % 2, :], ALU.add).then_inc(xsum_done, 1)
            if k == 4:
                dve.wait_ge(row_ps, 1)
                for j in (0, 2):
                    V.tensor_copy(mod_row[:, j * HALF:(j + 1) * HALF], bank[4 + j][0:2, :])\
                        .then_inc(row_copied, 1)
        dve.wait_ge(mod1_ps, 1)
        own.link(V.tensor_tensor(mod1[:], bank[0][:, 0:32].rearrange("p (j c) -> p j c", c=2),
                                 ada_b[:, 0:16].unsqueeze(2).to_broadcast([P, 16, 2]), ALU.add))
        own.link(V.scalar_tensor_tensor(out=gain1[:], in0=mod1[:, 8:16, :], scalar=1.0,
                                        in1=norm_g[:, 0, :].unsqueeze(2).to_broadcast([P, KD, 2]),
                                        op0=ALU.add, op1=ALU.mult))
        dve.wait_ge(ssq_ps, 1)
        rsqrt_begin(bank[3][:, 0:NTA], slice(0, NTA), D, ms_ready)
        dve.wait_ge(sqrt_done, 1)
        dve.wait_ge(ms_ready, 1)
        rsqrt_end(slice(0, NTA))
        for t in range(NTA):
            V.tensor_scalar(diag[:, t, :], ident[:, :], rs[:, t:t + 1], None, ALU.mult).then_inc(diag_ready, 1)
        dve.wait_ge(rb_ps, 1)

        def h_lo(k):
            dve.wait_ge(h_hi_done, k + 1)
            V.tensor_tensor(hT_lo[:, k, 0:L], hfull[:, k % 2, :], hT_hi[:, k, 0:L].bitcast(F32), ALU.subtract)\
                .then_inc(h_done, 1)

        for k in range(KD):
            V.tensor_tensor(xT[:, k, 0:L], xT[:, k, 0:L], psflat[:, HALF:HALF + L], ALU.mult)\
                .then_inc(xr_ready, 1)
            if k:
                h_lo(k - 1)
        dve.wait_ge(rctx_ready, 1)
        V.tensor_tensor(xT[:, :, L:T], xT[:, :, L:T], rctx.unsqueeze(1).to_broadcast([P, KD, CTX]), ALU.mult)\
            .then_inc(ctx_xr, 1)
        h_lo(KD - 1)

        dve.wait_ge(ctx_hi_done, 1)
        V.tensor_tensor(hT_lo[:, :, L:T], xT[:, :, L:T], hT_hi[:, :, L:T].bitcast(F32), ALU.subtract)\
            .then_inc(ctx_done, 1)
        dve.wait_ge(ctx_done, 1)
        V.tensor_tensor(pw_lo[:], pw_raw[:], pw_hi[:].bitcast(F32), ALU.subtract).then_inc(pw_done, 1)
        V.memset(up[:, 0:PAD], 0.0).then_inc(pads_done, 1)
        V.memset(up[:, PAD + L:W], 0.0).then_inc(pads_done, 1)

        def y_lo(g):
            c = POOL_ORDER[g]
            for half in range(2):
                q = 2 * g + half
                dve.wait_ge(y_hi_done, q + 1)
                x = slice(half * HALF, (half + 1) * HALF)
                V.scalar_tensor_tensor(out=poolT_lo[:, c, x], in0=bank[Y_BANK[q]], scalar=pscale[:, c:c + 1],
                                       in1=poolT_hi[:, c, x].bitcast(F32), op0=ALU.mult, op1=ALU.subtract)\
                    .then_inc(y_done, 1)

        for g in range(NG):
            w = WINDOWS[g]
            dve.wait_ge(u_copied, 2 * g + 2)
            dve.wait_ge(pads_done, 2)
            if g:
                dve.wait_ge(d_hi_done, g)
                dve.wait_ge(d_done, g)
            b = (w.bit_length() - 1) % 2
            own.link(V.tensor_tensor(win[b][:, 1:W - 1], up[:, 0:W - 2], up[:, 1:W - 1], ALU.add))
            src, step, lo_i = win[b], 1, 1
            while 2 * step < w:
                b = 1 - b
                lo_i += step
                hi_i = W - lo_i
                own.link(V.tensor_tensor(win[b][:, lo_i:hi_i], src[:, lo_i - step:hi_i - step],
                                         src[:, lo_i + step:hi_i + step], ALU.add))
                src, step = win[b], 2 * step
            assert b == 1
            own.link(V.scalar_tensor_tensor(out=win[0][:, PAD:PAD + L], in0=src[:, PAD:PAD + L], scalar=1.0 / w,
                                            in1=up[:, PAD:PAD + L], op0=ALU.mult, op1=ALU.subtract))
            for n, e0 in enumerate((PAD, L)):
                e = slice(e0, e0 + PAD)
                own.link(V.tensor_tensor(edge_tmp[:, :], src[:, e], edge_inv[:, POOL_ORDER[g], n * PAD:(n + 1) * PAD],
                                         ALU.mult))
                ins = V.tensor_tensor(win[0][:, e], edge_tmp[:, :], up[:, e], ALU.subtract)
                if n:
                    ins.then_inc(d_made, 1)
                else:
                    own.link(ins)
            dve.wait_ge(d_hi_done, g + 1)
            V.tensor_tensor(dT_lo[:, :], win[0][:, PAD:PAD + L], dT_hi[:, :].bitcast(F32), ALU.subtract)\
                .then_inc(d_done, 1)
            if g:
                y_lo(g - 1)
        y_lo(NG - 1)

        def gate_turn(j):
            first = isinstance(j, int) and j == 0
            for e in range(2):
                for half in range(2):
                    d = j * 2 + e
                    for n in range(2):
                        k = 4 * e + 2 * half + n
                        dve.wait_ge(d_ada2[n], j * 64 + (k // 2) * 16 + 16)
                        if k == 0:
                            if not first:
                                dve.wait_ge(mod2_ps, j)
                            ins = V.tensor_scalar(acc[:, :], ada2[:, n, :], c_silu[:, k, 0:1], None, ALU.mult)
                        else:
                            dve.wait_ge(ada2_used, j * 8 + k)
                            ins = V.scalar_tensor_tensor(out=acc[:, :], in0=ada2[:, n, :], scalar=c_silu[:, k, 0:1],
                                                         in1=acc[:, :], op0=ALU.mult, op1=ALU.add)
                        ins.then_inc(ada2_used, 1)
                    if late(j, e, half):
                        continue
                    dve.wait_ge(sg_done, d * 4 + half * 2 + 1)
                    dve.wait_ge(m1_ps, d * 6 + half * 3 + (4 if first and e == half == 0 else 3))
                    if not first or e:
                        dve.wait_ge(spill_p[half], d * 16)
                    V.tensor_tensor(mpool[:, half, :], sgp[:, half, :], bank[3 * half + 2], ALU.mult)\
                        .then_inc(mp_done, 1)
            dve.wait_ge(ada2_used, j * 8 + 8)
            V.tensor_copy(edge_tmp[:, 0:1], acc[:, 0:1]).then_inc(acc_ready, 1)
            dve.wait_ge(mod2_ps, j + 1)
            V.tensor_copy(mod2[:, j, :], bank[6][:, 0:KD]).then_inc(mod2_done, 1)

        gate_turn(0)
        with dve.Fori(1, 3) as j:
            gate_turn(j)
        gate_turn(3)

        dve.wait_ge(mod2_done, 4)
        own.link(V.tensor_tensor(mod2[:], mod2[:], ada_b[:, 16:48].rearrange("p (m k) -> p m k", k=KD), ALU.add))
        own.link(V.scalar_tensor_tensor(out=gain2[:, :], in0=mod2[:, 2, :], scalar=1.0, in1=norm_g[:, 1, :],
                                        op0=ALU.add, op1=ALU.mult))
        dve.wait_ge(m1_ps, M1_LAST)
        dve.wait_ge(sg_done, 4 * KD - 2)
        V.memset(z[:, NT:NTA, 0:P], 1.0).then_inc(z_set, 1)
        dve.wait_ge(d_att, 48)
        V.tensor_scalar(qk_g[:, 0:P], qk_g[:, 0:P], HD ** -0.5, None, ALU.mult).then_inc(gain_set, 1)

        def sum_squares(p, t):
            dve.wait_ge(zsq_done, p * NTA + t + 1)
            V.tensor_reduce(rs[:, 4 * t:4 * t + 4], sq[:, t % 2, :].rearrange("p (s n) -> p s n", n=HD),
                            AX.X, ALU.add).then_inc(zsum_done, 1)

        def qk_mean(p, t0=0, t1=NTA):
            dve.wait_ge(zsum_done, p * NTA + t1)
            rsqrt_begin(rs[:, 4 * t0:4 * t1], slice(4 * t0, 4 * t1), HD, qk_ms)

        def qk_rsqrt(n, t0=0, t1=NTA):
            dve.wait_ge(qk_sqrt, n)
            rsqrt_end(slice(4 * t0, 4 * t1))

        def normalise(p, half):
            ts = slice(5 * half, 5 * half + 5)
            dve.wait_ge(zg_done, p * NTA + 5 * half + 5)
            V.tensor_tensor(nrm[:, ts, :].rearrange("p t (s n) -> p t s n", n=HD),
                            z[:, ts, 0:256].rearrange("p t (s n) -> p t s n", n=HD),
                            rs[:, 20 * half:20 * half + 20].rearrange("p (t s) -> p t s", s=4).unsqueeze(3)
                            .to_broadcast([P, 5, 4, HD]), ALU.mult).then_inc(nrm_done, 1)

        def rotate_q(p, hh):
            x = slice(hh * HD, (hh + 1) * HD)
            prod = rot_q[:, :, hh, :]
            if hh:
                dve.wait_ge(rotq_done, 2 * p + 1)
            else:
                dve.wait_ge(nrm_done, 2 * p + 2)
            own.done(V.tensor_tensor(prod, nrm[:, 0:NT, x], rope_c[:, :, :], ALU.mult))
            xh = nrm[:, 0:NT, x].rearrange("p t (c h n) -> p t c h n", h=2, n=HD // 4)
            sh = rope_s[:, :, :].rearrange("p t (c h n) -> p t c h n", h=2, n=HD // 4)
            th = rope_u[:, :, :].rearrange("p t (c h n) -> p t c h n", h=2, n=HD // 4)
            for h in range(2):
                own.done(V.tensor_tensor(th[:, :, :, h, :], xh[:, :, :, 1 - h, :], sh[:, :, :, h, :], ALU.mult))
            own.wait()
            V.tensor_tensor(prod, prod, rope_u[:, :, :], ALU.add).then_inc(rotq_done, 1)

        def take_v(p):
            dve.wait_ge(z_copied, p * NTA + NTA)
            V.tensor_copy(vcur[:, :, :], z[:, :, 256:384]).then_inc(v_taken, 1)

        def head_lo(p, hh, n0, n1):
            own_rows, other = slice(hh * HD, (hh + 1) * HD), slice((1 - hh) * HD, (2 - hh) * HD)
            for n in range(n0, n1):
                dve.wait_ge(t_hi_done, p * 14 + hh * 7 + n + 1)
                src = bank[T_BANK[n]]
                if 2 <= n < 6:
                    q = (qrT, qpT)[n // 2 - 1][:, (n % 2) * HALF:(n % 2 + 1) * HALF]
                    ins = V.tensor_tensor(q[other], src[own_rows, :], q[own_rows].bitcast(F32), ALU.subtract)
                elif n < 2:
                    x = slice((n % 2) * HALF, (n % 2 + 1) * HALF)
                    ins = V.tensor_tensor(krT_lo[:, x], src, krT_hi[:, x].bitcast(F32), ALU.subtract)
                else:
                    ins = V.tensor_tensor(kcT_lo[:, :], src[:, 0:CTX], kcT_hi[:, :].bitcast(F32), ALU.subtract)
                ins.then_inc(t_done, 1)

        def soften(p, hh, i):
            s = p * 16 + hh * 8 + i
            n = i % 2
            w = HALF + (HD if inner(i) else 0)
            b0 = SLOTS_FULL * GRID_W if inner(i) else (2 * key_tile(i) - 2 * i + 6) * GRID_W
            flat = psflat[:, 2 * n * HALF:2 * n * HALF + w + CTX]
            dve.wait_ge(s_ps, s + 1)
            if i == 0:
                dve.wait_ge(d_bias, p * 32 + hh * 16 + 16)
            own.done(V.tensor_reduce(cmax[:, n:n + 1], flat[:, w:w + CTX], AX.X, ALU.max))
            own.link(V.tensor_tensor_reduce(flat[:, 0:w], flat[:, 0:w], bias[:, b0:b0 + w], 1.0,
                                            BIG, ALU.add, ALU.max, smax[:, n:n + 1]))
            V.tensor_scalar(nmax[:, n:n + 1], smax[:, n:n + 1], cmax[:, n:n + 1], -1.0, ALU.max, ALU.mult)\
                .then_inc(sm_ready, 1)

        def take_ctx_probs(p, hh, i):
            s = p * 16 + hh * 8 + i
            dve.wait_ge(pt_ps, s + 1)
            if i:
                dve.wait_ge(pv_ps, s)
            if inner(i):
                V.tensor_copy(probT[0:HD, 6, :], bank[5][0:HD, CTX:CTX + P])
            V.tensor_copy(probT[:, 4:6, :], bank[5][:, 0:CTX].rearrange("p (e n) -> p e n", n=P))\
                .then_inc(ptB_copied, 1)

        def take_values(p, hh, i):
            s = p * 16 + hh * 8 + i
            c = slice(i % 4, i % 4 + 1)
            dve.wait_ge(exp_done, s + 1)
            own.link(V.reciprocal(rden[:, c], den[:, c]))
            dve.wait_ge(pv_ps, s + 1)
            V.tensor_scalar(na_tok[:, i, hh * HD:(hh + 1) * HD], bank[6][:, 0:HD],
                            rden[:, c], None, ALU.mult).then_inc(na_done, 1)

        def attend(p, ahead):
            for hh in range(2):
                if ahead:
                    sum_squares(p + 1, 9 if hh else 0)
                if ahead and hh:
                    qk_mean(p + 1)
                soften(p, hh, 0)
                for i in range(8):
                    if i < 7:
                        soften(p, hh, i + 1)
                    if i == 1 and hh == 0:
                        dve.wait_ge(na_room, p * 16 + 16)
                    if i == 7 and hh == 0:
                        head_lo(p, 1, 0, 2)
                    if i:
                        take_values(p, hh, i - 1)
                    if not (ahead and hh and i in NORM_STEPS):
                        take_ctx_probs(p, hh, i)
                    if i == 7 and hh == 0:
                        head_lo(p, 1, 2, 4)
                    if ahead and hh == 0:
                        sum_squares(p + 1, i + 1)
                    if ahead and hh:
                        if i == 0:
                            qk_rsqrt(p + 3)
                        elif i in NORM_STEPS[:2]:
                            normalise(p + 1, NORM_STEPS.index(i))
                        elif i in NORM_STEPS[2:]:
                            rotate_q(p + 1, NORM_STEPS.index(i) - 2)
                    if not ahead and hh and i < 6:
                        result_lo(i // 2, i % 2)
                take_values(p, hh, 7)
                if hh == 0:
                    head_lo(p, 1, 4, 7)
            if ahead:
                take_v(p + 1)
                head_lo(p + 1, 0, 0, 7)

        def result_lo(k, half):
            n = 2 * k + half
            x = slice(half * HALF, (half + 1) * HALF)
            b = 7 if k < PAIRS - 1 else 4 + half
            dve.wait_ge(nat_hi_done, n + 1)
            V.tensor_tensor(naT_lo[k][:, x], bank[b], naT_hi[k][:, x].bitcast(F32), ALU.subtract)\
                .then_inc(nat_split, 1)

        for t in range(NTA):
            sum_squares(0, t)
            if t == 4:
                qk_mean(0, 0, 5)
            if t == 5:
                qk_rsqrt(1, 0, 5)
                normalise(0, 0)
        qk_mean(0, 5, NTA)
        qk_rsqrt(2, 5, NTA)
        normalise(0, 1)
        rotate_q(0, 0)
        rotate_q(0, 1)
        dve.wait_ge(sg_done, 4 * KD - 1)
        V.tensor_tensor(mpool_late[:, :], sgp_late[:, :], bank[5], ALU.mult).then_inc(mp_done, 1)
        dve.wait_ge(late_ps, 2)
        take_v(0)
        head_lo(0, 0, 0, 7)
        dve.wait_ge(spill_p[1], 16 * KD)
        V.memset(na_tok[:, 0, 0:1], 0.0).then_inc(na_room, 16)
        PER = 2 * 8 * (2 + 1) + 5 + 2 * 3
        with dve.Fori(0, PAIRS - 1) as p:
            own.enter(p, 0, PER)
            attend(p, True)
        own.leave(PAIRS - 1)
        dve.wait_ge(z_ps, PAIRS * NTA)
        for k in range(KD):
            V.tensor_scalar(g1diag[:, k, :], ident[:, :], mod2[:, 0, k:k + 1], None, ALU.mult).then_inc(g_diag, 1)
        attend(PAIRS - 1, False)

        for half in range(2):
            result_lo(PAIRS - 1, half)
        for n in range(16):
            d, x = n // 2, slice((n % 2) * HALF, (n % 2 + 1) * HALF)
            m = m_in[M_SLOT[d]]
            dve.wait_ge(m2_ps, n + 1)
            if n % 2 == 0:
                dve.wait_ge(d_m[M_SLOT[d]], 16 * M_SLOT[:d + 1].count(M_SLOT[d]))
            own.link(V.tensor_tensor(m[:, 0, x], m[:, 0, x], bank[n % 6], ALU.mult))
            V.tensor_tensor(m[:, 1, x], m[:, 1, x], m[:, 0, x], ALU.add).then_inc(m_sum, 1)
            dve.wait_ge(m_hi_done, n + 1)
            V.tensor_tensor(mT_lo[:, d, x], m[:, 1, x], mT_hi[:, d, x].bitcast(F32), ALU.subtract)\
                .then_inc(m_done, 1)
        dve.wait_ge(g_ready, 2)

        def renorm(t):
            dve.wait_ge(xss_done, t + 1)
            rsqrt_begin(row_ss[:, t:t + 1], slice(t, t + 1), D, xms)
            dve.wait_ge(xsqrt, t + 1)
            dve.wait_ge(xms, t + 1)
            rsqrt_end(slice(t, t + 1))
            V.tensor_scalar(nx[t // 4][:, t % 4, :], xn[:, t, :], rs[:, t:t + 1], None, ALU.mult)\
                .then_inc(nx_done, 1)

        def h2_lo_part(n):
            k, x = n % 8, slice((n // 8) * HALF, (n // 8 + 1) * HALF)
            dve.wait_ge(h2_hi_done, n + 1)
            V.tensor_tensor(h2_lo[:, k, x], h2tmp[:, n % 2, :], h2_hi[:, k, x].bitcast(F32), ALU.subtract)\
                .then_inc(h2_done, 1)

        for dh in range(2):
            for t in range(NT):
                n = 8 * dh + t
                dve.wait_ge(o_ps, n + 1)
                if dh == 0 and t % 4 == 0:
                    dve.wait_ge(d_xn[t // 4], 16)
                x = slice(dh * HALF, (dh + 1) * HALF)
                own.link(V.tensor_tensor(otmp[:, n % 2, :], gb[:, x], bank[n % 4], ALU.mult))
                V.tensor_tensor(xn[:, t, x], xn[:, t, x], otmp[:, n % 2, :], ALU.add).then_inc(xn_done, 1)
                if dh and 1 <= t < 7:
                    renorm(t - 1)
                if dh and t in (5, 6):
                    for k in range(4 * (t - 5), 4 * (t - 4)):
                        h2_lo_part(k)
        renorm(6)
        renorm(7)
        for n in range(8, 16):
            h2_lo_part(n)
        dve.wait_ge(h2_done, 16)
        for k in range(KD):
            V.tensor_scalar(g2diag[:, k, :], ident[:, :], mod2[:, 3, k:k + 1], None, ALU.mult).then_inc(g_diag, 1)

        def mlp_turn(g):
            first = isinstance(g, int)
            for pos in range(8):
                n = FIRST_ORDER[pos] if first else pos
                f, x = n // 2, slice((n % 2) * HALF, (n % 2 + 1) * HALF)
                dve.wait_ge(relu_done, g * 8 + pos + 1)
                if not first and n == 0:
                    dve.wait_ge(f2_ps, g * 16)
                own.link(V.tensor_copy(aT_hi[:, f, x], relu[:, pos % 2, :]))
                V.tensor_tensor(aT_lo[:, f, x], relu[:, pos % 2, :], aT_hi[:, f, x].bitcast(F32), ALU.subtract)\
                    .then_inc(a_done, 1)
            for n in range(16):
                dh, t = n // 8, n % 8
                x = slice(dh * HALF, (dh + 1) * HALF)
                dve.wait_ge(f2_ps, g * 16 + n + 1)
                if n == 0 and first:
                    dve.wait_ge(g_ready, 4)
                own.link(V.tensor_tensor(ytmp[:, n % 2, :], gb[:, x], bank[4 + n % 4], ALU.mult))
                V.tensor_tensor(xn[:, t, x], xn[:, t, x], ytmp[:, n % 2, :], ALU.add).then_inc(x_done, 1)

        mlp_turn(0)
        with dve.Fori(1, NFG) as g:
            own.enter(g, 1, 24)
            mlp_turn(g)
        own.leave(NFG - 1)


def shape_constants():
    t = np.arange(L)
    n_freq = HD // 4
    inv = np.float32(10000.0) ** (-np.arange(n_freq, dtype=np.float32) / np.float32(n_freq))
    ang = [(t // GRID_W).astype(np.float32)[:, None] * inv, (t % GRID_W).astype(np.float32)[:, None] * inv]
    cos = np.concatenate([f(x) for x in ang for f in (np.cos, np.cos)], 1)
    sin = np.concatenate([s * np.sin(x) for x in ang for s in (np.float32(-1), np.float32(1))], 1)
    tile = lambda m: np.ascontiguousarray(m.reshape(NT, P, HD).transpose(1, 0, 2).astype(np.float32))
    edge = np.zeros((NG, 2 * PAD), np.float32)
    for g, w in enumerate((2, 4, 8, 16)):
        pos = np.concatenate([np.arange(PAD), np.arange(L - PAD, L)])
        edge[g] = 1.0 / (np.minimum(pos + w // 2, L) - np.maximum(pos - w // 2, 0))
    return {"rope_c": tile(cos), "rope_s": tile(sin), "ident": np.eye(P, dtype=np.float32),
            "ones": np.ones((P, P), np.float32),
            "edge_inv": np.ascontiguousarray(np.broadcast_to(edge, (P, NG, 2 * PAD)))}


def bias_layout(rpb):
    q = np.arange(GRID_W)
    c0 = np.clip(q - NA_COLS // 2, 0, GRID_W - NA_COLS)
    rel = q[None, :] - q[:, None] + NA_COLS - 1
    seen = (q[None, :] >= c0[:, None]) & (q[None, :] < c0[:, None] + NA_COLS)
    rel = np.where(seen, rel, 0)
    out = np.full((HEADS, 2, GRID_W, SLOTS_FULL + SLOTS_INNER, GRID_W), BIG, np.float32)
    for odd in range(2):
        for s in range(SLOTS_FULL):
            out[:, odd, :, s, :] = np.where(seen[None], rpb[:, s + 1 - odd][:, rel], np.float32(BIG))
        for m in range(SLOTS_INNER):
            if m - odd in range(NA_ROWS):
                out[:, odd, :, SLOTS_FULL + m, :] = out[:, odd, :, m + 2, :]
    return out.reshape(HEADS, P, BIASW)


def by_k(w):
    return w.reshape(-1, P, w.shape[1]).transpose(1, 0, 2).reshape(P, -1)


def units_layout(i):
    w_in, w_bp, w_bn = i["w_in"][0], i["w_branch_pool"][0], i["w_branch_na"][0]
    w_out, w1, w2 = i["w_out"][0], i["mlp_w1"][0], i["mlp_w2"][0]
    u = np.zeros((UNITS, P, 1024), np.float32)
    for n, g in enumerate(POOL_ORDER):
        u[U_POOL + n] = by_k(w_in[:, g * P:(g + 1) * P])
    for d in range(KD):
        c = slice(d * P, (d + 1) * P)
        u[U_GATE + 3 * d] = by_k(w_in[:, 2048:3072][:, c])
        u[U_GATE + 3 * d + 1] = by_k(w_in[:, 3072:4096][:, c])
        u[U_GATE + 3 * d + 2, :, 0:512] = by_k(w_bp[:, c])
        u[U_NA + d // 2, :, (d % 2) * 512:(d % 2 + 1) * 512] = by_k(w_bn[:, c])
    for p in range(PAIRS):
        for n in range(3):
            u[U_ATT + 3 * p + n] = by_k(w_in[:, 512 * (n + 1) + p * P:512 * (n + 1) + (p + 1) * P])
    for dh in range(2):
        for n in range(4):
            u[U_OUT + 4 * dh + n] = by_k(w_out[n * 256:(n + 1) * 256, dh * HALF:(dh + 1) * HALF])
    for g in range(NFG):
        for r, (kind, c, _) in enumerate(MLP_ORDER):
            f = slice(g * FG + c * P, g * FG + (c + 1) * P)
            u[U_MLP + 8 * g + r] = by_k(w1[:, f]) if kind == "w1" else w2[f]
    return u


def lay_out(inputs):
    i = {k: np.asarray(v) for k, v in inputs.items()}
    x = i["x"][0]
    ada = i["ada_w"][0]
    col = lambda v: np.ascontiguousarray(v.reshape(-1, P).T)
    g = {
        "x": x,
        "xT": np.concatenate([x, i["ctx"][0]], 0).T.reshape(KD, P, T),
        "c_col": np.stack([col(i["c"][0]), col(i["c_ctx"])], -1),
        "norm_g": np.stack([col(i["norm1_g"][0]), col(i["norm2_g"][0])], 1),
        "ada_b": col(i["ada_b"][0]),
        "pscale": col(i["pool_scale"][0]),
        "pool_w": i["pool_w"][0].transpose(1, 0, 2),
        "qk_g": np.broadcast_to(np.concatenate([i["q_norm_g"][0]] * 2 + [i["k_norm_g"][0]] * 2), (P, 256)),
        "ada1": ada[:, 0:2048].reshape(KD, P, 2048),
        "ada2": ada[:, 2048:].reshape(KD, P, 4, 1024).transpose(2, 0, 1, 3).reshape(32, P, 1024),
        "bias": bias_layout(i["rpb"][0]),
        "units": units_layout(i),
    }
    g.update(shape_constants())
    return {k: np.ascontiguousarray(v) for k, v in g.items()}


def kernel(**inputs):
    import concourse.bacc as bacc
    from concourse.bass_utils import run_bass_kernel_spmd

    nc = bacc.Bacc("TRN2", target_bir_lowering=False, num_devices=1)
    arrays = {f"in_{k}": v for k, v in lay_out(inputs).items()}
    a = {k[3:]: nc.dram_tensor(k, v.shape, F32, kind="ExternalInput").ap() for k, v in arrays.items()}
    out = nc.dram_tensor("x_out", (L, D), F32, kind="ExternalOutput").ap()
    build(nc, a, out)
    r = run_bass_kernel_spmd(nc, [arrays], core_ids=[0])
    return r.results[0]["x_out"].reshape(1, L, D)
```
